# Optimizing a Trainium2 kernel written in Bass

```python
import jax, jax.numpy as jnp
from jax import lax
import numpy as np

D_MODEL = 1024
BATCH = 1
SEQ = 512
DEPTH = 2
DEC_BATCH = 8
DEC_SEQ = 16
PAST_LEN = 256

CHUNK = 64
EPS = 1e-6
N_EVEN = (DEPTH + 1) // 2
N_ODD = DEPTH // 2
A_HEADS = 4
A_DK = 128
A_DV = 128
A_KW = A_HEADS * A_DK
A_VW = A_HEADS * A_DV
B_HEADS = 4
B_DK = 128
B_DV = 128
B_KW = B_HEADS * B_DK
B_VW = B_HEADS * B_DV
ROPE_BASE = 10000.0
IN0_WIDTH = 2 * A_KW + 2 * A_VW + 2 * B_KW + 2 * B_VW
MIX_WIDTH = A_VW + B_VW
C_HEADS = 4
C_INNER = 2 * D_MODEL
C_DH = C_INNER // C_HEADS
C_CONV = 4
C_BLOCK = 4
C_NBLK = C_INNER // C_BLOCK
D_FF = -(-8 * D_MODEL // (3 * 256)) * 256

kernel_name = 'hybrid_hgrn2_retnet_mlstm_stream_step'

def _rmsnorm(x, g):
    xf = x.astype(jnp.float32)
    y = xf * lax.rsqrt(jnp.mean(xf * xf, axis=-1, keepdims=True) + EPS)
    return (y * g.astype(jnp.float32)).astype(x.dtype)

def _head_layernorm(x, g):
    xf = x.astype(jnp.float32)
    xc = xf - jnp.mean(xf, axis=-1, keepdims=True)
    var = jnp.mean(xc * xc, axis=-1, keepdims=True)
    return xc * lax.rsqrt(var + EPS) * g.astype(jnp.float32)

def _to_chunks(t, L):
    b, T, h, d = t.shape
    return t.reshape(b, T // L, L, h, d).transpose(1, 0, 3, 2, 4)

def _from_chunks(t):
    nc, b, h, L, d = t.shape
    return t.transpose(1, 0, 3, 2, 4).reshape(b, nc * L, h, d)

def _gates_to_chunks(t, L):
    b, T, h = t.shape
    return t.reshape(b, T // L, L, h).transpose(1, 0, 3, 2)

def _rotary(t, pos):
    half = t.shape[-1] // 2
    inv = ROPE_BASE ** (-jnp.arange(half, dtype=jnp.float32) / half)
    ang = pos[:, None] * inv[None, :]
    cos = jnp.cos(ang)[None, :, None, :]
    sin = jnp.sin(ang)[None, :, None, :]
    t1, t2 = t[..., :half], t[..., half:]
    return jnp.concatenate([t1 * cos - t2 * sin, t1 * sin + t2 * cos], axis=-1)

def _blockdiag(t, w):
    b, T, n = t.shape
    y = jnp.einsum('btni,nio->btno', t.reshape(b, T, C_NBLK, C_BLOCK), w.astype(jnp.float32))
    return y.reshape(b, T, n)

def _hgrn2_chunked(q, k, v, logf, S0):
    T = q.shape[1]
    L = min(CHUNK, T)
    causal = jnp.tril(jnp.ones((L, L), dtype=bool))

    def step(S, inp):
        qb, kb, vb, fb = inp
        b = jnp.cumsum(fb, axis=2)
        o_inter = jnp.einsum('bhjk,bhkv->bhjv', qb * jnp.exp(b), S)
        diff = b[:, :, :, None, :] - b[:, :, None, :, :]
        decay = jnp.exp(jnp.where(causal[:, :, None], diff, -jnp.inf))
        att = jnp.einsum('bhjc,bhjsc,bhsc->bhjs', qb, decay, kb)
        o = o_inter + jnp.einsum('bhjs,bhsv->bhjv', att, vb)
        bL = b[:, :, -1:, :]
        S_new = jnp.exp(bL[:, :, 0, :])[..., None] * S + jnp.einsum('bhsk,bhsv->bhkv', kb * jnp.exp(bL - b), vb)
        return S_new, o

    xs = (_to_chunks(q, L), _to_chunks(k, L), _to_chunks(v, L), _to_chunks(logf, L))
    S, o = lax.scan(step, S0, xs)
    return _from_chunks(o), S

def _retention_chunked(q, k, v, log_gamma, S0):
    T = q.shape[1]
    L = min(CHUNK, T)
    idx = jnp.arange(L, dtype=jnp.float32)
    rel = idx[:, None] - idx[None, :]
    D = jnp.where(rel >= 0, jnp.exp(log_gamma[:, None, None] * jnp.maximum(rel, 0.0)), 0.0)
    w_in = jnp.exp(log_gamma[:, None] * (idx + 1.0))
    w_tail = jnp.exp(log_gamma[:, None] * (L - 1.0 - idx))
    g_L = jnp.exp(log_gamma * L)

    def step(S, inp):
        qb, kb, vb = inp
        att = jnp.einsum('bhjd,bhsd->bhjs', qb, kb) * D[None]
        o = jnp.einsum('bhjs,bhsv->bhjv', att, vb) + w_in[None, :, :, None] * jnp.einsum('bhjd,bhdv->bhjv', qb, S)
        S_new = g_L[None, :, None, None] * S + jnp.einsum('bhsd,bhsv->bhdv', kb * w_tail[None, :, :, None], vb)
        return S_new, o

    xs = (_to_chunks(q, L), _to_chunks(k, L), _to_chunks(v, L))
    S, o = lax.scan(step, S0, xs)
    return _from_chunks(o), S

def _mlstm_chunked(q, k, v, ig, logf, C0, n0, m0):
    T = q.shape[1]
    L = min(CHUNK, T)
    causal = jnp.tril(jnp.ones((L, L), dtype=bool))

    def step(carry, inp):
        C, n, m = carry
        qb, kb, vb, ib, fb = inp
        b = jnp.cumsum(fb, axis=-1)
        lw = jnp.where(causal, b[..., :, None] - b[..., None, :] + ib[..., None, :], -jnp.inf)
        lp = b + m[..., None]
        mj = jnp.maximum(lp, jnp.max(lw, axis=-1))
        w = jnp.exp(lw - mj[..., None])
        wp = jnp.exp(lp - mj)
        s = jnp.einsum('bhjd,bhsd->bhjs', qb, kb) * w
        num = jnp.einsum('bhjs,bhsv->bhjv', s, vb) + wp[..., None] * jnp.einsum('bhvd,bhjd->bhjv', C, qb)
        den = jnp.sum(s, axis=-1) + wp * jnp.einsum('bhd,bhjd->bhj', n, qb)
        h = num / jnp.maximum(jnp.abs(den), jnp.exp(-mj))[..., None]
        m_new = mj[..., -1]
        bL = b[..., -1]
        wsL = jnp.exp(bL[..., None] - b + ib - m_new[..., None])
        wpL = jnp.exp(bL + m - m_new)
        C_new = wpL[..., None, None] * C + jnp.einsum('bhs,bhsv,bhsd->bhvd', wsL, vb, kb)
        n_new = wpL[..., None] * n + jnp.einsum('bhs,bhsd->bhd', wsL, kb)
        return (C_new, n_new, m_new), h

    xs = (_to_chunks(q, L), _to_chunks(k, L), _to_chunks(v, L), _gates_to_chunks(ig, L), _gates_to_chunks(logf, L))
    (C, n, m), h = lax.scan(step, (C0, n0, m0), xs)
    return _from_chunks(h), C, n, m

def _trunk(x, pos0, st_hgrn, st_ret, st_c, st_n, st_m, st_conv, p):
    f32 = jnp.float32
    B, T, _ = x.shape
    pos = (jnp.arange(T) + pos0).astype(f32)
    hd = lambda t, H: t.reshape(B, T, H, -1)
    new_hgrn, new_ret, new_c, new_n, new_m, new_conv = [], [], [], [], [], []
    splits = [int(s) for s in np.cumsum([A_KW, A_KW, A_VW, A_VW, B_KW, B_KW, B_VW])]
    for l in range(DEPTH):
        h = _rmsnorm(x, p['norm_mix'][l])
        if l % 2 == 0:
            a = l // 2
            z = (h @ p['w_in0'][a]).astype(f32)
            aq, af, ai, ag, bq, bk, bv, bg = jnp.split(z, splits, axis=-1)
            lb = jnp.cumsum(jax.nn.softmax(p['lb_logits'].astype(f32), axis=0), axis=0)[a]
            f = lb + (1.0 - lb) * jax.nn.sigmoid(af)
            oA, SA = _hgrn2_chunked(hd(aq, A_HEADS), hd(1.0 - f, A_HEADS), hd(ai, A_HEADS),
                                    hd(jnp.log(f), A_HEADS), st_hgrn[a].astype(f32))
            oA = _rmsnorm(oA * jax.nn.sigmoid(hd(ag, A_HEADS)), p['hgrn_norm'][a])
            qB = _rotary(hd(bq, B_HEADS), pos)
            kB = _rotary(hd(bk, B_HEADS), pos) * (B_DK ** -0.5)
            log_gamma = jnp.log1p(-jnp.exp2(-5.0 - jnp.arange(B_HEADS, dtype=f32)))
            oB, SB = _retention_chunked(qB, kB, hd(bv, B_HEADS), log_gamma, st_ret[a].astype(f32))
            oB = _rmsnorm(oB, p['ret_norm'][a]) * jax.nn.silu(hd(bg, B_HEADS))
            mix = jnp.concatenate([oA.reshape(B, T, A_VW), oB.reshape(B, T, B_VW)], axis=-1).astype(x.dtype)
            x = x + mix @ p['w_out0'][a]
            new_hgrn.append(SA)
            new_ret.append(SB)
        else:
            c = l // 2
            up = (h @ p['w_up1'][c]).astype(f32)
            xm, zg = jnp.split(up, 2, axis=-1)
            xpad = jnp.concatenate([st_conv[c].astype(f32), xm], axis=1)
            cw = p['conv_w'][c].astype(f32)
            xc = p['conv_b'][c].astype(f32) + xpad[:, 0:T] * cw[0]
            for w in range(1, C_CONV):
                xc = xc + xpad[:, w:w + T] * cw[w]
            xc = jax.nn.silu(xc)
            q = _blockdiag(xc, p['w_q1'][c])
            k = _blockdiag(xc, p['w_k1'][c]) * (C_DH ** -0.5)
            v = _blockdiag(xm, p['w_v1'][c])
            gin = jnp.concatenate([q, k, v], axis=-1)
            ig = gin @ p['w_ig'][c].astype(f32) + p['b_ig'][c].astype(f32)
            logf = jax.nn.log_sigmoid(gin @ p['w_fg'][c].astype(f32) + p['b_fg'][c].astype(f32))
            hC, Cn, nn_, mn = _mlstm_chunked(hd(q, C_HEADS), hd(k, C_HEADS), hd(v, C_HEADS), ig, logf,
                                            st_c[c].astype(f32), st_n[c].astype(f32), st_m[c].astype(f32))
            hC = _head_layernorm(hC, p['mlstm_norm'][c]).reshape(B, T, C_INNER) + p['mlstm_skip'][c].astype(f32) * xc
            x = x + (hC * jax.nn.silu(zg)).astype(x.dtype) @ p['w_down1'][c]
            new_c.append(Cn)
            new_n.append(nn_)
            new_m.append(mn)
            new_conv.append(xpad[:, T:])
        h = _rmsnorm(x, p['norm_ffn'][l])
        x = x + (jax.nn.silu(h @ p['w_ffn_gate'][l]) * (h @ p['w_ffn_up'][l])) @ p['w_ffn_down'][l]
    y = _rmsnorm(x, p['norm_final'])
    st = lambda lst: jnp.stack(lst, axis=0).astype(x.dtype)
    return y, st(new_hgrn), st(new_ret), st(new_c), st(new_n), st(new_m), st(new_conv)

def setup_inputs(seed: int = 0) -> dict:
    key = jax.random.key(seed)
    ks = iter(jax.random.split(key, 48))
    f32 = jnp.float32
    nrm = lambda shape, scale: scale * jax.random.normal(next(ks), shape, f32)
    gain = lambda shape: 1.0 + 0.05 * jax.random.normal(next(ks), shape, f32)
    return {
        'x_prompt': nrm((BATCH, SEQ, D_MODEL), 1.0),
        'x_sample': nrm((DEC_BATCH, DEC_SEQ, D_MODEL), 1.0),
        'state_hgrn': nrm((N_EVEN, DEC_BATCH, A_HEADS, A_DK, A_DV), 0.5),
        'state_ret': nrm((N_EVEN, DEC_BATCH, B_HEADS, B_DK, B_DV), 0.5),
        'state_mlstm_c': nrm((N_ODD, DEC_BATCH, C_HEADS, C_DH, C_DH), 0.1),
        'state_mlstm_n': nrm((N_ODD, DEC_BATCH, C_HEADS, C_DH), 0.1),
        'state_mlstm_m': nrm((N_ODD, DEC_BATCH, C_HEADS), 1.0),
        'state_conv': nrm((N_ODD, DEC_BATCH, C_CONV - 1, C_INNER), 1.0),
        'norm_mix': gain((DEPTH, D_MODEL)),
        'norm_ffn': gain((DEPTH, D_MODEL)),
        'norm_final': gain((D_MODEL,)),
        'w_in0': nrm((N_EVEN, D_MODEL, IN0_WIDTH), D_MODEL ** -0.5),
        'lb_logits': nrm((N_EVEN + 1, A_KW), 0.5),
        'hgrn_norm': gain((N_EVEN, A_DV)),
        'ret_norm': gain((N_EVEN, B_DV)),
        'w_out0': nrm((N_EVEN, MIX_WIDTH, D_MODEL), MIX_WIDTH ** -0.5),
        'w_up1': nrm((N_ODD, D_MODEL, 2 * C_INNER), D_MODEL ** -0.5),
        'conv_w': nrm((N_ODD, C_CONV, C_INNER), C_CONV ** -0.5),
        'conv_b': nrm((N_ODD, C_INNER), 0.02),
        'w_q1': nrm((N_ODD, C_NBLK, C_BLOCK, C_BLOCK), C_BLOCK ** -0.5),
        'w_k1': nrm((N_ODD, C_NBLK, C_BLOCK, C_BLOCK), C_BLOCK ** -0.5),
        'w_v1': nrm((N_ODD, C_NBLK, C_BLOCK, C_BLOCK), C_BLOCK ** -0.5),
        'w_ig': nrm((N_ODD, 3 * C_INNER, C_HEADS), (3 * C_INNER) ** -0.5),
        'b_ig': nrm((N_ODD, C_HEADS), 0.1),
        'w_fg': nrm((N_ODD, 3 * C_INNER, C_HEADS), (3 * C_INNER) ** -0.5),
        'b_fg': jnp.linspace(3.0, 6.0, C_HEADS, dtype=f32)[None, :] + nrm((N_ODD, C_HEADS), 0.1),
        'mlstm_norm': gain((N_ODD, C_DH)),
        'mlstm_skip': gain((N_ODD, C_INNER)),
        'w_down1': nrm((N_ODD, C_INNER, D_MODEL), C_INNER ** -0.5),
        'w_ffn_gate': nrm((DEPTH, D_MODEL, D_FF), D_MODEL ** -0.5),
        'w_ffn_up': nrm((DEPTH, D_MODEL, D_FF), D_MODEL ** -0.5),
        'w_ffn_down': nrm((DEPTH, D_FF, D_MODEL), D_FF ** -0.5),
    }

def reference(x_prompt, x_sample, state_hgrn, state_ret, state_mlstm_c, state_mlstm_n, state_mlstm_m, state_conv,
              norm_mix, norm_ffn, norm_final, w_in0, lb_logits, hgrn_norm, ret_norm, w_out0,
              w_up1, conv_w, conv_b, w_q1, w_k1, w_v1, w_ig, b_ig, w_fg, b_fg, mlstm_norm, mlstm_skip, w_down1,
              w_ffn_gate, w_ffn_up, w_ffn_down):
    p = dict(norm_mix=norm_mix, norm_ffn=norm_ffn, norm_final=norm_final, w_in0=w_in0, lb_logits=lb_logits,
             hgrn_norm=hgrn_norm, ret_norm=ret_norm, w_out0=w_out0, w_up1=w_up1, conv_w=conv_w, conv_b=conv_b,
             w_q1=w_q1, w_k1=w_k1, w_v1=w_v1, w_ig=w_ig, b_ig=b_ig, w_fg=w_fg, b_fg=b_fg,
             mlstm_norm=mlstm_norm, mlstm_skip=mlstm_skip, w_down1=w_down1,
             w_ffn_gate=w_ffn_gate, w_ffn_up=w_ffn_up, w_ffn_down=w_ffn_down)
    zeros = lambda shape: jnp.zeros(shape, x_prompt.dtype)
    y_prompt, hg_p, rt_p, mc_p, mn_p, mm_p, cv_p = _trunk(
        x_prompt, 0,
        zeros((N_EVEN, BATCH, A_HEADS, A_DK, A_DV)), zeros((N_EVEN, BATCH, B_HEADS, B_DK, B_DV)),
        zeros((N_ODD, BATCH, C_HEADS, C_DH, C_DH)), zeros((N_ODD, BATCH, C_HEADS, C_DH)),
        zeros((N_ODD, BATCH, C_HEADS)), zeros((N_ODD, BATCH, C_CONV - 1, C_INNER)), p)
    y_sample, hg_s, rt_s, mc_s, mn_s, mm_s, cv_s = _trunk(
        x_sample, PAST_LEN, state_hgrn, state_ret, state_mlstm_c, state_mlstm_n, state_mlstm_m, state_conv, p)
    return (y_prompt, y_sample, hg_p, hg_s, rt_p, rt_s, mc_p, mc_s, mn_p, mn_s, mm_p, mm_s, cv_p, cv_s)


_drawn_inputs = setup_inputs


def setup_inputs(seed=0):
    import zlib

    import numpy as np

    out = dict(_drawn_inputs(seed))
    spreads = {}
    factors = {'mlstm_norm': 2.968, 'mlstm_skip': 4.634}
    for name, (base, spread) in spreads.items():
        noise = np.random.default_rng([zlib.crc32(name.encode()), seed]).standard_normal(out[name].shape)
        drawn = base * np.exp(spread * noise) if base else spread * noise
        out[name] = __import__('jax').numpy.asarray(drawn.astype(out[name].dtype))
    for name, factor in factors.items():
        out[name] = (out[name] * factor).astype(out[name].dtype)
    return out
```

```python
from contextlib import ExitStack

import concourse.bass as bass
from concourse import mybir

F32 = mybir.dt.float32
F32R = mybir.dt.float32r
U8 = mybir.dt.uint8
ACT = mybir.ActivationFunctionType
ALU = mybir.AluOpType

P = 128
D = 1024
SEQ, NB, TS = 512, 8, 16
NP = SEQ // P
T = SEQ + NB * TS
HT = T // 2
KD = D // P
H = 4
FF_PARTS = (16, 6)
CI = 16
KH = 4
DH = KH * P
NCONV = 4
XS = NCONV - 1 + TS
XW = NCONV - 1 + SEQ + NB * XS
EPS = 1e-6
NEVER = -1e30
LEVELS = (1, 2, 4, 8, 16, 32, 64)

U_IN0 = 0
U_OUT0 = U_IN0 + 32
FF_UNITS = sum(2 * f + 8 * (2 if f > 8 else 1) for f in FF_PARTS)
U_FF0 = U_OUT0 + 8
U_UP1 = U_FF0 + FF_UNITS
U_DN1 = U_UP1 + 32
U_FF1 = U_DN1 + 16
N_UNITS = U_FF1 + FF_UNITS

PAR = {}
_at = 0
for _name, _n in (("mix", 16), ("ffn", 16), ("final", 8), ("lb", 8), ("hgrn", 1), ("ret", 1), ("convw", 64),
                  ("convb", 16), ("mnorm", 4), ("skip", 16)):
    PAR[_name] = _at
    _at += _n
N_PAR = _at
CON = {}
_at = 0
for _name, _n in (("ident", 128), ("ones", 128), ("perm", 128), ("reset", T), ("ind", 8), ("tail", 8),
                  ("glast", 8), ("eps", 1), ("bd", 128), ("caus", 256), ("sel", 512)):
    CON[_name] = _at
    _at += _n
N_CON = _at


class Steps:

    def __init__(self, sem, names, base=0):
        self.sem, self.names, self.n, self.base = sem, {x: i + 1 for i, x in enumerate(names)}, len(names), base

    def at(self, name, r=0):
        return r * self.n + self.base + self.names[name]

    def rounds(self, r):
        return r * self.n + self.base


def trunk(nc, io):
    ctx = ExitStack()
    with ctx:
        sem = lambda name: ctx.enter_context(nc.semaphore(name))
        top = [16512]

        def sb(name, shape, dt=F32, at=None):
            n = mybir.dt.size(dt)
            for x in shape[1:]:
                n *= x
            n = (n + 31) // 32 * 32
            if at is None:
                off = top[0]
                top[0] += n
            else:
                off = at[0]
                at[0] += n
            assert top[0] <= 229312, (name, top[0])
            return nc.alloc_sbuf_tensor_at(name, shape, dt, offset=off)

        xT = sb("xT", [P, KD, T])
        at_h = top[0]
        xh = sb("xh", [P, KD, T], F32R)
        xl = sb("xl", [P, KD, T], F32R)
        wraw = [sb(f"wraw{s}", [P, KD, P]) for s in range(2)]
        whi = [sb(f"whi{s}", [P, KD, P], F32R) for s in range(2)]
        wlo = [sb(f"wlo{s}", [P, KD, P], F32R) for s in range(2)]
        at_a = top[0]
        ah = sb("ah", [P, CI, T], F32R)
        top[0] = at_a + CI * XW * 4
        al = sb("al", [P, CI, T], F32R)
        par = sb("par", [P, N_PAR])
        con = sb("con", [P, N_CON])
        masks = sb("masks", [P, len(LEVELS), P], U8)
        eps = con[:, CON["eps"]:CON["eps"] + 1]
        ident = con[:, CON["ident"]:CON["ident"] + P]
        ones = con[:, CON["ones"]:CON["ones"] + P]
        perm = con[:, CON["perm"]:CON["perm"] + P]
        reset = con[:, CON["reset"]:CON["reset"] + T]
        at_r = top[0]

        a0, r0 = [at_a], [at_r]
        zq, zf, zi, zg, zbq, zbk, zbv, zbg = [sb(f"z_{x}", [P, T], at=a0) for x in
                                              ("aq", "af", "ai", "ag", "bq", "bk", "bv", "bg")]
        mix = sb("mix", [P, 8, T], at=a0)
        ga = {x: sb(f"a_{x}", [P, T], at=a0) for x in ("f", "k", "b", "eb", "q", "kh", "att")}
        dlev = [sb(f"dlev{s}", [P, T], at=a0) for s in range(2)]
        qk = [sb(f"qk{s}", [P, T], at=a0) for s in range(2)]
        cos = sb("cos", [P, T], at=a0)
        sin = sb("sin", [P, T], at=a0)
        dret = sb("dret", [P, 2, P], at=a0)
        win = sb("win", [P, 2, P], at=a0)
        bst = sb("bst", [P, P], at=a0)
        ast = sb("ast", [P, P], at=a0)
        lbt = sb("lbt", [P, 5, H], at=a0)
        assert a0[0] <= at_a + 2 * 16 * T * 4, a0[0] - at_a
        gb = {x: sb(f"b_{x}", [P, T], at=r0) for x in ("q", "k", "t", "kt", "vt")}
        ga["kt"] = sb("a_kt", [P, T], at=r0)
        ga["vt"] = sb("a_vt", [P, T], at=r0)
        asmp = sb("asmp", [P, NB, P], at=r0)
        bsmp = sb("bsmp", [P, NB, P], at=r0)
        vmask = sb("vmask", [P, NB, P], at=r0)
        assert r0[0] <= 229312, r0[0]
        n0 = [at_r]
        sq = [sb(f"sq{s}", [P, T], at=n0) for s in range(2)]
        nacc = sb("nacc", [P, T], at=n0)
        rstd = sb("rstd", [P, T], at=n0)
        ntmp = [sb(f"ntmp{s}", [P, T], at=n0) for s in range(2)]
        ffs = [sb(f"ffs{s}", [P, T], at=n0) for s in range(2)]
        fft = [sb(f"fft{s}", [P, T], at=n0) for s in range(2)]

        psd = [ctx.enter_context(nc.psum_tensor(f"psd{s}", [P, 2, 512], F32)) for s in range(2)]
        psm = ctx.enter_context(nc.psum_tensor("psm", [P, 4, 512], F32))

        w_loaded = [sem(f"w_loaded{s}") for s in range(2)]
        w_taken = sem("w_taken")
        w_high = sem("w_high")
        w_split = sem("w_split")
        pe_unit = sem("pe_unit")
        evac = [sem(f"evac{s}") for s in range(2)]
        con_in = sem("con_in")
        x_in = sem("x_in")
        out_sem = sem("out_sem")

        def halves(t, k, cut):
            return t[:, k, 0:cut], t[:, k, cut:T]

        def two(ap):
            return ap.rearrange("p (a c) -> p a c", a=2)

        def pe_dense(pe, n, g, hi, lo, k0=0, nk=8, first=True, last=True, ready=None, between=None, cut=HT):
            (nc_, ne), (gc, ge) = n, g
            slot, pair = nc_ % 2, gc % 2
            pe.wait_ge(w_split, nc_ + 2 * ne + 1)
            if first and not (isinstance(ge, int) and gc + 2 * ge < 2):
                pe.wait_ge(evac[pair], gc // 2 + ge)
            for k in range(nk):
                if ready is not None:
                    pe.wait_ge(ready[0], ready[1] + k)
                x0, x1 = halves(hi, k0 + k, cut)
                l0, l1 = halves(lo, k0 + k, cut)
                wh, wl = whi[slot][:, k, :], wlo[slot][:, k, :]
                o0, o1 = psd[pair][:, 0, 0:cut], psd[pair][:, 1, 0:T - cut]
                st, en = first and k == 0, last and k == nk - 1
                pe.matmul(o0, wh, x0, start=st, stop=False)
                pe.matmul(o1, wh, x1, start=st, stop=False)
                pe.matmul(o0, wh, l0, start=False, stop=False)
                pe.matmul(o1, wh, l1, start=False, stop=False)
                pe.matmul(o0, wl, x0, start=False, stop=en)
                mm = pe.matmul(o1, wl, x1, start=False, stop=en)
                if k == nk // 2 - 1 and between is not None:
                    between()
            mm.then_inc(pe_unit, 1)

        class Norm:

            def __init__(self, name, gain, g, free_at, x_at, final=False):
                self.sq_done = sem(f"{name}_sq")
                self.acc_done = sem(f"{name}_acc")
                self.sum_done = sem(f"{name}_sum")
                self.std_done = sem(f"{name}_std")
                self.v_done = sem(f"{name}_v")
                self.hi_done = sem(f"{name}_hi")
                self.lo_done = sem(f"{name}_lo")
                self.gain, self.g, self.free_at, self.x_at, self.final = gain, g, free_at, x_at, final

            def act(self, a):
                for k in range(KD):
                    a.wait_ge(*self.x_at(k))
                    if k >= 2:
                        a.wait_ge(self.acc_done, k - 1)
                    a.activation(sq[k % 2][:], xT[:, k, :], ACT.Square).then_inc(self.sq_done, 1)
                a.wait_ge(self.sum_done, 1)
                a.activation(two(rstd[:]), psd[self.g % 2][:, :, 0:HT], ACT.Sqrt, bias=eps,
                             scale=1.0 / D).then_inc(self.std_done, 1)
                a.wait_ge(self.std_done, 1)
                a.sem_inc(evac[self.g % 2], 1)
                if self.final:
                    return
                a.wait_ge(pe_unit, self.free_at)
                for k in range(KD):
                    a.wait_ge(self.v_done, k + 2)
                    a.activation(xh[:, k, :], ntmp[k % 2][:], ACT.Copy).then_inc(self.hi_done, 1)

            def vec(self, v):
                for k in range(KD):
                    v.wait_ge(self.sq_done, k + 1)
                    if k == 0:
                        v.tensor_copy(nacc[:], sq[0][:]).then_inc(self.acc_done, 1)
                    else:
                        v.wait_ge(self.acc_done, k)
                        v.tensor_tensor(nacc[:], nacc[:], sq[k % 2][:], ALU.add).then_inc(self.acc_done, 1)
                v.wait_ge(self.std_done, 1)
                v.reciprocal(rstd[:], rstd[:]).then_inc(self.v_done, 1)
                v.wait_ge(self.v_done, 1)
                for k in range(KD + 1):
                    if k < KD:
                        if k >= 2 and self.final:
                            v.wait_ge(y_stored[k % 2], 16 * (k // 2))
                        elif k >= 2:
                            v.wait_ge(self.lo_done, k - 1)
                        v.scalar_tensor_tensor(ntmp[k % 2][:], xT[:, k, :], par[:, self.gain + k:self.gain + k + 1],
                                               rstd[:], ALU.mult, ALU.mult).then_inc(self.v_done, 1)
                    if k >= 1 and not self.final:
                        v.wait_ge(self.hi_done, k)
                        v.tensor_tensor(xl[:, k - 1, :], ntmp[(k - 1) % 2][:], xh[:, k - 1, :].bitcast(F32),
                                        ALU.subtract).then_inc(self.lo_done, 1)

            def pe(self, p):
                p.wait_ge(self.acc_done, KD)
                if self.g >= 2:
                    p.wait_ge(evac[self.g % 2], self.g // 2)
                p.matmul(psd[self.g % 2][:, 0, 0:HT], ones, nacc[:, 0:HT], start=True, stop=True)
                p.matmul(psd[self.g % 2][:, 1, 0:HT], ones, nacc[:, HT:T], start=True,
                         stop=True).then_inc(self.sum_done, 1)

        G_N0 = 0
        G_IN0 = 1
        G_OUT0 = G_IN0 + 32
        G_N1 = G_OUT0 + 8
        G_FF0 = G_N1 + 1
        N_FF = sum(2 * f + 8 for f in FF_PARTS)
        G_N2 = G_FF0 + N_FF
        G_UP1 = G_N2 + 1
        G_DN1 = G_UP1 + 32
        G_N3 = G_DN1 + 8
        G_FF1 = G_N3 + 1
        G_NF = G_FF1 + N_FF

        def left(g):
            return evac[g % 2], g // 2 + 1
        y_stored = [sem(f"y_stored{s}") for s in range(2)]
        norm0 = Norm("n0", PAR["mix"], G_N0, 0, lambda k: (x_in, 16))
        norm1 = Norm("n1", PAR["ffn"], G_N1, U_FF0, lambda k: left(G_OUT0 + k))
        norm2 = Norm("n2", PAR["mix"] + 8, G_N2, U_UP1, lambda k: left(G_N2 - 8 + k))
        norm3 = Norm("n3", PAR["ffn"] + 8, G_N3, U_FF1, lambda k: left(G_DN1 + k))
        normf = Norm("nf", PAR["final"], G_NF, None, lambda k: left(G_NF - 8 + k), final=True)

        NL = len(LEVELS)
        z_done = Steps(sem("z_done"), ["aq", "af", "ai", "ag", "bq", "bk", "bv", "bg"])
        lv = [("p", l) for l in range(NL + 1)]
        aV = Steps(sem("aV"), ["f", "k", "b", "q", "dk0", "dk1", "kh"]
                   + [x for l in range(NL) for x in ((("d1", l), ("d0", l)))][:2] + [("cp", 0)]
                   + [x for l in range(NL) for x in (
                       [("qk1", l), ("qk0", l)] + ([("d1", l + 1), ("d0", l + 1)] if l + 1 < NL else []) + [("cp", l + 1)])]
                   + ["S0", "S1", "S2", "S3", "vm", "Sd", "Sa0", "Sa1", "u0", "u1", "mixg", "mixn"])
        aS = Steps(sem("aS"), ["ln", "eb", "ek"] + [("g", l) for l in range(NL)] + ["vt", "kt", "sq", "lnr", "r"])
        aP = Steps(sem("aP"), [("p", l) for l in range(NL + 1)] + ["vt", "kt", "st0", "o0", "st1", "o1", "st2", "o2",
                   "st3", "o3", "s0", "s1", "oS", "n"])
        bV = Steps(sem("bV"), ["tq", "sq", "q", "tk", "sk", "k", "d0", "d1", "qh0", "qh1",
                   "S0", "S1", "S2", "S3", "vm", "Sa0", "Sa1", "u0", "u1", "mixn", "mixg"])
        bS = Steps(sem("bS"), ["vt", "kt0", "kt1", "sq", "lnr", "r"])
        bP = Steps(sem("bP"), ["pq", "pk", "vt", "kt", "att", "st0", "o0", "st1", "o1", "st2", "o2",
                   "st3", "o3", "s0", "s1", "oS", "n"])
        a_in = sem("a_in")
        b_in = sem("b_in")
        a_out = sem("a_out")
        b_out = sem("b_out")
        lb_done = sem("lb_done")
        lb_act = sem("lb_act")
        cp_turn = sem("cp_turn")

        bank = [psm[:, i, :] for i in range(4)]

        def tt(i):
            return slice(i * P, (i + 1) * P)

        def a_pe_level(pe, h, l):
            if l == 0:
                pe.wait_ge(aV.sem, aV.at("k", h))
            else:
                pe.wait_ge(aV.sem, aV.at(("qk0", l - 1), h))
            b0, b1 = bank[2 * (l % 2)], bank[2 * (l % 2) + 1]
            if l == 1 and not (isinstance(h, int) and h == 0):
                pe.wait_ge(bS.sem, bS.at("lnr", h - 1))
            if l >= 2:
                pe.wait_ge(aV.sem, aV.at(("cp", l - 2), h))
            tiles = NP + (l == 0 or LEVELS[l - 1] < TS)
            for t in range(tiles):
                lhs = ga["k"][:, tt(t)] if l == 0 else qk[(l - 1) % 2][:, tt(t)]
                rhs = zq[:, tt(t)] if l == 0 else lhs
                o = b0[:, tt(t)] if t < NP else b1[:, 0:P]
                mm = pe.matmul(o, lhs, rhs, start=True, stop=True)
            mm.then_inc(aP.sem, 1)

        def pe_turn(pe, src, b0, b1, done):
            for t in range(NP + 1):
                o = b0[:, tt(t)] if t < NP else b1[:, 0:P]
                mm = pe.transpose(o, src[:, tt(t)], ident)
            mm.then_inc(done, 1)

        def pe_states(pe, h, g, PS, VS, kt_at, SS, att, q, S, t0, t1):
            for t in range(t0, t1):
                if t == 0:
                    pe.wait_ge(SS.sem, SS.at(kt_at, h))
                else:
                    pe.wait_ge(VS.sem, VS.at(f"S{t - 1}", h))
                pe.matmul(bank[2 + t % 2][:, 0:P], g["kt"][:, tt(t)], g["vt"][:, tt(t)], start=True,
                          stop=True).then_inc(PS.sem, 1)
                mm = pe.matmul(bank[0][:, tt(t)], g["vt"][:, tt(t)], att[:, tt(t)], start=True, stop=(t == 0))
                if t > 0:
                    mm = pe.matmul(bank[0][:, tt(t)], S[:], q[:, tt(t)], start=False, stop=True)
                mm.then_inc(PS.sem, 1)

        def pe_sample(pe, h, g, PS, VS, smp, s_in, att, q):
            pe.wait_ge(s_in, 16 * (h + 1))
            pe.wait_ge(VS.sem, VS.at("vm", h))
            for r in range(2):
                pe.matmul(bank[2 + r], g["kt"][:, tt(NP)], vmask[:, 4 * r:4 * r + 4, :].rearrange("p b v -> p (b v)"),
                          start=True, stop=True).then_inc(PS.sem, 1)
            for b in range(NB):
                c = b * TS
                pe.matmul(bank[1][:, c:c + TS], smp[:, b, :], q[:, SEQ + c:SEQ + c + TS], start=(b == 0), stop=False,
                          skip_group_check=True)
            mm = pe.matmul(bank[1][:, 0:P], g["vt"][:, tt(NP)], att[:, tt(NP)], start=False, stop=True,
                           skip_group_check=True)
            mm.then_inc(PS.sem, 1)

        def pe_headnorm(pe, h, PS, SS, src):
            pe.wait_ge(SS.sem, SS.at("sq", h))
            pe.matmul(bank[2][:, 0:HT], ones, src[:, 0:HT], start=True, stop=True)
            pe.matmul(bank[3][:, 0:HT], ones, src[:, HT:T], start=True, stop=True).then_inc(PS.sem, 1)

        def a_pe_turns(pe, h):
            pe.wait_ge(aV.sem, aV.at(("cp", NL - 1), h))
            pe_turn(pe, zi, bank[0], bank[1], aP.sem)
            pe.wait_ge(aV.sem, aV.at(("cp", NL), h))
            pe_turn(pe, ga["kh"], bank[2], bank[3], aP.sem)

        def a_pe_head(pe, h):
            pe_states(pe, h, ga, aP, aV, "kt", aS, ga["att"], ga["q"], ast, 0, NP)

        def a_pe_tail(pe, h):
            pe.wait_ge(aV.sem, aV.at("S3", h))
            pe_sample(pe, h, ga, aP, aV, asmp, a_in, ga["att"], ga["q"])

        def a_pe_norm(pe, h):
            pe_headnorm(pe, h, aP, aS, ga["kh"])

        def b_pe_rot(pe, h):
            pe.wait_ge(z_done.sem, z_done.at("bk", h))
            pe.wait_ge(aS.sem, aS.at("r", h))
            pe.matmul(bank[0][:, 0:HT], perm, zbq[:, 0:HT], start=True, stop=True)
            pe.matmul(bank[1][:, 0:HT], perm, zbq[:, HT:T], start=True, stop=True).then_inc(bP.sem, 1)
            pe.matmul(bank[2][:, 0:HT], perm, zbk[:, 0:HT], start=True, stop=True)
            pe.matmul(bank[3][:, 0:HT], perm, zbk[:, HT:T], start=True, stop=True).then_inc(bP.sem, 1)

        def b_pe_turns(pe, h):
            pe.wait_ge(z_done.sem, z_done.at("bv", h))
            pe.wait_ge(bV.sem, bV.at("sq", h))
            pe_turn(pe, zbv, bank[0], bank[1], bP.sem)
            pe.wait_ge(bV.sem, bV.at("k", h))
            pe_turn(pe, gb["k"], bank[2], bank[3], bP.sem)

        def b_pe_scores(pe, h):
            pe.wait_ge(bS.sem, bS.at("vt", h))
            for t in range(NP + 1):
                o = bank[0][:, tt(t)] if t < NP else bank[1][:, 0:P]
                mm = pe.matmul(o, gb["k"][:, tt(t)], gb["q"][:, tt(t)], start=True, stop=True)
            mm.then_inc(bP.sem, 1)

        def b_pe_states(pe, h):
            pe.wait_ge(bV.sem, bV.at("qh1", h))
            pe_states(pe, h, gb, bP, bV, "kt1", bS, gb["t"], gb["q"], bst, 0, NP)

        def b_pe_tail(pe, h):
            pe.wait_ge(bV.sem, bV.at("S3", h))
            pe_sample(pe, h, gb, bP, bV, bsmp, b_in, gb["t"], gb["q"])

        def b_pe_norm(pe, h):
            pe_headnorm(pe, h, bP, bS, gb["k"])

        def in0_unit(pe, h, j, between=None, ready=None):
            pe_dense(pe, (U_IN0 + j, 4 * h), (G_IN0 + j, 4 * h), xh, xl, between=between, ready=ready)

        def seqs(ap, lo, n, w):
            return ap[:, lo:lo + n * w].rearrange("p (n w) -> p n w", w=w)

        def a_vec_gates(v, h):
            lbh, omh = lbt[:, 3, bass.ds(h, 1)], lbt[:, 4, bass.ds(h, 1)]
            v.wait_ge(z_done.sem, z_done.at("af", h))
            v.tensor_scalar(ga["f"][:], zf[:], omh, lbh, ALU.mult, ALU.add).then_inc(aV.sem, 1)
            v.wait_ge(aV.sem, aV.at("f", h))
            v.tensor_scalar(ga["k"][:], ga["f"][:], -1.0, 1.0, ALU.mult, ALU.add).then_inc(aV.sem, 1)
            v.wait_ge(aS.sem, aS.at("ln", h))
            v.tensor_tensor_scan(ga["b"][:], reset, ga["f"][:], 0.0, ALU.mult, ALU.add).then_inc(aV.sem, 1)
            v.wait_ge(aS.sem, aS.at("eb", h))
            v.tensor_tensor(ga["q"][:], zq[:], ga["eb"][:], ALU.mult).then_inc(aV.sem, 1)
            for lo, n, w in ((0, NP, P), (SEQ, NB, TS)):
                b = seqs(ga["b"], lo, n, w)
                v.tensor_tensor(seqs(ga["kh"], lo, n, w), b[:, :, w - 1:w].broadcast_to([P, n, w]), b,
                                ALU.subtract).then_inc(aV.sem, 1)
            v.wait_ge(aS.sem, aS.at("ek", h))
            v.tensor_tensor(ga["kh"][:], ga["k"][:], ga["kh"][:], ALU.mult).then_inc(aV.sem, 1)

        def width(l):
            return T if LEVELS[l] < TS else SEQ

        def a_vec_diff(v, h, l):
            m = LEVELS[l]
            n = width(l) // (2 * m)
            b = ga["b"][:, 0:width(l)].rearrange("p (n s m) -> p n s m", s=2, m=m)
            d = dlev[l % 2][:, 0:width(l)].rearrange("p (n s m) -> p n s m", s=2, m=m)
            mid = b[:, :, 0, m - 1:m].broadcast_to([P, n, m])
            if l == 0:
                v.wait_ge(aV.sem, aV.at("b", h))
            v.tensor_tensor(d[:, :, 1, :], b[:, :, 1, :], mid, ALU.subtract).then_inc(aV.sem, 1)
            v.tensor_tensor(d[:, :, 0, :], mid, b[:, :, 0, :], ALU.subtract).then_inc(aV.sem, 1)

        def a_vec_qk(v, h, l):
            m = LEVELS[l]
            four = lambda x: x[:, 0:width(l)].rearrange("p (n s m) -> p n s m", s=2, m=m)
            g, o = four(dlev[l % 2]), four(qk[l % 2])
            v.wait_ge(aS.sem, aS.at(("g", l), h))
            if l >= 2:
                v.wait_ge(aP.sem, aP.at(("p", l - 1), h))
            v.tensor_tensor(o[:, :, 1, :], four(zq)[:, :, 1, :], g[:, :, 1, :], ALU.mult).then_inc(aV.sem, 1)
            v.tensor_tensor(o[:, :, 0, :], four(ga["k"])[:, :, 0, :], g[:, :, 0, :], ALU.mult).then_inc(aV.sem, 1)

        def a_vec_take(v, h, l):
            b0, b1 = 2 * (l % 2), 2 * (l % 2) + 1
            att = ga["att"]
            v.wait_ge(aP.sem, aP.at(("p", l), h))
            if l == 0:
                v.tensor_tensor(seqs(att, 0, NP, P), bank[b0].rearrange("p (n w) -> p n w", w=P),
                                ident.unsqueeze(1).broadcast_to([P, NP, P]), ALU.mult)
                v.tensor_tensor(att[:, SEQ:T], bank[b1][:, 0:P], ident, ALU.mult).then_inc(aV.sem, 1)
                return
            mk = masks[:, l - 1, :]
            v.wait_ge(aV.sem, aV.at(("cp", l - 1), h))
            v.sem_inc(cp_turn, 1)
            if LEVELS[l - 1] < TS:
                v.copy_predicated(att[:, SEQ:T], mk, bank[b1][:, 0:P])
            v.copy_predicated(seqs(att, 0, NP, P), mk.unsqueeze(1).broadcast_to([P, NP, P]),
                              bank[b0].rearrange("p (n w) -> p n w", w=P)).then_inc(aV.sem, 1)

        def a_vec_levels(v, h):
            a_vec_diff(v, h, 0)
            a_vec_take(v, h, 0)
            for l in range(NL):
                a_vec_qk(v, h, l)
                if l + 1 < NL:
                    a_vec_diff(v, h, l + 1)
                a_vec_take(v, h, l + 1)

        def vec_prompt_states(v, h, PS, VS, S, out, decay):
            for t in range(NP):
                v.wait_ge(PS.sem, PS.at(f"st{t}", h))
                src = bank[2 + t % 2][:, 0:P]
                if t == 0:
                    if not isinstance(h, int) or h:
                        v.wait_ge(out, 16 * (2 * h))
                    v.tensor_copy(S[:], src).then_inc(VS.sem, 1)
                else:
                    v.wait_ge(PS.sem, PS.at(f"o{t}", h))
                    v.wait_ge(VS.sem, VS.at(f"S{t - 1}", h))
                    v.scalar_tensor_tensor(S[:], S[:], decay(t), src, ALU.mult, ALU.add).then_inc(VS.sem, 1)

        def vec_mask_v(v, h, g, VS, SS):
            ind = con[:, CON["ind"]:CON["ind"] + NB]
            v.wait_ge(SS.sem, SS.at("vt", h))
            v.tensor_tensor(vmask[:], g["vt"][:, tt(NP)].unsqueeze(1).broadcast_to([P, NB, P]),
                            ind.unsqueeze(2).broadcast_to([P, NB, P]), ALU.mult).then_inc(VS.sem, 1)

        def a_vec_states(v, h):
            vec_prompt_states(v, h, aP, aV, ast, a_out, lambda t: ga["eb"][:, t * P + P - 1:t * P + P])

        def a_vec_tail(v, h):
            vec_mask_v(v, h, ga, aV, aS)
            v.wait_ge(aP.sem, aP.at("oS", h))
            dec = seqs(ga["eb"], SEQ, NB, TS)[:, :, TS - 1:TS].broadcast_to([P, NB, P])
            v.tensor_tensor(asmp[:], asmp[:], dec, ALU.mult).then_inc(aV.sem, 1)
            v.wait_ge(aV.sem, aV.at("Sd", h))
            for r in range(2):
                s = asmp[:, 4 * r:4 * r + 4, :].rearrange("p b v -> p (b v)")
                v.tensor_tensor(s, s, bank[2 + r], ALU.add).then_inc(aV.sem, 1)
            v.wait_ge(z_done.sem, z_done.at("ag", h))
            v.tensor_tensor(ga["att"][:, 0:SEQ], bank[0], zg[:, 0:SEQ], ALU.mult).then_inc(aV.sem, 1)
            v.tensor_tensor(ga["att"][:, SEQ:T], bank[1][:, 0:P], zg[:, SEQ:T], ALU.mult).then_inc(aV.sem, 1)
            v.wait_ge(aV.sem, aV.at("u1", h))
            v.tensor_scalar(mix[:, bass.ds(h, 1), :].rearrange("p a c -> p (a c)"), ga["att"][:],
                            par[:, PAR["hgrn"]:PAR["hgrn"] + 1], None, ALU.mult).then_inc(aV.sem, 1)
            v.wait_ge(aS.sem, aS.at("r", h))
            v.wait_ge(aV.sem, aV.at("mixg", h))
            m = mix[:, bass.ds(h, 1), :].rearrange("p a c -> p (a c)")
            v.tensor_tensor(m, m, ga["kh"][:], ALU.mult).then_inc(aV.sem, 1)

        def b_vec_rot(v, h):
            for z, o, b0, st in ((zbq, gb["q"], 0, ("tq", "sq", "pq")), (zbk, gb["k"], 2, ("tk", "sk", "pk"))):
                if b0 == 0:
                    v.wait_ge(z_done.sem, z_done.at("bk", h))
                v.tensor_tensor(o[:], z[:], cos[:], ALU.mult).then_inc(bV.sem, 1)
                v.wait_ge(bP.sem, bP.at(st[2], h))
                v.tensor_tensor(two(gb["t"][:]), psm[:, b0:b0 + 2, 0:HT], two(sin[:]), ALU.mult).then_inc(bV.sem, 1)
                v.wait_ge(bV.sem, bV.at(st[1], h))
                v.tensor_tensor(o[:], o[:], gb["t"][:], ALU.add).then_inc(bV.sem, 1)
                v.wait_ge(bV.sem, bV.at("q" if b0 == 0 else "k", h))

        def b_vec_scores(v, h):
            v.wait_ge(bP.sem, bP.at("att", h))
            v.wait_ge(b_in, 16 * 3 * (h + 1))
            v.tensor_tensor(seqs(gb["t"], 0, NP, P), bank[0].rearrange("p (n w) -> p n w", w=P),
                            dret[:, 0:1, :].broadcast_to([P, NP, P]), ALU.mult).then_inc(bV.sem, 1)
            v.tensor_tensor(gb["t"][:, SEQ:T], bank[1][:, 0:P], dret[:, 1, :], ALU.mult).then_inc(bV.sem, 1)
            v.tensor_tensor(seqs(gb["q"], 0, NP, P), seqs(gb["q"], 0, NP, P),
                            win[:, 0:1, :].broadcast_to([P, NP, P]), ALU.mult).then_inc(bV.sem, 1)
            v.tensor_tensor(gb["q"][:, SEQ:T], gb["q"][:, SEQ:T], win[:, 1, :], ALU.mult).then_inc(bV.sem, 1)

        def b_vec_states(v, h):
            vec_prompt_states(v, h, bP, bV, bst, b_out,
                              lambda t: con[:, bass.ds(CON["glast"] + 2 * h, 1)])

        def b_vec_tail(v, h):
            vec_mask_v(v, h, gb, bV, bS)
            v.wait_ge(bP.sem, bP.at("oS", h))
            for r in range(2):
                s = bsmp[:, 4 * r:4 * r + 4, :].rearrange("p b v -> p (b v)")
                v.scalar_tensor_tensor(s, s, con[:, bass.ds(CON["glast"] + 2 * h + 1, 1)], bank[2 + r], ALU.mult,
                                       ALU.add).then_inc(bV.sem, 1)
            v.tensor_copy(gb["t"][:, 0:SEQ], bank[0]).then_inc(bV.sem, 1)
            v.tensor_copy(gb["t"][:, SEQ:T], bank[1][:, 0:P]).then_inc(bV.sem, 1)
            v.wait_ge(bS.sem, bS.at("r", h))
            v.scalar_tensor_tensor(gb["t"][:], gb["t"][:], par[:, PAR["ret"]:PAR["ret"] + 1], gb["k"][:], ALU.mult,
                                   ALU.mult).then_inc(bV.sem, 1)
            v.wait_ge(bV.sem, bV.at("mixn", h))
            v.wait_ge(z_done.sem, z_done.at("bg", h))
            v.tensor_tensor(mix[:, bass.ds(h + 4, 1), :].rearrange("p a c -> p (a c)"), gb["t"][:], zbg[:],
                            ALU.mult).then_inc(bV.sem, 1)

        def in0_evac(a, h, j):
            name = ["aq", "af", "ai", "ag", "bq", "bk", "bv", "bg"][j]
            func = {"af": ACT.Sigmoid, "ag": ACT.Sigmoid, "bg": ACT.Silu}.get(name, ACT.Copy)
            dst = (zq, zf, zi, zg, zbq, zbk, zbv, zbg)[j]
            again = not isinstance(h, int) or h > 0
            if again:
                user = {"aq": (aV, ("qk1", NL - 1)), "af": (aV, "f"), "ai": (aP, "vt"), "ag": (aV, "u1"),
                        "bq": (bV, "k"), "bk": (bV, "k"), "bv": (bP, "vt"), "bg": (bV, "mixg")}[name]
                a.wait_ge(user[0].sem, user[0].at(user[1], h - 1))
                if name == "bk":
                    a.wait_ge(bP.sem, bP.at("pk", h - 1))
                if name == "bq":
                    a.wait_ge(bP.sem, bP.at("pq", h - 1))
                if name == "aq":
                    a.wait_ge(aP.sem, aP.at(("p", 0), h - 1))
            n = U_IN0 + j
            a.wait_ge(pe_unit, n + 8 * h + 1)
            g = G_IN0 + j
            scale = float(P) ** -0.5 if name == "bk" else 1.0
            a.activation(two(dst[:]), psd[g % 2][:, :, 0:HT], func, scale=scale).then_inc(z_done.sem, 1)
            a.wait_ge(z_done.sem, z_done.at(name, h))
            a.sem_inc(evac[g % 2], 1)

        def a_act_gates(a, h):
            a.wait_ge(aV.sem, aV.at("k", h))
            a.activation(ga["f"][:], ga["f"][:], ACT.Ln).then_inc(aS.sem, 1)
            a.wait_ge(aV.sem, aV.at("b", h))
            a.activation(ga["eb"][:], ga["b"][:], ACT.Exp).then_inc(aS.sem, 1)
            a.wait_ge(aV.sem, aV.at("dk1", h))
            a.activation(ga["kh"][:], ga["kh"][:], ACT.Exp).then_inc(aS.sem, 1)

        def a_act_level(a, h, l):
            a.wait_ge(aV.sem, aV.at(("d0", l), h))
            d = dlev[l % 2][:, 0:width(l)]
            a.activation(d, d, ACT.Exp).then_inc(aS.sem, 1)

        def act_turned(a, h, dst, b0, PS, SS, name, scales=(1.0, 1.0), steps=1):
            a.wait_ge(PS.sem, PS.at(name, h))
            i = a.activation(dst[:, 0:SEQ], bank[b0], ACT.Copy, scale=scales[0])
            if steps == 2:
                i.then_inc(SS.sem, 1)
            a.activation(dst[:, SEQ:T], bank[b0 + 1][:, 0:P], ACT.Copy, scale=scales[1]).then_inc(SS.sem, 1)

        def a_act_turns(a, h):
            act_turned(a, h, ga["vt"], 0, aP, aS, "vt")
            act_turned(a, h, ga["kt"], 2, aP, aS, "kt")

        def act_headnorm(a, h, PS, VS, SS, src, buf):
            a.wait_ge(VS.sem, VS.at("u1", h))
            a.activation(buf[:], src[:], ACT.Square).then_inc(SS.sem, 1)
            a.wait_ge(PS.sem, PS.at("n", h))
            a.activation(two(buf[:]), psm[:, 2:4, 0:HT], ACT.Ln, bias=eps, scale=1.0 / P).then_inc(SS.sem, 1)
            a.wait_ge(SS.sem, SS.at("lnr", h))
            a.activation(buf[:], buf[:], ACT.Exp, scale=-0.5).then_inc(SS.sem, 1)

        def a_act_norm(a, h):
            act_headnorm(a, h, aP, aV, aS, ga["att"], ga["kh"])

        def b_act_turns(a, h):
            act_turned(a, h, gb["vt"], 0, bP, bS, "vt")
            tail = lambda i: con[:, bass.ds(CON["tail"] + 2 * h + i, 1)]
            act_turned(a, h, gb["kt"], 2, bP, bS, "kt", (tail(0), tail(1)), 2)

        def b_act_norm(a, h):
            act_headnorm(a, h, bP, bV, bS, gb["t"], gb["k"])

        mh = sem("mh")
        ml = sem("ml")

        kept = sem("kept")
        x1, h1, r1 = [16512], [at_h], [at_r]
        xp = sb("xp", [P, CI, XW], at=[at_a])
        xc = sb("xc", [P, CI, T], at=[at_a + CI * XW * 4])
        assert nc.sbuf_base >= 0
        qT, kT = sb("qT", [P, KH, T], at=h1), sb("kT", [P, KH, T], at=h1)
        ktok = sb("ktok", [P, NP + 1, DH], at=h1)
        zt = sb("zt", [P, KH, T], at=[h1[0] - 4 * (NP + 1) * DH])
        vtok = sb("vtok", [P, NP + 1, DH], at=h1)
        wqkv = sb("wqkv", [P, 3, CI, 4], at=r1)
        nS = sb("nS", [P, H, KH, NB], at=r1)
        nP = sb("nP", [P, H, KH], at=r1)
        acol = sb("acol", [P, NP + 1, H], at=r1)
        rowM = sb("rowM", [H, T], at=r1)
        rowW = sb("rowW", [H, T], at=r1)
        rowE = sb("rowE", [H, T], at=r1)
        selh = sb("selh", [H, P], at=r1)
        wl = sb("wl", [P, NP + 1], at=r1)
        dec = sb("dec", [P, NP + NB], at=r1)
        gsm = sb("gsm", [H, 2 + NB], at=r1)
        mo = sb("mo", [H, 1 + NB], at=r1)
        r2 = [r1[0]]
        cv = [sb(f"cv{s}", [P, T], at=r2) for s in range(2)]
        zb = [sb(f"zb{s}", [P, T], at=r2) for s in range(2)]
        cst = sb("cst", [P, CI, NB, NCONV - 1], at=r2)
        cpo = sb("cpo", [P, CI, NCONV - 1], at=r2)
        gt = sb("gt", [P, CI, 8], at=r2)
        gC = sb("gC", [P, CI, 8], at=r2)
        gX = sb("gX", [P, CI, 8], at=r2)
        wgx = sb("wgx", [P, 3, CI, 4, 8], at=r2)
        assert r2[0] <= 229312, r2[0]
        pre = sb("pre", [8, T], at=x1)
        fgr, igr, t1, bro, mro, i2, l2 = [sb(f"row_{n}", [H, T], at=x1) for n in
                                          ("f", "i", "t", "b", "m", "i2", "l2")]
        assert x1[0] <= at_h
        r3, x3 = [r1[0]], [16512]
        Cs = [sb(f"Cs{s}", [P, KH, DH], at=x3) for s in range(2)]
        blk = [sb(f"blk{s}", [P, 3, P], at=x3) for s in range(2)]
        assert x3[0] <= at_h
        Cp = sb("Cp", [P, KH, DH], at=r3)
        att1 = sb("att1", [P, T], at=r3)
        vtmp = [sb(f"vtmp{s}", [P, T], at=r3) for s in range(2)]
        rs_at = [r3[0]]
        kw = sb("kw", [P, DH], at=r3)
        vm = [sb(f"vm{s}", [P, DH], at=r3) for s in range(2)]
        rs = sb("rs", [P, T], at=rs_at)
        assert r3[0] <= 229312, r3[0]

        flat = lambda p: p.rearrange("p a c -> p (a c)")
        pD = [flat(psd[s][:, :, :]) for s in range(2)]
        pM = [flat(psm[:, 2 * s:2 * s + 2, :]) for s in range(2)]
        U = [bank[2], bank[3], psd[0][:, 0, :], psd[0][:, 1, :]]
        tiles5 = range(NP + 1)

        def streams(ap, c0, w):
            return ap[:, NCONV - 1 + SEQ:XW].rearrange("p (b c) -> p b c", c=XS)[:, :, c0:c0 + w]

        class MLstm:
            def __init__(self):
                self.w_in = sem("m_w_in")
                self.pad = sem("m_pad")
                self.conv = sem("m_conv")
                self.xc = sem("m_xc")
                self.zsil = sem("m_zsil")
                self.zst = [sem(f"m_zst{s}") for s in range(2)]
                self.outs = sem("m_outs")
                self.gw = sem("m_gw")
                gP = ["gate", "sel"] + [("a", t) for t in tiles5]
                self.gP = Steps(sem("m_gP"), ["gate", "sel", "a"])
                self.gS = Steps(sem("m_gS"), ["pre", "abs", "exp", "ln", "E", "W", "a"])
                self.gV = Steps(sem("m_gV"), ["f", "i", "lf", "b", "i2", "l2", "lm", "ix", "lx", "m", "M", "a",
                                              "w0", "w1", "w2", "mo0", "mo1", "cpo", "cso"])
                kts = range(KH)
                self.P = Steps(sem("m_P"), base=1, names=[(x, k) for k in kts for x in ("q", "k", "v", "tk", "tv")]
                               + ["sc", "rM", "rW"]
                               + [x for t in range(NP) for x in ([("num", t), ("den", t)]
                                  + [("upd", t, k) for k in kts] + [("nu", t)])]
                               + [x for b in range(NB) for x in ([("int", b)] + [("su", b, k) for k in kts])]
                               + [("num", NP), ("den", NP), ("nu", NP), "rE", "sum", "var"])
                self.V = Steps(sem("m_V"), base=1, names=["sel"]
                               + [x for k in kts for x in (("bq", k), ("bk", k), ("bv", k), ("v", k), ("tv", k))]
                               + [("ex", t) for t in tiles5] + ["wl0", "wl1", "att", "dec0", "dec1"]
                               + [("qh", k) for k in kts]
                               + [x for t in range(NP) for x in (([("qn", t)] if t else []) + [("kw", t)]
                                  + [("C", t, k) for k in kts] + [("n", t)])]
                               + [("kw", NP)]
                               + [x for b in range(NB) for x in ([("vm", b)] + [("Cs", b, k) for k in kts])]
                               + [("qn", NP), "nd", ("n", NP), "dmax", "rden"] + [("hd", k) for k in kts]
                               + [("xc", k) for k in kts]
                               + [x for k in kts for x in (("ln", k), ("sk", k), ("z", k), ("lo", k))])
                self.S = Steps(sem("m_S"), base=1, names=[(x, k) for k in kts for x in ("q", "k", "tk")] + ["w"]
                               + [("num", t) for t in tiles5] + ["dn"] + [("sqr", k) for k in kts] + ["lnv", "rs"]
                               + [("hi", k) for k in kts])
                self.cin = [sem(f"m_cin{s}") for s in range(2)]
                self.cst = [sem(f"m_cst{s}") for s in range(2)]
                self.zin = sem("m_zin")
                self.cpst = sem("m_cpst")
                self.cp_free = sem("m_cp_free")
                self.lo = sem("m_lo")

            def evac_x(self, a, i, s):
                g = G_UP1 + s
                a.wait_ge(pe_unit, U_UP1 + 2 * i + s + 1)
                dst = xp[:, bass.ds(2 * i + s, 1), :].rearrange("p a c -> p (a c)")
                a.activation(dst[:, NCONV - 1:NCONV - 1 + SEQ], pD[g % 2][:, 0:SEQ], ACT.Copy)
                a.activation(streams(dst, NCONV - 1, TS), pD[g % 2][:, SEQ:T].rearrange("p (b c) -> p b c", c=TS),
                             ACT.Copy).then_inc(evac[g % 2], 1)

            def silu_x(self, a, ft, s):
                a.wait_ge(self.conv, 4 * ft + 4)
                a.activation(xc[:, bass.ds(ft, 1), :].rearrange("p a c -> p (a c)"), cv[s][:], ACT.Silu)\
                    .then_inc(self.xc, 1)

            def conv_tile(self, v, ft, s, later):
                g = G_UP1 + s
                if later:
                    v.wait_ge(self.xc, ft - 1)
                v.wait_ge(evac[g % 2], g // 2 + (ft - s) // 2 + 1 if isinstance(ft, int) else g // 2 + self.i + 1)
                src = xp[:, bass.ds(ft, 1), :].rearrange("p a c -> p (a c)")
                out = (cv[s][:, 0:SEQ], cv[s][:, SEQ:T].rearrange("p (b c) -> p b c", c=TS))
                for tap in range(NCONV):
                    w = par[:, bass.ds(PAR["convw"] + CI * tap + ft, 1)]
                    part = (src[:, tap:tap + SEQ], streams(src, tap, TS))
                    if tap:
                        v.wait_ge(self.conv, 4 * ft + tap)
                    for n in range(2):
                        if tap == 0:
                            ins = v.tensor_scalar(out[n], part[n], w, par[:, bass.ds(PAR["convb"] + ft, 1)],
                                                  ALU.mult, ALU.add)
                        else:
                            ins = v.scalar_tensor_tensor(out[n], part[n], w, out[n], ALU.mult, ALU.add)
                    ins.then_inc(self.conv, 1)

            def act(self, a):
                a.wait_ge(a_out, 32 * H)
                a.dma_start(cst[:], io["conv"]).then_inc(self.w_in, 16)
                a.dma_start(wqkv[:], io["wqkv"]).then_inc(self.w_in, 16)
                a.dma_start(wgx[:], io["wgx"]).then_inc(self.w_in, 16)
                a.dma_start(gsm[:], io["gsm"]).then_inc(self.w_in, 16)
                a.dma_start(nS[:], io["st_n"]).then_inc(self.w_in, 16)
                for s in range(2):
                    self.evac_x(a, 0, s)
                    if s:
                        self.silu_x(a, 0, 0)
                with a.Fori(1, CI // 2) as i:
                    for s in range(2):
                        self.evac_x(a, i, s)
                        self.silu_x(a, 2 * i + s - 1, (s + 1) % 2)
                self.silu_x(a, CI - 1, 1)

                def gate_tile(i, s):
                    g = G_UP1 + CI + s
                    a.wait_ge(pe_unit, U_UP1 + CI + 2 * i + s + 1)
                    if not isinstance(i, int):
                        a.wait_ge(self.zst[s], 16 * i)
                    a.activation(two(zb[s][:]), psd[g % 2][:, :, 0:HT], ACT.Silu).then_inc(evac[g % 2], 1)
                    a.wait_ge(evac[g % 2], g // 2 + i + 1)
                    a.dma_start(io["z_kept"][bass.ds(2 * i + s, 1)].rearrange("a p c -> p (a c)"), zb[s][:])\
                        .then_inc(self.zst[s], 16)
                for s in range(2):
                    gate_tile(0, s)
                with a.Fori(1, CI // 2) as i:
                    for s in range(2):
                        gate_tile(i, s)
                P_, V_, S_ = self.gP, self.gV, self.gS
                a.wait_ge(P_.sem, P_.at("gate"))
                a.activation(pre[:], pM[0][0:8, 0:T], ACT.Copy).then_inc(S_.sem, 1)
                a.wait_ge(V_.sem, V_.at("f"))
                a.activation(t1[:], fgr[:], ACT.Abs).then_inc(S_.sem, 1)
                a.wait_ge(S_.sem, S_.at("abs"))
                a.activation(t1[:], t1[:], ACT.Exp, scale=-1.0).then_inc(S_.sem, 1)
                a.wait_ge(S_.sem, S_.at("exp"))
                a.activation(t1[:], t1[:], ACT.Ln, bias=con[0:H, CON["ones"]:CON["ones"] + 1]).then_inc(S_.sem, 1)
                a.wait_ge(V_.sem, V_.at("m"))
                a.activation(rowE[:], mro[:], ACT.Exp, scale=-1.0).then_inc(S_.sem, 1)
                a.wait_ge(V_.sem, V_.at("w2"))
                a.activation(rowW[:], rowW[:], ACT.Exp).then_inc(S_.sem, 1)
                a.wait_ge(P_.sem, P_.at("a"))
                a.activation(acol[:].rearrange("p t h -> p (t h)"), bank[1][:, 0:(NP + 1) * H], ACT.Copy)\
                    .then_inc(S_.sem, 1)
                a.wait_ge(V_.sem, V_.at("cso"))
                for dst, src in (("conv_p", cpo), ("conv_s", cst), ("m_out", mo)):
                    a.dma_start(io[dst], src[:]).then_inc(self.outs, 16)
                a.wait_ge(self.outs, 48)
                for s in range(2):
                    a.wait_ge(self.zst[s], 16 * CI // 2)
                a.sem_inc(self.S.sem, 1)
                with a.Fori(0, H) as h:
                    self.act_head(a, h)
                a.dma_start(io["n_s"], nS[:]).then_inc(self.outs, 16)
                a.dma_start(io["n_p"], nP[:]).then_inc(self.outs, 16)
                a.wait_ge(self.outs, 80)

            def fold(self, v):
                n = [0]

                def link(ins):
                    n[0] += 1
                    ins.then_inc(self.gw, 1)
                    v.wait_ge(self.gw, n[0])
                link(v.tensor_scalar(wqkv[:, 1, :, :], wqkv[:, 1, :, :], float(DH) ** -0.5, None, ALU.mult))
                for dst, xs in ((gC, (0, 1)), (gX, (2,))):
                    for x in xs:
                        for o in range(4):
                            w = wqkv[:, x, :, o:o + 1].broadcast_to([P, CI, 8])
                            first = x == xs[0] and o == 0
                            link(v.tensor_tensor((dst if first else gt)[:], wgx[:, x, :, o, :], w, ALU.mult))
                            if not first:
                                link(v.tensor_tensor(dst[:], dst[:], gt[:], ALU.add))
                self.n_fold = n[0]

            def vec(self, v):
                v.wait_ge(self.w_in, 80)
                v.wait_ge(pe_unit, U_UP1)
                v.memset(xp[:, :, 0:NCONV - 1], 0.0)
                v.tensor_copy(xp[:, :, NCONV - 1 + SEQ:XW].rearrange("p f (b c) -> p f b c", c=XS)[:, :, :, 0:NCONV - 1],
                              cst[:]).then_inc(self.pad, 1)
                v.wait_ge(self.pad, 1)
                for s in range(2):
                    self.conv_tile(v, s, s, False)
                with v.Fori(1, CI // 2) as i:
                    self.i = i
                    for s in range(2):
                        self.conv_tile(v, 2 * i + s, s, True)
                self.fold(v)
                P_, V_, S_ = self.gP, self.gV, self.gS
                st = lambda r: r[:, SEQ:T].rearrange("p (b c) -> p b c", c=TS)
                first = lambda r: st(r)[:, :, 0:1]
                m0 = gsm[:, 2:2 + NB].unsqueeze(2)
                v.wait_ge(kept, 16)
                v.wait_ge(P_.sem, P_.at("sel"))
                v.tensor_scalar(fgr[:], pM[0][0:H, 0:T], gsm[:, 1:2], None, ALU.add).then_inc(V_.sem, 1)
                v.tensor_scalar(igr[:], pM[1][0:H, 0:T], gsm[:, 0:1], None, ALU.add).then_inc(V_.sem, 1)
                v.wait_ge(S_.sem, S_.at("ln"))
                v.scalar_tensor_tensor(fgr[:], fgr[:], 0.0, t1[:], ALU.min, ALU.subtract).then_inc(V_.sem, 1)
                v.wait_ge(V_.sem, V_.at("lf"))
                v.tensor_tensor_scan(bro[:], reset[0:H, :], fgr[:], 0.0, ALU.mult, ALU.add).then_inc(V_.sem, 1)
                v.tensor_copy(i2[:], igr[:]).then_inc(V_.sem, 1)
                v.tensor_copy(l2[:], fgr[:]).then_inc(V_.sem, 1)
                v.tensor_tensor(mo[:, 0:NB].unsqueeze(2), first(fgr), m0, ALU.add).then_inc(V_.sem, 1)
                v.wait_ge(V_.sem, V_.at("lm"))
                v.tensor_tensor(first(i2), first(i2), mo[:, 0:NB].unsqueeze(2), ALU.max).then_inc(V_.sem, 1)
                v.memset(first(l2), NEVER).then_inc(V_.sem, 1)
                v.wait_ge(V_.sem, V_.at("lx"))
                v.tensor_tensor_scan(mro[:], l2[:], i2[:], 0.0, ALU.add, ALU.max).then_inc(V_.sem, 1)
                v.wait_ge(V_.sem, V_.at("m"))
                v.tensor_tensor(rowM[:], bro[:], mro[:], ALU.subtract).then_inc(V_.sem, 1)
                v.tensor_tensor(igr[:], igr[:], bro[:], ALU.subtract).then_inc(V_.sem, 1)
                v.wait_ge(V_.sem, V_.at("M"))
                ch = lambda r, t0, n: r[:, t0 * P:(t0 + n) * P].rearrange("p (t c) -> p t c", c=P)
                v.tensor_copy(rowW[:, 0:P], rowM[:, 0:P]).then_inc(V_.sem, 1)
                v.tensor_tensor(ch(rowW, 1, NP - 1), ch(rowM, 1, NP - 1),
                                ch(mro, 0, NP - 1)[:, :, P - 1:P].broadcast_to([H, NP - 1, P]), ALU.add)\
                    .then_inc(V_.sem, 1)
                v.tensor_tensor(st(rowW), st(rowM), m0.broadcast_to([H, NB, TS]), ALU.add).then_inc(V_.sem, 1)
                v.tensor_copy(mo[:, 0:1], mro[:, SEQ - 1:SEQ]).then_inc(V_.sem, 1)
                v.tensor_copy(mo[:, 1:1 + NB].unsqueeze(2), st(mro)[:, :, TS - 1:TS]).then_inc(V_.sem, 1)
                v.tensor_copy(cpo[:], xp[:, :, SEQ:SEQ + NCONV - 1]).then_inc(V_.sem, 1)
                v.tensor_copy(cst[:], xp[:, :, NCONV - 1 + SEQ:XW].rearrange("p f (b c) -> p f b c", c=XS)
                              [:, :, :, TS:XS]).then_inc(V_.sem, 1)
                v.wait_ge(self.outs, 48)
                for s in range(2):
                    v.wait_ge(self.zst[s], 16 * CI // 2)
                v.sem_inc(self.V.sem, 1)
                with v.Fori(0, H) as h:
                    self.vec_head(v, h)

            def pe(self, pe):
                for j in range(2):
                    pe_dense(pe, (U_UP1 + j, 0), (G_UP1 + j, 0), xh, xl, ready=(norm2.lo_done, 1) if j == 0 else None,
                             cut=SEQ)
                with pe.Fori(1, CI // 2) as i:
                    for j in range(2):
                        pe_dense(pe, (U_UP1 + j, i), (G_UP1 + j, i), xh, xl, cut=SEQ)
                with pe.Fori(CI // 2, CI) as i:
                    for j in range(2):
                        pe_dense(pe, (U_UP1 + j, i), (G_UP1 + j, i), xh, xl)
                P_, V_, S_ = self.gP, self.gV, self.gS
                pe.wait_ge(self.gw, 23)
                pe.wait_ge(self.xc, CI)
                for part in range(2):
                    for ft in range(CI):
                        xs = (xp[:, ft, NCONV - 1:NCONV - 1 + SEQ], streams(xp[:, ft, :], NCONV - 1, TS))
                        cs = (xc[:, ft, 0:SEQ], xc[:, ft, SEQ:T])
                        for w, src in ((gC, cs), (gX, xs)):
                            o = pM[0][0:8, 0:SEQ] if part == 0 else pM[0][0:8, SEQ:T]
                            mm = pe.matmul(o, w[:, ft, :], src[part], start=(ft == 0 and w is gC),
                                           stop=(ft == CI - 1 and w is gX))
                mm.then_inc(P_.sem, 1)
                pe.wait_ge(S_.sem, S_.at("pre"))
                for row, o in ((4, pM[0]), (0, pM[1])):
                    for c0, c1 in ((0, SEQ), (SEQ, T)):
                        mm = pe.matmul(o[0:H, c0:c1], con[0:8, CON["ident"] + row:CON["ident"] + row + 4],
                                       pre[:, c0:c1], start=True, stop=True)
                mm.then_inc(P_.sem, 1)
                pe.wait_ge(V_.sem, V_.at("a"))
                for t in tiles5:
                    mm = pe.transpose(bank[1][:, t * H:(t + 1) * H], igr[:, tt(t)], ident[0:H, 0:H])
                mm.then_inc(P_.sem, 1)
                pe.sem_inc(self.P.sem, 1)
                with pe.Fori(0, H) as h:
                    self.pe_head(pe, h)

            def pe_head(self, pe, h):
                P_, V_, S_ = self.P, self.V, self.S
                cuts = ((0, SEQ), (SEQ, T))
                pe.wait_ge(V_.sem, V_.rounds(h))
                pe.wait_ge(S_.sem, S_.rounds(h))
                pe.wait_ge(self.gS.sem, self.gS.n)
                n = 0
                for k in range(KH):
                    x = xp[:, bass.ds(KH * h + k, 1), :].rearrange("p a c -> p (a c)")
                    c = xc[:, bass.ds(KH * h + k, 1), :].rearrange("p a c -> p (a c)")
                    srcs = {"q": (c[:, 0:SEQ], c[:, SEQ:T]), "k": (c[:, 0:SEQ], c[:, SEQ:T]),
                            "v": (x[:, NCONV - 1:NCONV - 1 + SEQ], streams(x, NCONV - 1, TS))}
                    for j, name in enumerate("qkv"):
                        pe.wait_ge(V_.sem, V_.at(("b" + name, k), h))
                        if n >= 2:
                            before, kb = "qkv"[(n - 2) % 3], (n - 2) // 3
                            who = V_ if before == "v" else S_
                            pe.wait_ge(who.sem, who.at((before, kb), h))
                        for (c0, c1), src in zip(cuts, srcs[name]):
                            mm = pe.matmul(pD[n % 2][:, c0:c1], blk[k % 2][:, j, :], src, start=True, stop=True)
                        mm.then_inc(P_.sem, 1)
                        n += 1
                    pe.wait_ge(S_.sem, S_.at(("k", k), h))
                    for t in tiles5:
                        mm = pe.transpose(pM[0][:, tt(t)], kT[:, k, tt(t)], ident)
                    mm.then_inc(P_.sem, 1)
                    pe.wait_ge(V_.sem, V_.at(("v", k), h))
                    for t in tiles5:
                        mm = pe.transpose(pM[1][:, tt(t)], vtmp[k % 2][:, tt(t)], ident)
                    mm.then_inc(P_.sem, 1)
                pe.wait_ge(S_.sem, S_.at(("tk", KH - 1), h))
                for t in tiles5:
                    for k in range(KH):
                        mm = pe.matmul(pD[0][:, tt(t)], kT[:, k, tt(t)], qT[:, k, tt(t)], start=(k == 0),
                                       stop=(k == KH - 1))
                mm.then_inc(P_.sem, 1)
                for row, o in ((rowM, pD[1]), (rowW, pM[0])):
                    for c0, c1 in cuts:
                        mm = pe.matmul(o[:, c0:c1], selh[:], row[:, c0:c1], start=True, stop=True)
                    mm.then_inc(P_.sem, 1)
                pe.wait_ge(V_.sem, V_.at(("qh", KH - 1), h))
                for t in range(NP):
                    if t:
                        pe.wait_ge(V_.sem, V_.at(("C", t - 1, KH - 1), h))
                    if t >= 2:
                        pe.wait_ge(S_.sem, S_.at(("num", t - 2), h))
                    for f in range(KH):
                        o = bank[t % 2][:, tt(f)]
                        mm = pe.matmul(o, vtok[:, t, tt(f)], att1[:, tt(t)], start=True, stop=(t == 0))
                        for k in range(KH if t else 0):
                            mm = pe.matmul(o, Cp[:, k, tt(f)], qT[:, k, tt(t)], start=False, stop=(k == KH - 1))
                    mm.then_inc(P_.sem, 1)
                    mm = pe.matmul(pD[1][:, tt(t)], ones, att1[:, tt(t)], start=True, stop=(t == 0))
                    if t:
                        pe.wait_ge(V_.sem, V_.at(("qn", t), h))
                        for k in range(KH):
                            mm = pe.matmul(pD[1][:, tt(t)], ones, vm[0][:, tt(k)], start=False, stop=(k == KH - 1))
                    mm.then_inc(P_.sem, 1)
                    pe.wait_ge(V_.sem, V_.at(("kw", t), h))
                    for k in range(KH):
                        if t:
                            pe.wait_ge(V_.sem, V_.at(("C", t - 1, k), h))
                        pe.matmul(U[k], kw[:, tt(k)], vtok[:, t, :], start=True, stop=True).then_inc(P_.sem, 1)
                    if t:
                        pe.wait_ge(V_.sem, V_.at(("n", t - 1), h))
                    for k in range(KH):
                        mm = pe.matmul(pD[1][:, T + 64 + k:T + 65 + k], kw[:, tt(k)], ones[:, 0:1], start=True,
                                       stop=True)
                    mm.then_inc(P_.sem, 1)
                pe.wait_ge(S_.sem, S_.at(("num", NP - 2), h))
                for b in range(NB):
                    c = SEQ + b * TS
                    pe.wait_ge(self.cin[b % 2], 16 * (4 * h + b // 2 + 1))
                    for f in range(KH):
                        for k in range(KH):
                            o = f * P + b * TS
                            mm = pe.matmul(bank[0][:, o:o + TS], Cs[b % 2][:, k, tt(f)], qT[:, k, c:c + TS],
                                           start=(b == 0 and f == 0 and k == 0), stop=False, skip_group_check=True)
                    mm.then_inc(P_.sem, 1)
                    pe.wait_ge(V_.sem, V_.at(("vm", b), h))
                    for k in range(KH):
                        last = ("Cs", b - 1, k) if b else ("C", NP - 1, k)
                        pe.wait_ge(V_.sem, V_.at(last, h))
                        pe.matmul(U[k], kw[:, tt(k)], vm[b % 2][:], start=True, stop=True).then_inc(P_.sem, 1)
                for f in range(KH):
                    mm = pe.matmul(bank[0][:, tt(f)], vtok[:, NP, tt(f)], att1[:, tt(NP)], start=False, stop=True,
                                   skip_group_check=True)
                mm.then_inc(P_.sem, 1)
                pe.wait_ge(V_.sem, V_.at("nd", h))
                pe.matmul(pD[1][:, tt(NP)], ones, att1[:, tt(NP)], start=True, stop=False)
                for k in range(KH):
                    mm = pe.matmul(pD[1][:, tt(NP)], ones, vm[0][:, tt(k)], start=False, stop=(k == KH - 1))
                mm.then_inc(P_.sem, 1)
                pe.wait_ge(V_.sem, V_.at(("Cs", NB - 1, KH - 1), h))
                for k in range(KH):
                    mm = pe.matmul(bank[3][:, k * NB:(k + 1) * NB], kw[:, tt(k)],
                                   con[:, CON["ind"]:CON["ind"] + NB], start=True, stop=True)
                mm.then_inc(P_.sem, 1)
                for c0, c1 in cuts:
                    mm = pe.matmul(pD[0][:, c0:c1], selh[:], rowE[:, c0:c1], start=True, stop=True)
                mm.then_inc(P_.sem, 1)
                pe.wait_ge(S_.sem, S_.at("dn", h))
                for k in range(KH):
                    pe.wait_ge(V_.sem, V_.at(("hd", k), h))
                    for c0, c1 in cuts:
                        mm = pe.matmul(pM[0][:, c0:c1], ones, qT[:, k, c0:c1], start=(k == 0), stop=(k == KH - 1))
                mm.then_inc(P_.sem, 1)
                for k in range(KH):
                    pe.wait_ge(S_.sem, S_.at(("sqr", k), h))
                    for c0, c1 in cuts:
                        mm = pe.matmul(pM[1][:, c0:c1], ones, sq4[k][:, c0:c1], start=(k == 0), stop=(k == KH - 1))
                mm.then_inc(P_.sem, 1)

            def vec_head(self, v, h):
                P_, V_, S_ = self.P, self.V, self.S
                v.wait_ge(P_.sem, P_.rounds(h))
                v.wait_ge(S_.sem, S_.rounds(h))
                one = lambda x, i: x[:, bass.ds(i, 1), :].rearrange("p a c -> p (a c)")
                v.tensor_copy(selh[:], con[0:H, bass.ds(CON["sel"] + P * h, P)]).then_inc(V_.sem, 1)

                def blocks(k):
                    if k >= 2:
                        v.wait_ge(P_.sem, P_.at(("v", k - 2), h))
                    for j in range(3):
                        w = wqkv[:, j, bass.ds(KH * h + k, 1), :]
                        v.tensor_tensor(blk[k % 2][:, j, :].rearrange("p (b o) -> p b o", o=4),
                                        con[:, CON["bd"]:CON["bd"] + P].rearrange("p (b o) -> p b o", o=4),
                                        w.broadcast_to([P, P // 4, 4]), ALU.mult).then_inc(V_.sem, 1)
                for k in range(KH):
                    blocks(k)
                    v.wait_ge(P_.sem, P_.at(("v", k), h))
                    if k >= 2:
                        v.wait_ge(P_.sem, P_.at(("tv", k - 2), h))
                    v.tensor_copy(vtmp[k % 2][:], pD[(3 * k + 2) % 2][:, 0:T]).then_inc(V_.sem, 1)
                    v.wait_ge(P_.sem, P_.at(("tv", k), h))
                    v.tensor_copy(vtok[:, :, tt(k)], pM[1][:, 0:T].rearrange("p (t c) -> p t c", c=P))\
                        .then_inc(V_.sem, 1)
                v.wait_ge(P_.sem, P_.at("rM", h))
                for t in tiles5:
                    see = con[:, CON["caus"] + (P if t == NP else 0):][:, 0:P]
                    v.scalar_tensor_tensor(att1[:, tt(t)], pD[1][:, tt(t)],
                                           acol[:, t, bass.ds(h, 1)], see, ALU.add, ALU.min).then_inc(V_.sem, 1)
                v.wait_ge(S_.sem, S_.at("w", h))
                v.tensor_copy(wl[:, 0:NP].unsqueeze(2), seqs(att1, 0, NP, P)[:, :, P - 1:P]).then_inc(V_.sem, 1)
                v.tensor_reduce(wl[:, NP:NP + 1], seqs(att1, SEQ, NB, TS)[:, :, TS - 1], mybir.AxisListType.X, ALU.add)\
                    .then_inc(V_.sem, 1)
                v.wait_ge(V_.sem, V_.at("wl1", h))
                v.tensor_tensor(att1[:], att1[:], pD[0][:, 0:T], ALU.mult).then_inc(V_.sem, 1)
                v.wait_ge(P_.sem, P_.at("rW", h))
                v.tensor_copy(dec[:, 0:NP].unsqueeze(2),
                              pM[0][:, 0:SEQ].rearrange("p (t c) -> p t c", c=P)[:, :, P - 1:P]).then_inc(V_.sem, 1)
                v.tensor_copy(dec[:, NP:NP + NB].unsqueeze(2),
                              pM[0][:, SEQ:T].rearrange("p (t c) -> p t c", c=TS)[:, :, TS - 1:TS]).then_inc(V_.sem, 1)
                for k in range(KH):
                    v.tensor_tensor(qT[:, k, :], qT[:, k, :], pM[0][:, 0:T], ALU.mult).then_inc(V_.sem, 1)
                v.wait_ge(V_.sem, V_.at(("qh", KH - 1), h))
                nh = one(nP, h)
                vmv = lambda x: x[:].rearrange("p (k c) -> p k c", c=P)
                for t in range(NP):
                    if t:
                        v.wait_ge(V_.sem, V_.at(("n", t - 1), h))
                        v.wait_ge(P_.sem, P_.at(("den", t - 1), h))
                        v.tensor_tensor(vmv(vm[0]), qT[:, :, tt(t)], nh.unsqueeze(2).broadcast_to([P, KH, P]),
                                        ALU.mult).then_inc(V_.sem, 1)
                        v.wait_ge(P_.sem, P_.at(("nu", t - 1), h))
                    v.tensor_scalar(kw[:], ktok[:, t, :], wl[:, t:t + 1], None, ALU.mult).then_inc(V_.sem, 1)
                    if t == 0:
                        v.wait_ge(self.cp_free, h + 1)
                    for k in range(KH):
                        v.wait_ge(P_.sem, P_.at(("upd", t, k), h))
                        if t == 0:
                            v.tensor_copy(Cp[:, k, :], U[k]).then_inc(V_.sem, 1)
                        else:
                            v.scalar_tensor_tensor(Cp[:, k, :], Cp[:, k, :], dec[:, t:t + 1], U[k], ALU.mult,
                                                   ALU.add).then_inc(V_.sem, 1)
                    v.wait_ge(P_.sem, P_.at(("nu", t), h))
                    nu = pD[1][:, T + 64:T + 64 + KH]
                    if t == 0:
                        v.tensor_copy(nh, nu).then_inc(V_.sem, 1)
                    else:
                        v.scalar_tensor_tensor(nh, nh, dec[:, t:t + 1], nu, ALU.mult, ALU.add).then_inc(V_.sem, 1)
                v.tensor_scalar(kw[:], ktok[:, NP, :], wl[:, NP:NP + 1], None, ALU.mult).then_inc(V_.sem, 1)
                for b in range(NB):
                    if b >= 2:
                        v.wait_ge(P_.sem, P_.at(("su", b - 2, KH - 1), h))
                    v.tensor_scalar(vm[b % 2][:], vtok[:, NP, :], con[:, CON["ind"] + b:CON["ind"] + b + 1], None,
                                    ALU.mult).then_inc(V_.sem, 1)
                    for k in range(KH):
                        v.wait_ge(P_.sem, P_.at(("su", b, k), h))
                        C = Cs[b % 2][:, k, :]
                        v.scalar_tensor_tensor(C, C, dec[:, NP + b:NP + b + 1], U[k], ALU.mult, ALU.add)\
                            .then_inc(V_.sem, 1)
                ns = nS[:, bass.ds(h, 1), :, :].rearrange("p a k b -> p (a k) b")
                v.tensor_tensor(vmv(vm[0]).rearrange("p k (b c) -> p k b c", c=TS),
                                qT[:, :, SEQ:T].rearrange("p k (b c) -> p k b c", c=TS),
                                ns.unsqueeze(3).broadcast_to([P, KH, NB, TS]), ALU.mult).then_inc(V_.sem, 1)
                v.wait_ge(V_.sem, V_.at(("qn", NP), h))
                v.tensor_tensor(ns, ns, dec[:, NP:NP + NB].unsqueeze(1).broadcast_to([P, KH, NB]), ALU.mult)\
                    .then_inc(V_.sem, 1)
                v.wait_ge(P_.sem, P_.at(("nu", NP), h))
                v.wait_ge(V_.sem, V_.at("nd", h))
                v.tensor_tensor(ns, ns, bank[3][:, 0:KH * NB].rearrange("p (k b) -> p k b", b=NB), ALU.add)\
                    .then_inc(V_.sem, 1)
                v.wait_ge(S_.sem, S_.at("dn", h))
                v.wait_ge(P_.sem, P_.at("rE", h))
                v.tensor_tensor(att1[:], att1[:], pD[0][:, 0:T], ALU.max).then_inc(V_.sem, 1)
                v.wait_ge(V_.sem, V_.at("dmax", h))
                v.reciprocal(att1[:], att1[:]).then_inc(V_.sem, 1)
                v.wait_ge(V_.sem, V_.at("rden", h))
                for k in range(KH):
                    v.tensor_tensor(qT[:, k, :], qT[:, k, :], att1[:], ALU.mult).then_inc(V_.sem, 1)
                v.wait_ge(P_.sem, P_.at("sum", h))
                for k in range(KH):
                    v.scalar_tensor_tensor(qT[:, k, :], pM[0][:, 0:T], -1.0 / DH, qT[:, k, :], ALU.mult, ALU.add)\
                        .then_inc(V_.sem, 1)
                v.wait_ge(S_.sem, S_.at("rs", h))
                v.wait_ge(self.zin, 16 * (h + 1))
                for k in range(KH):
                    hk = qT[:, k, :]
                    v.scalar_tensor_tensor(hk, hk, par[:, PAR["mnorm"] + k:PAR["mnorm"] + k + 1], rs[:], ALU.mult,
                                           ALU.mult).then_inc(V_.sem, 1)
                    v.wait_ge(V_.sem, V_.at(("ln", k), h))
                    v.scalar_tensor_tensor(hk, one(xc, KH * h + k), par[:, bass.ds(PAR["skip"] + KH * h + k, 1)], hk,
                                           ALU.mult, ALU.add).then_inc(V_.sem, 1)
                    v.wait_ge(V_.sem, V_.at(("sk", k), h))
                    v.tensor_tensor(hk, hk, zt[:, k, :], ALU.mult).then_inc(V_.sem, 1)
                    v.wait_ge(S_.sem, S_.at(("hi", k), h))
                    v.tensor_tensor(one(al, KH * h + k), hk, one(ah, KH * h + k).bitcast(F32), ALU.subtract)\
                        .then_inc(V_.sem, 1)

            def act_head(self, a, h):
                P_, V_, S_ = self.P, self.V, self.S
                a.wait_ge(V_.sem, V_.rounds(h))
                a.wait_ge(P_.sem, P_.rounds(h))
                for k in range(KH):
                    for j, (name, dst) in enumerate((("q", qT), ("k", kT))):
                        a.wait_ge(P_.sem, P_.at((name, k), h))
                        a.activation(dst[:, k, :], pD[(3 * k + j) % 2][:, 0:T], ACT.Copy).then_inc(S_.sem, 1)
                    a.wait_ge(P_.sem, P_.at(("tk", k), h))
                    a.activation(ktok[:, :, tt(k)], pM[0][:, 0:T].rearrange("p (t c) -> p t c", c=P), ACT.Copy)\
                        .then_inc(S_.sem, 1)
                a.wait_ge(V_.sem, V_.at(("ex", NP), h))
                a.activation(att1[:], att1[:], ACT.Exp).then_inc(S_.sem, 1)
                for t in tiles5:
                    a.wait_ge(P_.sem, P_.at(("num", t), h))
                    a.wait_ge(P_.sem, P_.at(("den", t), h))
                    a.activation(qT[:, :, tt(t)], bank[t % 2].rearrange("p (k c) -> p k c", c=P), ACT.Copy)\
                        .then_inc(S_.sem, 1)
                a.activation(att1[:], pD[1][:, 0:T], ACT.Abs).then_inc(S_.sem, 1)
                for k in range(KH):
                    a.wait_ge(V_.sem, V_.at(("xc", k), h))
                    a.activation(sq4[k][:], qT[:, k, :], ACT.Square).then_inc(S_.sem, 1)
                a.wait_ge(P_.sem, P_.at("var", h))
                a.activation(rs[:], pM[1][:, 0:T], ACT.Ln, bias=eps, scale=1.0 / DH).then_inc(S_.sem, 1)
                a.wait_ge(S_.sem, S_.at("lnv", h))
                a.activation(rs[:], rs[:], ACT.Exp, scale=-0.5).then_inc(S_.sem, 1)
                for k in range(KH):
                    a.wait_ge(V_.sem, V_.at(("z", k), h))
                    a.activation(ah[:, bass.ds(KH * h + k, 1), :].rearrange("p a c -> p (a c)"), qT[:, k, :],
                                 ACT.Copy).then_inc(S_.sem, 1)

            def sp(self, sp):
                P_, V_, S_ = self.P, self.V, self.S
                sp.wait_ge(self.gS.sem, self.gS.n)
                sp.wait_ge(self.gV.sem, self.gV.n)
                sp.sem_inc(self.cp_free, 1)

                def head(h, later):
                    def store(b):
                        sp.wait_ge(V_.sem, V_.at(("Cs", b, KH - 1), h))
                        sp.dma_start(io["c_s"][bass.ds(h * NB + b, 1)].rearrange("a p k c -> p (a k) c"), Cs[b % 2][:])\
                            .then_inc(self.cst[b % 2], 16)
                    for b in range(NB):
                        if later or b >= 2:
                            sp.wait_ge(self.cst[b % 2], 16 * (4 * h + b // 2))
                        sp.dma_start(Cs[b % 2][:], io["st_c"][bass.ds(h * NB + b, 1)].rearrange("a p k c -> p (a k) c"))\
                            .then_inc(self.cin[b % 2], 16)
                        if b == 1:
                            sp.wait_ge(V_.sem, V_.at(("kw", NP), h))
                            sp.dma_start(zt[:], io["z_kept"][bass.ds(KH * h, KH)].rearrange("k p c -> p k c"))\
                                .then_inc(self.zin, 16)
                            sp.wait_ge(P_.sem, P_.at(("int", 0), h))
                            sp.dma_start(io["c_p"][bass.ds(h, 1)].rearrange("a p k c -> p (a k) c"), Cp[:])\
                                .then_inc(self.cpst, 16)
                        if b:
                            store(b - 1)
                    store(NB - 1)
                    sp.wait_ge(self.cpst, 16 * (h + 1))
                    sp.sem_inc(self.cp_free, 1)
                head(0, False)
                with sp.Fori(1, H) as h:
                    head(h, True)
                for s in range(2):
                    sp.wait_ge(self.cst[s], 16 * 16)
                sp.wait_ge(self.zin, 16 * H)
                sp.wait_ge(V_.sem, V_.rounds(H))
                sp.dma_start(xT[:], io["x_kept"]).then_inc(kept, 16)

        sq4 = [vtmp[0], vtmp[1], kT[:, 0, :], kT[:, 1, :]]
        mlstm = MLstm()
        def vec_residual(v, units, g0):
            with v.Fori(0, KD // 2) as i:
                for s in range(2):
                    v.wait_ge(pe_unit, units[0] + units[1] * (2 * i + s + 1))
                    x = xT[:, bass.ds(2 * i + s, 1), :].rearrange("p a (c d) -> p (a c) d", c=2)
                    v.tensor_tensor(x, x, psd[(g0 + s) % 2][:, :, 0:HT], ALU.add).then_inc(evac[(g0 + s) % 2], 1)

        def pe_down(pe, u0, g0, nu, nk, ready, ready_at):
            for j in range(2):
                for q in range(nu):
                    pe_dense(pe, (u0 + nu * j + q, 0), (g0 + j, 0), ah, al, k0=q * KD, nk=nk, first=q == 0,
                             last=q == nu - 1, ready=(ready, ready_at + q * KD) if j == 0 and ready is not None else None)
            with pe.Fori(1, KD // 2) as i:
                for j in range(2):
                    for q in range(nu):
                        pe_dense(pe, (u0 + nu * j + q, nu * i), (g0 + j, i), ah, al, k0=q * KD, nk=nk, first=q == 0,
                                 last=q == nu - 1)

        class FeedForward:

            def __init__(self, name, u, g, norm):
                self.hi, self.lo = sem(f"{name}_hi"), sem(f"{name}_lo")
                self.u, self.g, self.norm = u, g, norm

            def parts(self):
                u, g, before = self.u, self.g, 0
                for f in FF_PARTS:
                    nu = -(-f // KD)
                    yield f, before, u, g, nu
                    u, g, before = u + 2 * f + KD * nu, g + 2 * f + KD, before + f

            def act(self, a):
                for f, before, u, g, nu in self.parts():
                    with a.Fori(0, f // 2) as i:
                        for s in range(2):
                            gg = g + 2 * s
                            a.wait_ge(pe_unit, u + 4 * i + 2 * s + 1)
                            a.activation(two(ffs[s][:]), psd[gg % 2][:, :, 0:HT], ACT.Silu).then_inc(evac[gg % 2], 1)
                            a.wait_ge(evac[(gg + 1) % 2], (gg + 1) // 2 + 2 * i + 1)
                            if s == 0:
                                a.wait_ge(pe_unit, u)
                            a.activation(ah[:, bass.ds(2 * i + s, 1), :].rearrange("p a c -> p (a c)"), fft[s][:],
                                         ACT.Copy).then_inc(self.hi, 1)

            def vec(self, v):
                for f, before, u, g, nu in self.parts():
                    with v.Fori(0, f // 2) as i:
                        for s in range(2):
                            gg = g + 2 * s
                            v.wait_ge(evac[gg % 2], gg // 2 + 2 * i + 1)
                            v.wait_ge(pe_unit, u + 4 * i + 2 * s + 2)
                            v.tensor_tensor(two(fft[s][:]), two(ffs[s][:]), psd[(gg + 1) % 2][:, :, 0:HT],
                                            ALU.mult).then_inc(evac[(gg + 1) % 2], 1)
                            v.wait_ge(self.hi, before + 2 * i + s + 1)
                            one = lambda x: x[:, bass.ds(2 * i + s, 1), :].rearrange("p a c -> p (a c)")
                            v.tensor_tensor(one(al), fft[s][:], one(ah).bitcast(F32), ALU.subtract)\
                                .then_inc(self.lo, 1)
                    vec_residual(v, (u + 2 * f, nu), g + 2 * f)

            def pe(self, pe):
                for f, before, u, g, nu in self.parts():
                    for j in range(4):
                        pe_dense(pe, (u + j, 0), (g + j, 0), xh, xl,
                                 ready=(self.norm.lo_done, 1) if before == 0 and j == 0 else None)
                    with pe.Fori(1, f // 2) as i:
                        for j in range(4):
                            pe_dense(pe, (u + j, 2 * i), (g + j, 2 * i), xh, xl)
                    pe_down(pe, u + 2 * f, g + 2 * f, nu, min(f, KD), self.lo, before + 1)

        ffn0 = FeedForward("ff0", U_FF0, G_FF0, norm1)
        ffn1 = FeedForward("ff1", U_FF1, G_FF1, norm3)

        block = ctx.enter_context(nc.Block())

        @block.sync
        def _(sp):
            sp.dma_start(xT[:], io["x"]).then_inc(x_in, 16)
            sp.dma_start(par[:], io["par"]).then_inc(con_in, 16)
            sp.dma_start(con[:], io["con"]).then_inc(con_in, 16)
            sp.dma_start(vmask[:, 0:NL, :], io["masks"]).then_inc(con_in, 16)
            sp.dma_start(cos[:], io["cos"]).then_inc(con_in, 16)
            sp.dma_start(sin[:], io["sin"]).then_inc(con_in, 16)
            for s in range(2):
                sp.dma_start(wraw[s][:], io["w"][s]).then_inc(w_loaded[s], 16)
            def stream(u0, u1):
                with sp.Fori(u0 // 2, u1 // 2) as i:
                    for s in range(2):
                        sp.wait_ge(w_split, 2 * i + s - 1)
                        sp.dma_start(wraw[s][:], io["w"][bass.ds(2 * i + s, 1)].rearrange("a p k c -> p (a k) c"))\
                            .then_inc(w_loaded[s], 16)
            stream(2, U_FF0 + FF_UNITS)
            sp.wait_ge(norm2.lo_done, KD)
            sp.dma_start(io["x_kept"], xT[:]).then_inc(kept, 16)
            stream(U_UP1, U_DN1 + 2)
            mlstm.sp(sp)
            stream(U_DN1 + 2, N_UNITS)
            for k in range(KD):
                sp.wait_ge(normf.v_done, k + 2)
                sp.dma_start(io["yT"][:, k, :], ntmp[k % 2][:]).then_inc(y_stored[k % 2], 16)
            for s in range(2):
                sp.wait_ge(y_stored[s], 16 * KD // 2)

        @block.gpsimd
        def _(pool):
            def split(n, s, i, later):
                pool.wait_ge(w_loaded[s], 16 * i + 16)
                if later:
                    pool.wait_ge(pe_unit, n - 1)
                pool.sem_inc(w_taken, 1)
                pool.tensor_copy(whi[s][:], wraw[s][:]).then_inc(w_high, 1)
                pool.wait_ge(w_high, n + 1)
                pool.tensor_tensor(wlo[s][:], wraw[s][:], whi[s][:].bitcast(F32), ALU.subtract).then_inc(w_split, 1)
            for s in range(2):
                split(s, s, 0, False)
            with pool.Fori(1, N_UNITS // 2) as i:
                for s in range(2):
                    split(2 * i + s, s, i, True)

        @block.scalar
        def _(a):
            def load_head(h):
                if not (isinstance(h, int) and h == 0):
                    a.wait_ge(a_out, 16 * (2 * h))
                    a.wait_ge(b_out, 16 * (2 * h))
                a.dma_start(asmp[:], io["st_hgrn"][bass.ds(h, 1)].rearrange("a p b v -> p (a b) v")).then_inc(a_in, 16)
                a.dma_start(bsmp[:], io["st_ret"][bass.ds(h, 1)].rearrange("a p b v -> p (a b) v")).then_inc(b_in, 16)
                a.dma_start(dret[:], io["dret"][bass.ds(h, 1)].rearrange("a p b v -> p (a b) v")).then_inc(b_in, 16)
                a.dma_start(win[:], io["win"][bass.ds(h, 1)].rearrange("a p b v -> p (a b) v")).then_inc(b_in, 16)

            def store_a(h):
                a.wait_ge(aV.sem, aV.at("Sa1", h))
                a.dma_start(io["hgrn_p"][bass.ds(h, 1)].rearrange("a p v -> p (a v)"), ast[:]).then_inc(a_out, 16)
                a.dma_start(io["hgrn_s"][bass.ds(h, 1)].rearrange("a p b v -> p (a b) v"), asmp[:]).then_inc(a_out, 16)

            def store_b(h):
                a.wait_ge(bV.sem, bV.at("Sa1", h))
                a.dma_start(io["ret_p"][bass.ds(h, 1)].rearrange("a p v -> p (a v)"), bst[:]).then_inc(b_out, 16)
                a.dma_start(io["ret_s"][bass.ds(h, 1)].rearrange("a p b v -> p (a b) v"), bsmp[:]).then_inc(b_out, 16)

            a.wait_ge(con_in, 16 * 5)
            for r in range(2):
                a.wait_ge(lb_done, 2)
                a.activation(lbt[:, 1 + r, :], lbt[:, 1 + r, :], ACT.Exp).then_inc(lb_act, 1)
            norm0.act(a)

            def finish(h):
                a_act_norm(a, h)
                store_a(h)

            def finish_b(h):
                b_act_turns(a, h)

            load_head(0)

            def head(h, prev):
                if prev:
                    a_act_norm(a, h - 1)
                    store_a(h - 1)
                in0_evac(a, h, 0)
                if prev:
                    b_act_turns(a, h - 1)
                in0_evac(a, h, 1)
                in0_evac(a, h, 2)
                if prev:
                    b_act_norm(a, h - 1)
                    store_b(h - 1)
                    load_head(h)
                in0_evac(a, h, 3)
                a_act_gates(a, h)
                a_act_level(a, h, 0)
                a_act_level(a, h, 1)
                in0_evac(a, h, 4)
                a_act_level(a, h, 2)
                a_act_level(a, h, 3)
                in0_evac(a, h, 5)
                a_act_level(a, h, 4)
                a_act_level(a, h, 5)
                in0_evac(a, h, 6)
                a_act_level(a, h, 6)
                a_act_turns(a, h)
                in0_evac(a, h, 7)

            head(0, False)
            with a.Fori(1, H) as h:
                head(h, True)
            a_act_norm(a, H - 1)
            store_a(H - 1)
            b_act_turns(a, H - 1)
            b_act_norm(a, H - 1)
            store_b(H - 1)
            for k in range(8):
                a.wait_ge(aV.sem, aV.at("mixn", H - 1))
                a.wait_ge(bV.sem, bV.at("mixg", H - 1))
                a.wait_ge(pe_unit, U_OUT0)
                a.activation(xh[:, k, :], mix[:, k, :], ACT.Copy).then_inc(mh, 1)
            a.wait_ge(a_out, 32 * H)
            a.wait_ge(b_out, 32 * H)
            norm1.act(a)
            ffn0.act(a)
            norm2.act(a)
            mlstm.act(a)
            norm3.act(a)
            ffn1.act(a)
            normf.act(a)

        @block.vector
        def _(v):
            v.wait_ge(con_in, 16 * 5)
            v.tensor_copy(masks[:], vmask[:, 0:NL, :])
            lg = par[:, PAR["lb"]:PAR["lb"] + 8].rearrange("p (r h) -> p r h", r=2)
            v.tensor_tensor(lbt[:, 0, :], lg[:, 0, :], lg[:, 1, :], ALU.max).then_inc(lb_done, 1)
            v.wait_ge(lb_done, 1)
            v.tensor_tensor(lbt[:, 1:3, :], lg, lbt[:, 0:1, :].broadcast_to([P, 2, H]), ALU.subtract)\
                .then_inc(lb_done, 1)
            v.wait_ge(lb_act, 2)
            v.tensor_tensor(lbt[:, 0, :], lbt[:, 1, :], lbt[:, 2, :], ALU.add).then_inc(lb_done, 1)
            v.wait_ge(lb_done, 3)
            v.reciprocal(lbt[:, 0, :], lbt[:, 0, :]).then_inc(lb_done, 1)
            v.wait_ge(lb_done, 4)
            v.tensor_tensor(lbt[:, 3, :], lbt[:, 1, :], lbt[:, 0, :], ALU.mult).then_inc(lb_done, 1)
            v.wait_ge(lb_done, 5)
            v.tensor_scalar(lbt[:, 4, :], lbt[:, 3, :], -1.0, 1.0, ALU.mult, ALU.add).then_inc(lb_done, 1)
            v.wait_ge(lb_done, 6)
            norm0.vec(v)

            def head(h, prev):
                if prev:
                    a_vec_tail(v, h - 1)
                    b_vec_rot(v, h - 1)
                    b_vec_scores(v, h - 1)
                    b_vec_states(v, h - 1)
                    b_vec_tail(v, h - 1)
                a_vec_gates(v, h)
                a_vec_levels(v, h)
                a_vec_states(v, h)

            head(0, False)
            with v.Fori(1, H) as h:
                head(h, True)
            a_vec_tail(v, H - 1)
            b_vec_rot(v, H - 1)
            b_vec_scores(v, H - 1)
            b_vec_states(v, H - 1)
            b_vec_tail(v, H - 1)
            for k in range(8):
                v.wait_ge(mh, k + 1)
                v.tensor_tensor(xl[:, k, :], mix[:, k, :], xh[:, k, :].bitcast(F32), ALU.subtract).then_inc(ml, 1)
            vec_residual(v, (U_OUT0, 1), G_OUT0)
            norm1.vec(v)
            ffn0.vec(v)
            norm2.vec(v)
            mlstm.vec(v)
            v.wait_ge(kept, 32)
            vec_residual(v, (U_DN1, 2), G_DN1)
            norm3.vec(v)
            ffn1.vec(v)
            normf.vec(v)

        @block.tensor
        def _(pe):
            pe.wait_ge(con_in, 16 * 5)
            norm0.pe(pe)

            def head(h, prev):
                def both(*fs):
                    return lambda: [f(pe, h - 1) for f in fs]
                if prev:
                    in0_unit(pe, h, 0, both(a_pe_tail))
                    a_pe_norm(pe, h - 1)
                    b_pe_rot(pe, h - 1)
                    in0_unit(pe, h, 1, both(b_pe_turns))
                    b_pe_scores(pe, h - 1)
                    in0_unit(pe, h, 2, both(b_pe_states))
                    b_pe_tail(pe, h - 1)
                else:
                    in0_unit(pe, h, 0, ready=(norm0.lo_done, 1))
                    in0_unit(pe, h, 1)
                    in0_unit(pe, h, 2)
                in0_unit(pe, h, 3, (both(b_pe_norm) if prev else None))
                a_pe_level(pe, h, 0)
                for j, (l0, l1) in ((4, (1, 2)), (5, (3, 4)), (6, (5, 6))):
                    in0_unit(pe, h, j, lambda: a_pe_level(pe, h, l0))
                    a_pe_level(pe, h, l1)

                def last_half():
                    a_pe_level(pe, h, 7)
                    a_pe_turns(pe, h)
                in0_unit(pe, h, 7, last_half)
                a_pe_head(pe, h)

            head(0, False)
            with pe.Fori(1, H) as h:
                head(h, True)
            for f in (a_pe_tail, a_pe_norm, b_pe_rot, b_pe_turns, b_pe_scores, b_pe_states, b_pe_tail, b_pe_norm):
                f(pe, H - 1)
            for j in range(2):
                pe_dense(pe, (U_OUT0 + j, 0), (G_OUT0 + j, 0), xh, xl, ready=(ml, 1) if j == 0 else None)
            with pe.Fori(1, 4) as i:
                for s in range(2):
                    pe_dense(pe, (U_OUT0 + s, i), (G_OUT0 + s, i), xh, xl)
            norm1.pe(pe)
            ffn0.pe(pe)
            norm2.pe(pe)
            mlstm.pe(pe)
            pe.wait_ge(mlstm.V.sem, mlstm.V.rounds(H))
            pe_down(pe, U_DN1, G_DN1, 2, 8, None, 0)
            norm3.pe(pe)
            ffn1.pe(pe)
            normf.pe(pe)


def _constants():
    import numpy as np
    f = np.float32
    con = np.zeros((P, N_CON), f)
    con[:, CON["ident"]:CON["ident"] + P] = np.eye(P)
    con[:, CON["ones"]:CON["ones"] + P] = 1
    half = P // 2
    perm = np.zeros((P, P))
    for m in range(half):
        perm[m + half, m] = -1
        perm[m, m + half] = 1
    con[:, CON["perm"]:CON["perm"] + P] = perm
    start = np.zeros(T, bool)
    start[0:SEQ:P] = True
    start[SEQ::TS] = True
    con[:, CON["reset"]:CON["reset"] + T] = ~start
    con[:, CON["ind"]:CON["ind"] + NB] = np.arange(P)[:, None] // TS == np.arange(NB)
    lg = np.log1p(-np.exp2(-5.0 - np.arange(H)))
    i = np.arange(P)
    for h in range(H):
        con[:, CON["tail"] + 2 * h] = np.exp(lg[h] * (P - 1 - i))
        con[:, CON["tail"] + 2 * h + 1] = np.exp(lg[h] * (TS - 1 - i % TS))
        con[:, CON["glast"] + 2 * h] = np.exp(lg[h] * P)
        con[:, CON["glast"] + 2 * h + 1] = np.exp(lg[h] * TS)
    con[:, CON["eps"]] = EPS
    con[:, CON["bd"]:CON["bd"] + P] = i[:, None] // 4 == i // 4
    s, j = i[:, None], i[None, :]
    same = s // TS == j // TS
    con[:, CON["caus"]:CON["caus"] + P] = np.where(s <= j, 0, NEVER)
    con[:, CON["caus"] + P:CON["caus"] + 2 * P] = np.where((s <= j) & same, 0, NEVER)
    for h in range(H):
        con[h, CON["sel"] + h * P:CON["sel"] + (h + 1) * P] = 1
    masks = np.zeros((P, len(LEVELS), P), f)
    for l, m in enumerate(LEVELS):
        masks[:, l] = (s // (2 * m) == j // (2 * m)) & (s // m % 2 == 0) & (j // m % 2 == 1)
    dret = np.zeros((H, P, 2, P), f)
    win = np.zeros((H, P, 2, P), f)
    for h in range(H):
        d = np.exp(lg[h] * np.maximum(j - s, 0)) * (s <= j)
        dret[h, :, 0] = d
        dret[h, :, 1] = d * same
        win[h, :, 0] = np.exp(lg[h] * (i + 1.0))
        win[h, :, 1] = np.exp(lg[h] * (i % TS + 1.0))
    pos = np.concatenate([np.arange(SEQ), np.tile(256 + np.arange(TS), NB)]).astype(f)
    inv = f(10000.0) ** (-(np.arange(half, dtype=f)) / f(half))
    ang = (pos[None, :] * np.tile(inv, 2)[:, None].astype(f)).astype(np.float64)
    return {"con": con, "masks": masks, "dret": dret, "win": win, "cos": np.cos(ang).astype(f),
            "sin": np.sin(ang).astype(f)}


def _arrays(a):
    import numpy as np

    def tiles(w, order=None):
        k, n = w.shape
        u = w.reshape(k // P, P, n // P, P).transpose(2, 1, 0, 3)
        return u if order is None else u[order]

    def down(w):
        u = tiles(w)
        nk = u.shape[2]
        pad = -nk % KD
        u = np.concatenate([u, np.zeros((*u.shape[:2], pad, P), u.dtype)], 2) if pad else u
        nu = u.shape[2] // KD
        return u.reshape(u.shape[0], P, nu, KD, P).transpose(0, 2, 1, 3, 4).reshape(-1, P, KD, P)

    def ffn(l):
        g, u = tiles(a["w_ffn_gate"][l]), tiles(a["w_ffn_up"][l])
        gu = np.stack([g, u], 1)
        out, at = [], 0
        for f in FF_PARTS:
            out.append(gu[at:at + f].reshape(-1, P, KD, P))
            out.append(down(a["w_ffn_down"][l][at * P:(at + f) * P]))
            at += f
        return out

    w = np.concatenate([
        tiles(a["w_in0"][0], [j * H + h for h in range(H) for j in range(8)]),
        tiles(a["w_out0"][0]), *ffn(0), tiles(a["w_up1"][0]), down(a["w_down1"][0]), *ffn(1)])
    assert w.shape[0] == N_UNITS, w.shape
    x = np.concatenate([a["x_prompt"].reshape(SEQ, D), a["x_sample"].reshape(NB * TS, D)])
    cols = lambda v: v.reshape(-1, P).T
    par = np.concatenate([cols(a["norm_mix"][0]), cols(a["norm_mix"][1]), cols(a["norm_ffn"][0]),
                          cols(a["norm_ffn"][1]), cols(a["norm_final"]), cols(a["lb_logits"][0]),
                          cols(a["lb_logits"][1]), cols(a["hgrn_norm"]), cols(a["ret_norm"]),
                          *[cols(a["conv_w"][0, i]) for i in range(4)], cols(a["conv_b"]), cols(a["mlstm_norm"]),
                          cols(a["mlstm_skip"])], 1)
    assert par.shape[1] == N_PAR
    wg = np.concatenate([a["w_ig"][0], a["w_fg"][0]], 1).reshape(3, CI, P // 4, 4, 8)
    wgx = np.repeat(wg[:, :, :, None], 4, 3).reshape(3, CI, P, 4, 8).transpose(2, 0, 1, 3, 4)
    wqkv = np.stack([a[n][0].reshape(CI, P, 4) for n in ("w_q1", "w_k1", "w_v1")]).transpose(2, 0, 1, 3)
    gsm = np.concatenate([a["b_ig"].T, a["b_fg"].T, a["state_mlstm_m"][0].T], 1)
    st_n = a["state_mlstm_n"][0].reshape(NB, H, KH, P).transpose(3, 1, 2, 0)
    st_c = a["state_mlstm_c"][0].transpose(1, 0, 3, 2).reshape(H * NB, KH, P, DH).transpose(0, 2, 1, 3)
    conv = a["state_conv"][0].reshape(NB, NCONV - 1, CI, P).transpose(3, 2, 0, 1)
    more = {"wgx": wgx, "wqkv": wqkv, "gsm": gsm, "st_n": st_n, "st_c": st_c, "conv": conv}
    return more | {"x": x.T.reshape(KD, P, T).transpose(1, 0, 2), "w": w, "par": par,
            "st_hgrn": a["state_hgrn"][0].transpose(1, 2, 0, 3), "st_ret": a["state_ret"][0].transpose(1, 2, 0, 3)}


_OUT = {"yT": (P, KD, T), "hgrn_p": (H, P, P), "hgrn_s": (H, P, NB, P), "ret_p": (H, P, P), "ret_s": (H, P, NB, P),
        "c_p": (H, P, KH, DH), "c_s": (H * NB, P, KH, DH), "n_p": (P, H, KH), "n_s": (P, H, KH, NB),
        "m_out": (H, 1 + NB), "conv_p": (P, CI, NCONV - 1), "conv_s": (P, CI, NB, NCONV - 1)}
_KEPT = {"x_kept": (P, KD, T), "z_kept": (CI, P, T)}


def kernel(**inputs):
    import numpy as np
    import concourse.bacc as bacc
    from concourse.bass_utils import run_bass_kernel_spmd
    a = {k: np.asarray(v) for k, v in inputs.items()}
    arrays = {k: np.ascontiguousarray(v) for k, v in (_arrays(a) | _constants()).items()}
    nc = bacc.Bacc("TRN2", target_bir_lowering=False, num_devices=1)
    io = {n: nc.dram_tensor(n, x.shape, F32, kind="ExternalInput").ap() for n, x in arrays.items()}
    io |= {n: nc.dram_tensor(n, s, F32, kind="ExternalOutput").ap() for n, s in _OUT.items()}
    io |= {n: nc.dram_tensor(n, s, F32, kind="Internal").ap() for n, s in _KEPT.items()}
    trunk(nc, io)
    r = run_bass_kernel_spmd(nc, [arrays], core_ids=[0]).results[0]
    y = r["yT"].transpose(2, 1, 0).reshape(T, D)
    c_s = r["c_s"].reshape(H, NB, P, KH, DH).transpose(1, 0, 4, 3, 2).reshape(1, NB, H, DH, DH)
    return tuple(np.ascontiguousarray(x) for x in (
        y[:SEQ].reshape(1, SEQ, D), y[SEQ:].reshape(NB, TS, D),
        r["hgrn_p"].reshape(1, 1, H, P, P), r["hgrn_s"].transpose(2, 0, 1, 3)[None],
        r["ret_p"].reshape(1, 1, H, P, P), r["ret_s"].transpose(2, 0, 1, 3)[None],
        r["c_p"].transpose(0, 3, 2, 1).reshape(1, 1, H, DH, DH), c_s,
        r["n_p"].transpose(1, 2, 0).reshape(1, 1, H, DH), r["n_s"].transpose(3, 1, 2, 0).reshape(1, NB, H, DH),
        r["m_out"][:, 0].reshape(1, 1, H), r["m_out"][:, 1:].T[None],
        r["conv_p"].transpose(2, 1, 0).reshape(1, 1, NCONV - 1, CI * P),
        r["conv_s"].transpose(2, 3, 1, 0).reshape(1, NB, NCONV - 1, CI * P)))
```

```python
from contextlib import ExitStack

import concourse.bass as bass
from concourse import mybir

F32 = mybir.dt.float32
F32R = mybir.dt.float32r
U8 = mybir.dt.uint8
ACT = mybir.ActivationFunctionType
ALU = mybir.AluOpType

P = 128
D = 1024
SEQ, NB, TS = 512, 8, 16
NP = SEQ // P
T = SEQ + NB * TS
HT = T // 2
KD = D // P
H = 4
FF_PARTS = (16, 6)
CI = 16
KH = 4
DH = KH * P
NCONV = 4
XS = NCONV - 1 + TS
XW = NCONV - 1 + SEQ + NB * XS
EPS = 1e-6
NEVER = -1e30
LEVELS = (1, 2, 4, 8, 16, 32, 64)

U_IN0 = 0
U_OUT0 = U_IN0 + 32
FF_UNITS = sum(2 * f + 8 * (2 if f > 8 else 1) for f in FF_PARTS)
U_FF0 = U_OUT0 + 8
U_UP1 = U_FF0 + FF_UNITS
U_DN1 = U_UP1 + 32
U_FF1 = U_DN1 + 16
N_UNITS = U_FF1 + FF_UNITS

PAR = {}
_at = 0
for _name, _n in (("mix", 16), ("ffn", 16), ("final", 8), ("lb", 8), ("hgrn", 1), ("ret", 1), ("convw", 64),
                  ("convb", 16), ("mnorm", 4), ("skip", 16)):
    PAR[_name] = _at
    _at += _n
N_PAR = _at
CON = {}
_at = 0
for _name, _n in (("ident", 128), ("ones", 128), ("perm", 128), ("reset", T), ("ind", 8), ("tail", 8),
                  ("glast", 8), ("eps", 1), ("bd", 128), ("caus", 256), ("sel", 512)):
    CON[_name] = _at
    _at += _n
N_CON = _at


class Steps:

    def __init__(self, sem, names, base=0):
        self.sem, self.names, self.n, self.base = sem, {x: i + 1 for i, x in enumerate(names)}, len(names), base

    def at(self, name, r=0):
        return r * self.n + self.base + self.names[name]

    def rounds(self, r):
        return r * self.n + self.base


def trunk(nc, io):
    ctx = ExitStack()
    with ctx:
        sem = lambda name: ctx.enter_context(nc.semaphore(name))
        top = [16512]

        def sb(name, shape, dt=F32, at=None):
            n = mybir.dt.size(dt)
            for x in shape[1:]:
                n *= x
            n = (n + 31) // 32 * 32
            if at is None:
                off = top[0]
                top[0] += n
            else:
                off = at[0]
                at[0] += n
            assert top[0] <= 229312, (name, top[0])
            return nc.alloc_sbuf_tensor_at(name, shape, dt, offset=off)

        xT = sb("xT", [P, KD, T])
        at_h = top[0]
        xh = sb("xh", [P, KD, T], F32R)
        xl = sb("xl", [P, KD, T], F32R)
        at_w = top[0]
        wraw = [sb(f"wraw{s}", [P, KD, P]) for s in range(2)]
        whi = [sb(f"whi{s}", [P, KD, P], F32R) for s in range(2)]
        wlo = [sb(f"wlo{s}", [P, KD, P], F32R) for s in range(2)]
        at_a = top[0]
        ah = sb("ah", [P, CI, T], F32R)
        top[0] = at_a + CI * XW * 4
        al = sb("al", [P, CI, T], F32R)
        par = sb("par", [P, N_PAR])
        con = sb("con", [P, N_CON])
        at_m = top[0]
        masks = sb("masks", [P, len(LEVELS), P], U8)
        eps = con[:, CON["eps"]:CON["eps"] + 1]
        ident = con[:, CON["ident"]:CON["ident"] + P]
        ones = con[:, CON["ones"]:CON["ones"] + P]
        perm = con[:, CON["perm"]:CON["perm"] + P]
        reset = con[:, CON["reset"]:CON["reset"] + T]
        at_r = top[0]

        a0, r0 = [at_a], [at_r]
        zq, zf, zi, zg, zbq, zbk, zbv, zbg = [sb(f"z_{x}", [P, T], at=a0) for x in
                                              ("aq", "af", "ai", "ag", "bq", "bk", "bv", "bg")]
        mix = sb("mix", [P, 8, T], at=a0)
        ga = {x: sb(f"a_{x}", [P, T], at=a0) for x in ("f", "k", "b", "eb", "q", "kh", "att")}
        dlev = [sb(f"dlev{s}", [P, T], at=a0) for s in range(2)]
        qk = [sb(f"qk{s}", [P, T], at=a0) for s in range(2)]
        cos = sb("cos", [P, T], at=a0)
        sin = sb("sin", [P, T], at=a0)
        dret = sb("dret", [P, 2, P], at=a0)
        win = sb("win", [P, 2, P], at=a0)
        bst = sb("bst", [P, P], at=a0)
        ast = sb("ast", [P, P], at=a0)
        lbt = sb("lbt", [P, 5, H], at=a0)
        assert a0[0] <= at_a + 2 * 16 * T * 4, a0[0] - at_a
        gb = {x: sb(f"b_{x}", [P, T], at=r0) for x in ("q", "k", "t", "kt", "vt")}
        ga["kt"] = sb("a_kt", [P, T], at=r0)
        ga["vt"] = sb("a_vt", [P, T], at=r0)
        asmp = sb("asmp", [P, NB, P], at=r0)
        bsmp = sb("bsmp", [P, NB, P], at=r0)
        vmask = sb("vmask", [P, NB, P], at=r0)
        assert r0[0] <= 229312, r0[0]
        n0 = [at_r]
        sq = [sb(f"sq{s}", [P, T], at=n0) for s in range(2)]
        nacc = sb("nacc", [P, T], at=n0)
        rstd = sb("rstd", [P, T], at=n0)
        ntmp = [sb(f"ntmp{s}", [P, T], at=n0) for s in range(2)]
        ffs = [sb(f"ffs{s}", [P, T], at=n0) for s in range(2)]
        fft = [sb(f"fft{s}", [P, T], at=n0) for s in range(2)]

        psd = [ctx.enter_context(nc.psum_tensor(f"psd{s}", [P, 2, 512], F32)) for s in range(2)]
        psm = ctx.enter_context(nc.psum_tensor("psm", [P, 4, 512], F32))

        w_loaded = [sem(f"w_loaded{s}") for s in range(2)]
        w_taken = sem("w_taken")
        w_high = sem("w_high")
        w_split = sem("w_split")
        pe_unit = sem("pe_unit")
        evac = [sem(f"evac{s}") for s in range(2)]
        con_in = sem("con_in")
        x_in = [sem(f"x_in{n}") for n in range(KD // 2)]
        tab_in = sem("tab_in")

        def halves(t, k, cut):
            return t[:, k, 0:cut], t[:, k, cut:T]

        def two(ap):
            return ap.rearrange("p (a c) -> p a c", a=2)

        def pe_dense(pe, n, g, hi, lo, k0=0, nk=8, first=True, last=True, ready=None, between=None, cut=HT):
            (nc_, ne), (gc, ge) = n, g
            slot, pair = nc_ % 2, gc % 2
            pe.wait_ge(w_split, nc_ + 2 * ne + 1)
            if first and not (isinstance(ge, int) and gc + 2 * ge < 2):
                pe.wait_ge(evac[pair], gc // 2 + ge)
            for k in range(nk):
                if ready is not None:
                    pe.wait_ge(ready[0], ready[1] + k)
                x0, x1 = halves(hi, k0 + k, cut)
                l0, l1 = halves(lo, k0 + k, cut)
                wh, wl = whi[slot][:, k, :], wlo[slot][:, k, :]
                o0, o1 = psd[pair][:, 0, 0:cut], psd[pair][:, 1, 0:T - cut]
                st, en = first and k == 0, last and k == nk - 1
                pe.matmul(o0, wh, x0, start=st, stop=False)
                pe.matmul(o1, wh, x1, start=st, stop=False)
                pe.matmul(o0, wh, l0, start=False, stop=False)
                pe.matmul(o1, wh, l1, start=False, stop=False)
                pe.matmul(o0, wl, x0, start=False, stop=en)
                mm = pe.matmul(o1, wl, x1, start=False, stop=en)
                if k == nk // 2 - 1 and between is not None:
                    between()
            mm.then_inc(pe_unit, 1)

        class Norm:

            def __init__(self, name, gain, g, free_at, x_at, final=False, own_sum=False):
                self.own_sum = own_sum
                self.sq_done = sem(f"{name}_sq")
                self.acc_done = sem(f"{name}_acc")
                self.sum_done = sem(f"{name}_sum")
                self.std_done = sem(f"{name}_std")
                self.v_done = sem(f"{name}_v")
                self.hi_done = sem(f"{name}_hi")
                self.lo_done = sem(f"{name}_lo")
                self.gain, self.g, self.free_at, self.x_at, self.final = gain, g, free_at, x_at, final

            def act(self, a):
                for k in range(KD):
                    a.wait_ge(*self.x_at(k))
                    if k >= 2:
                        a.wait_ge(self.acc_done, k)
                    a.activation(sq[k % 2][:], xT[:, k, :], ACT.Square).then_inc(self.sq_done, 1)
                a.wait_ge(self.sum_done, 1)
                a.activation(two(rstd[:]), psd[self.g % 2][:, :, 0:HT], ACT.Ln, bias=eps,
                             scale=1.0 / D).then_inc(self.std_done, 1)
                a.wait_ge(self.std_done, 1)
                a.activation(rstd[:], rstd[:], ACT.Exp, scale=-0.5).then_inc(self.std_done, 1)
                a.sem_inc(evac[self.g % 2], 1)
                if self.final:
                    return
                a.wait_ge(pe_unit, self.free_at)
                for k in range(KD):
                    a.wait_ge(self.v_done, k + 1)
                    a.activation(xh[:, k, :], ntmp[k % 2][:], ACT.Copy).then_inc(self.hi_done, 1)

            def begin(self, v):
                v.memset(nacc[:], 0.0).then_inc(self.acc_done, 1)

            def add(self, v, k, s):
                v.wait_ge(self.sq_done, k + 1)
                v.wait_ge(self.acc_done, k + 1)
                v.tensor_tensor(nacc[:], nacc[:], sq[s][:], ALU.add).then_inc(self.acc_done, 1)

            def vec(self, v):
                if self.own_sum:
                    self.begin(v)
                    for k in range(KD):
                        self.add(v, k, k % 2)
                v.wait_ge(self.std_done, 2)
                for k in range(KD + 1):
                    if k < KD:
                        if k >= 2 and self.final:
                            v.wait_ge(y_stored[k % 2], 16 * (k // 2))
                        elif k >= 2:
                            v.wait_ge(self.lo_done, k - 1)
                        v.scalar_tensor_tensor(ntmp[k % 2][:], xT[:, k, :], par[:, self.gain + k:self.gain + k + 1],
                                               rstd[:], ALU.mult, ALU.mult).then_inc(self.v_done, 1)
                    if k >= 1 and not self.final:
                        v.wait_ge(self.hi_done, k)
                        v.tensor_tensor(xl[:, k - 1, :], ntmp[(k - 1) % 2][:], xh[:, k - 1, :].bitcast(F32),
                                        ALU.subtract).then_inc(self.lo_done, 1)

            def pe(self, p):
                p.wait_ge(self.acc_done, KD + 1)
                if self.g >= 2:
                    p.wait_ge(evac[self.g % 2], self.g // 2)
                p.matmul(psd[self.g % 2][:, 0, 0:HT], ones, nacc[:, 0:HT], start=True, stop=True)
                p.matmul(psd[self.g % 2][:, 1, 0:HT], ones, nacc[:, HT:T], start=True,
                         stop=True).then_inc(self.sum_done, 1)

        G_N0 = 0
        G_IN0 = 1
        G_OUT0 = G_IN0 + 32
        G_N1 = G_OUT0 + 8
        G_FF0 = G_N1 + 1
        N_FF = sum(2 * f + 8 for f in FF_PARTS)
        G_N2 = G_FF0 + N_FF
        G_UP1 = G_N2 + 1
        G_DN1 = G_UP1 + 32
        G_N3 = G_DN1 + 8
        G_FF1 = G_N3 + 1
        G_NF = G_FF1 + N_FF

        def left(g):
            return evac[g % 2], g // 2 + 1
        y_stored = [sem(f"y_stored{s}") for s in range(2)]
        norm0 = Norm("n0", PAR["mix"], G_N0, 0, lambda k: (x_in[k // 2], 16), own_sum=True)
        norm1 = Norm("n1", PAR["ffn"], G_N1, U_FF0, lambda k: left(G_OUT0 + k))
        norm2 = Norm("n2", PAR["mix"] + 8, G_N2, U_UP1, lambda k: left(G_N2 - 8 + k))
        norm3 = Norm("n3", PAR["ffn"] + 8, G_N3, U_FF1, lambda k: left(G_DN1 + k))
        normf = Norm("nf", PAR["final"], G_NF, None, lambda k: left(G_NF - 8 + k), final=True)

        NL = len(LEVELS)
        z_done = Steps(sem("z_done"), ["aq", "af", "ai", "ag", "bq", "bk", "bv", "bg"])
        lv = [("p", l) for l in range(NL + 1)]
        aV = Steps(sem("aV"), ["f", "k", "b", "q", "dk0", "dk1", "kh"]
                   + [x for l in range(NL) for x in ((("d1", l), ("d0", l)))][:2] + [("cp", 0)]
                   + [x for l in range(NL) for x in (
                       [("qk1", l), ("qk0", l)] + ([("d1", l + 1), ("d0", l + 1)] if l + 1 < NL else []) + [("cp", l + 1)])]
                   + ["S0", "S1", "S2", "S3", "vm", "Sd", "Sa0", "Sa1", "u0", "u1", "mixg", "mixn"])
        aS = Steps(sem("aS"), ["ln", "eb", "ek"] + [("g", l) for l in range(NL)] + ["vt", "kt", "sq", "lnr", "r"])
        aP = Steps(sem("aP"), [("p", l) for l in range(NL + 1)] + ["vt", "kt", "st0", "o0", "st1", "o1", "st2", "o2",
                   "st3", "o3", "s0", "s1", "oS", "n"])
        bV = Steps(sem("bV"), ["tq", "sq", "q", "tk", "sk", "k", "d0", "d1", "qh0", "qh1",
                   "S0", "S1", "S2", "S3", "vm", "Sa0", "Sa1", "u0", "u1", "mixn", "mixg"])
        bS = Steps(sem("bS"), ["vt", "kt0", "kt1", "sq", "lnr", "r"])
        bP = Steps(sem("bP"), ["pq", "pk", "vt", "kt", "att", "st0", "o0", "st1", "o1", "st2", "o2",
                   "st3", "o3", "s0", "s1", "oS", "n"])
        a_in = sem("a_in")
        b_in = sem("b_in")
        a_out = sem("a_out")
        b_out = sem("b_out")
        lb_done = sem("lb_done")
        lb_act = sem("lb_act")
        cp_turn = sem("cp_turn")

        bank = [psm[:, i, :] for i in range(4)]

        def tt(i):
            return slice(i * P, (i + 1) * P)

        def a_pe_level(pe, h, l):
            if l == 0:
                pe.wait_ge(aV.sem, aV.at("k", h))
            else:
                pe.wait_ge(aV.sem, aV.at(("qk0", l - 1), h))
            b0, b1 = bank[2 * (l % 2)], bank[2 * (l % 2) + 1]
            if l == 1 and not (isinstance(h, int) and h == 0):
                pe.wait_ge(bS.sem, bS.at("lnr", h - 1))
            if l >= 2:
                pe.wait_ge(aV.sem, aV.at(("cp", l - 2), h))
            tiles = NP + (l == 0 or LEVELS[l - 1] < TS)
            for t in range(tiles):
                lhs = ga["k"][:, tt(t)] if l == 0 else qk[(l - 1) % 2][:, tt(t)]
                rhs = zq[:, tt(t)] if l == 0 else lhs
                o = b0[:, tt(t)] if t < NP else b1[:, 0:P]
                mm = pe.matmul(o, lhs, rhs, start=True, stop=True)
            mm.then_inc(aP.sem, 1)

        def pe_turn(pe, src, b0, b1, done):
            for t in range(NP + 1):
                o = b0[:, tt(t)] if t < NP else b1[:, 0:P]
                mm = pe.transpose(o, src[:, tt(t)], ident)
            mm.then_inc(done, 1)

        def pe_states(pe, h, g, PS, VS, kt_at, SS, att, q, S, t0, t1):
            for t in range(t0, t1):
                if t == 0:
                    pe.wait_ge(SS.sem, SS.at(kt_at, h))
                else:
                    pe.wait_ge(VS.sem, VS.at(f"S{t - 1}", h))
                pe.matmul(bank[2 + t % 2][:, 0:P], g["kt"][:, tt(t)], g["vt"][:, tt(t)], start=True,
                          stop=True).then_inc(PS.sem, 1)
                mm = pe.matmul(bank[0][:, tt(t)], g["vt"][:, tt(t)], att[:, tt(t)], start=True, stop=(t == 0))
                if t > 0:
                    mm = pe.matmul(bank[0][:, tt(t)], S[:], q[:, tt(t)], start=False, stop=True)
                mm.then_inc(PS.sem, 1)

        def pe_sample(pe, h, g, PS, VS, smp, s_in, att, q):
            pe.wait_ge(s_in, 16 * (h + 1))
            pe.wait_ge(VS.sem, VS.at("vm", h))
            for r in range(2):
                pe.matmul(bank[2 + r], g["kt"][:, tt(NP)], vmask[:, 4 * r:4 * r + 4, :].rearrange("p b v -> p (b v)"),
                          start=True, stop=True).then_inc(PS.sem, 1)
            for b in range(NB):
                c = b * TS
                pe.matmul(bank[1][:, c:c + TS], smp[:, b, :], q[:, SEQ + c:SEQ + c + TS], start=(b == 0), stop=False,
                          skip_group_check=True)
            mm = pe.matmul(bank[1][:, 0:P], g["vt"][:, tt(NP)], att[:, tt(NP)], start=False, stop=True,
                           skip_group_check=True)
            mm.then_inc(PS.sem, 1)

        def pe_headnorm(pe, h, PS, SS, src):
            pe.wait_ge(SS.sem, SS.at("sq", h))
            pe.matmul(bank[2][:, 0:HT], ones, src[:, 0:HT], start=True, stop=True)
            pe.matmul(bank[3][:, 0:HT], ones, src[:, HT:T], start=True, stop=True).then_inc(PS.sem, 1)

        def a_pe_turns(pe, h):
            pe.wait_ge(aV.sem, aV.at(("cp", NL - 1), h))
            pe_turn(pe, zi, bank[0], bank[1], aP.sem)
            pe.wait_ge(aV.sem, aV.at(("cp", NL), h))
            pe_turn(pe, ga["kh"], bank[2], bank[3], aP.sem)

        def a_pe_head(pe, h):
            pe_states(pe, h, ga, aP, aV, "kt", aS, ga["att"], ga["q"], ast, 0, NP)

        def a_pe_tail(pe, h):
            pe.wait_ge(aV.sem, aV.at("S3", h))
            pe_sample(pe, h, ga, aP, aV, asmp, a_in, ga["att"], ga["q"])

        def a_pe_norm(pe, h):
            pe_headnorm(pe, h, aP, aS, ga["kh"])

        def b_pe_rot(pe, h):
            pe.wait_ge(z_done.sem, z_done.at("bk", h))
            pe.matmul(bank[0][:, 0:HT], perm, zbq[:, 0:HT], start=True, stop=True)
            pe.matmul(bank[1][:, 0:HT], perm, zbq[:, HT:T], start=True, stop=True).then_inc(bP.sem, 1)
            pe.wait_ge(aS.sem, aS.at("lnr", h))
            pe.matmul(bank[2][:, 0:HT], perm, zbk[:, 0:HT], start=True, stop=True)
            pe.matmul(bank[3][:, 0:HT], perm, zbk[:, HT:T], start=True, stop=True).then_inc(bP.sem, 1)

        def b_pe_turns(pe, h):
            pe.wait_ge(z_done.sem, z_done.at("bv", h))
            pe.wait_ge(bV.sem, bV.at("sq", h))
            pe_turn(pe, zbv, bank[0], bank[1], bP.sem)

        def b_pe_turn_k(pe, h):
            pe.wait_ge(bV.sem, bV.at("k", h))
            pe_turn(pe, gb["k"], bank[2], bank[3], bP.sem)

        def b_pe_scores(pe, h):
            pe.wait_ge(bS.sem, bS.at("vt", h))
            for t in range(NP + 1):
                o = bank[0][:, tt(t)] if t < NP else bank[1][:, 0:P]
                mm = pe.matmul(o, gb["k"][:, tt(t)], gb["q"][:, tt(t)], start=True, stop=True)
            mm.then_inc(bP.sem, 1)

        def b_pe_states(pe, h):
            pe.wait_ge(bV.sem, bV.at("qh1", h))
            pe_states(pe, h, gb, bP, bV, "kt1", bS, gb["t"], gb["q"], bst, 0, NP)

        def b_pe_tail(pe, h):
            pe.wait_ge(bV.sem, bV.at("S3", h))
            pe_sample(pe, h, gb, bP, bV, bsmp, b_in, gb["t"], gb["q"])

        def b_pe_norm(pe, h):
            pe_headnorm(pe, h, bP, bS, gb["k"])

        def in0_unit(pe, h, j, between=None, ready=None):
            pe_dense(pe, (U_IN0 + j, 4 * h), (G_IN0 + j, 4 * h), xh, xl, between=between, ready=ready)

        def seqs(ap, lo, n, w):
            return ap[:, lo:lo + n * w].rearrange("p (n w) -> p n w", w=w)

        def a_vec_gates(v, h):
            lbh, omh = lbt[:, 3, bass.ds(h, 1)], lbt[:, 4, bass.ds(h, 1)]
            v.wait_ge(z_done.sem, z_done.at("af", h))
            v.tensor_scalar(ga["f"][:], zf[:], omh, lbh, ALU.mult, ALU.add).then_inc(aV.sem, 1)
            v.wait_ge(aV.sem, aV.at("f", h))
            v.tensor_scalar(ga["k"][:], ga["f"][:], -1.0, 1.0, ALU.mult, ALU.add).then_inc(aV.sem, 1)
            v.wait_ge(aS.sem, aS.at("ln", h))
            v.tensor_tensor_scan(ga["b"][:], reset, ga["f"][:], 0.0, ALU.mult, ALU.add).then_inc(aV.sem, 1)
            v.wait_ge(aS.sem, aS.at("eb", h))
            v.tensor_tensor(ga["q"][:], zq[:], ga["eb"][:], ALU.mult).then_inc(aV.sem, 1)
            for lo, n, w in ((0, NP, P), (SEQ, NB, TS)):
                b = seqs(ga["b"], lo, n, w)
                v.tensor_tensor(seqs(ga["kh"], lo, n, w), b[:, :, w - 1:w].broadcast_to([P, n, w]), b,
                                ALU.subtract).then_inc(aV.sem, 1)
            v.wait_ge(aS.sem, aS.at("ek", h))
            v.tensor_tensor(ga["kh"][:], ga["k"][:], ga["kh"][:], ALU.mult).then_inc(aV.sem, 1)

        def width(l):
            return T if LEVELS[l] < TS else SEQ

        def a_vec_diff(v, h, l):
            m = LEVELS[l]
            n = width(l) // (2 * m)
            b = ga["b"][:, 0:width(l)].rearrange("p (n s m) -> p n s m", s=2, m=m)
            d = dlev[l % 2][:, 0:width(l)].rearrange("p (n s m) -> p n s m", s=2, m=m)
            mid = b[:, :, 0, m - 1:m].broadcast_to([P, n, m])
            if l == 0:
                v.wait_ge(aV.sem, aV.at("b", h))
            v.tensor_tensor(d[:, :, 1, :], b[:, :, 1, :], mid, ALU.subtract).then_inc(aV.sem, 1)
            v.tensor_tensor(d[:, :, 0, :], mid, b[:, :, 0, :], ALU.subtract).then_inc(aV.sem, 1)

        def a_vec_qk(v, h, l):
            m = LEVELS[l]
            four = lambda x: x[:, 0:width(l)].rearrange("p (n s m) -> p n s m", s=2, m=m)
            g, o = four(dlev[l % 2]), four(qk[l % 2])
            v.wait_ge(aS.sem, aS.at(("g", l), h))
            if l >= 2:
                v.wait_ge(aP.sem, aP.at(("p", l - 1), h))
            v.tensor_tensor(o[:, :, 1, :], four(zq)[:, :, 1, :], g[:, :, 1, :], ALU.mult).then_inc(aV.sem, 1)
            v.tensor_tensor(o[:, :, 0, :], four(ga["k"])[:, :, 0, :], g[:, :, 0, :], ALU.mult).then_inc(aV.sem, 1)

        def a_vec_take(v, h, l):
            b0, b1 = 2 * (l % 2), 2 * (l % 2) + 1
            att = ga["att"]
            v.wait_ge(aP.sem, aP.at(("p", l), h))
            if l == 0:
                v.tensor_tensor(seqs(att, 0, NP, P), bank[b0].rearrange("p (n w) -> p n w", w=P),
                                ident.unsqueeze(1).broadcast_to([P, NP, P]), ALU.mult)
                v.tensor_tensor(att[:, SEQ:T], bank[b1][:, 0:P], ident, ALU.mult).then_inc(aV.sem, 1)
                return
            mk = masks[:, l - 1, :]
            v.wait_ge(aV.sem, aV.at(("cp", l - 1), h))
            v.sem_inc(cp_turn, 1)
            if LEVELS[l - 1] < TS:
                v.copy_predicated(att[:, SEQ:T], mk, bank[b1][:, 0:P])
            v.copy_predicated(seqs(att, 0, NP, P), mk.unsqueeze(1).broadcast_to([P, NP, P]),
                              bank[b0].rearrange("p (n w) -> p n w", w=P)).then_inc(aV.sem, 1)

        def a_vec_first_level(v, h):
            a_vec_take(v, h, 0)
            a_vec_qk(v, h, 0)
            a_vec_diff(v, h, 1)

        def a_vec_levels(v, h):
            a_vec_take(v, h, 1)
            for l in range(1, NL):
                a_vec_qk(v, h, l)
                if l + 1 < NL:
                    a_vec_diff(v, h, l + 1)
                a_vec_take(v, h, l + 1)

        def vec_prompt_states(v, h, PS, VS, S, out, decay):
            for t in range(NP):
                v.wait_ge(PS.sem, PS.at(f"st{t}", h))
                src = bank[2 + t % 2][:, 0:P]
                if t == 0:
                    if not isinstance(h, int) or h:
                        v.wait_ge(out, 16 * (2 * h))
                    v.tensor_copy(S[:], src).then_inc(VS.sem, 1)
                else:
                    v.wait_ge(PS.sem, PS.at(f"o{t}", h))
                    v.wait_ge(VS.sem, VS.at(f"S{t - 1}", h))
                    v.scalar_tensor_tensor(S[:], S[:], decay(t), src, ALU.mult, ALU.add).then_inc(VS.sem, 1)

        def vec_mask_v(v, h, g, VS, SS):
            ind = con[:, CON["ind"]:CON["ind"] + NB]
            v.wait_ge(SS.sem, SS.at("vt", h))
            v.tensor_tensor(vmask[:], g["vt"][:, tt(NP)].unsqueeze(1).broadcast_to([P, NB, P]),
                            ind.unsqueeze(2).broadcast_to([P, NB, P]), ALU.mult).then_inc(VS.sem, 1)

        def a_vec_states(v, h):
            vec_prompt_states(v, h, aP, aV, ast, a_out, lambda t: ga["eb"][:, t * P + P - 1:t * P + P])

        def a_vec_tail(v, h):
            vec_mask_v(v, h, ga, aV, aS)
            v.wait_ge(aP.sem, aP.at("oS", h))
            dec = seqs(ga["eb"], SEQ, NB, TS)[:, :, TS - 1:TS].broadcast_to([P, NB, P])
            v.tensor_tensor(asmp[:], asmp[:], dec, ALU.mult).then_inc(aV.sem, 1)
            v.wait_ge(aV.sem, aV.at("Sd", h))
            for r in range(2):
                s = asmp[:, 4 * r:4 * r + 4, :].rearrange("p b v -> p (b v)")
                v.tensor_tensor(s, s, bank[2 + r], ALU.add).then_inc(aV.sem, 1)
            v.wait_ge(z_done.sem, z_done.at("ag", h))
            v.tensor_tensor(ga["att"][:, 0:SEQ], bank[0], zg[:, 0:SEQ], ALU.mult).then_inc(aV.sem, 1)
            v.tensor_tensor(ga["att"][:, SEQ:T], bank[1][:, 0:P], zg[:, SEQ:T], ALU.mult).then_inc(aV.sem, 1)
            v.wait_ge(aV.sem, aV.at("u1", h))
            v.tensor_scalar(mix[:, bass.ds(h, 1), :].rearrange("p a c -> p (a c)"), ga["att"][:],
                            par[:, PAR["hgrn"]:PAR["hgrn"] + 1], None, ALU.mult).then_inc(aV.sem, 1)
            v.wait_ge(aS.sem, aS.at("r", h))
            v.wait_ge(aV.sem, aV.at("mixg", h))
            m = mix[:, bass.ds(h, 1), :].rearrange("p a c -> p (a c)")
            v.tensor_tensor(m, m, ga["kh"][:], ALU.mult).then_inc(aV.sem, 1)

        def b_vec_rot(v, h):
            for z, o, b0, st in ((zbq, gb["q"], 0, ("tq", "sq", "pq")), (zbk, gb["k"], 2, ("tk", "sk", "pk"))):
                if b0 == 0:
                    v.wait_ge(z_done.sem, z_done.at("bk", h))
                v.tensor_tensor(o[:], z[:], cos[:], ALU.mult).then_inc(bV.sem, 1)
                v.wait_ge(bP.sem, bP.at(st[2], h))
                v.tensor_tensor(two(gb["t"][:]), psm[:, b0:b0 + 2, 0:HT], two(sin[:]), ALU.mult).then_inc(bV.sem, 1)
                v.wait_ge(bV.sem, bV.at(st[1], h))
                v.tensor_tensor(o[:], o[:], gb["t"][:], ALU.add).then_inc(bV.sem, 1)
                v.wait_ge(bV.sem, bV.at("q" if b0 == 0 else "k", h))

        def b_vec_scores(v, h):
            v.wait_ge(bP.sem, bP.at("att", h))
            v.wait_ge(b_in, 16 * 3 * (h + 1))
            v.tensor_tensor(seqs(gb["t"], 0, NP, P), bank[0].rearrange("p (n w) -> p n w", w=P),
                            dret[:, 0:1, :].broadcast_to([P, NP, P]), ALU.mult).then_inc(bV.sem, 1)
            v.tensor_tensor(gb["t"][:, SEQ:T], bank[1][:, 0:P], dret[:, 1, :], ALU.mult).then_inc(bV.sem, 1)
            v.tensor_tensor(seqs(gb["q"], 0, NP, P), seqs(gb["q"], 0, NP, P),
                            win[:, 0:1, :].broadcast_to([P, NP, P]), ALU.mult).then_inc(bV.sem, 1)
            v.tensor_tensor(gb["q"][:, SEQ:T], gb["q"][:, SEQ:T], win[:, 1, :], ALU.mult).then_inc(bV.sem, 1)

        def b_vec_states(v, h):
            vec_prompt_states(v, h, bP, bV, bst, b_out,
                              lambda t: con[:, bass.ds(CON["glast"] + 2 * h, 1)])

        def b_vec_tail(v, h):
            v.wait_ge(bP.sem, bP.at("oS", h))
            for r in range(2):
                s = bsmp[:, 4 * r:4 * r + 4, :].rearrange("p b v -> p (b v)")
                v.scalar_tensor_tensor(s, s, con[:, bass.ds(CON["glast"] + 2 * h + 1, 1)], bank[2 + r], ALU.mult,
                                       ALU.add).then_inc(bV.sem, 1)
            v.tensor_copy(gb["t"][:, 0:SEQ], bank[0]).then_inc(bV.sem, 1)
            v.tensor_copy(gb["t"][:, SEQ:T], bank[1][:, 0:P]).then_inc(bV.sem, 1)

        def b_vec_mix(v, h):
            v.wait_ge(bS.sem, bS.at("r", h))
            v.scalar_tensor_tensor(gb["t"][:], gb["t"][:], par[:, PAR["ret"]:PAR["ret"] + 1], gb["k"][:], ALU.mult,
                                   ALU.mult).then_inc(bV.sem, 1)
            v.wait_ge(bV.sem, bV.at("mixn", h))
            v.wait_ge(z_done.sem, z_done.at("bg", h))
            v.tensor_tensor(mix[:, bass.ds(h + 4, 1), :].rearrange("p a c -> p (a c)"), gb["t"][:], zbg[:],
                            ALU.mult).then_inc(bV.sem, 1)

        def in0_evac(a, h, j):
            name = ["aq", "af", "ai", "ag", "bq", "bk", "bv", "bg"][j]
            func = {"af": ACT.Sigmoid, "ag": ACT.Sigmoid, "bg": ACT.Silu}.get(name, ACT.Copy)
            dst = (zq, zf, zi, zg, zbq, zbk, zbv, zbg)[j]
            again = not isinstance(h, int) or h > 0
            if again:
                user = {"aq": (aV, ("qk1", NL - 1)), "af": (aV, "f"), "ai": (aP, "vt"), "ag": (aV, "u1"),
                        "bq": (bV, "k"), "bk": (bV, "k"), "bv": (bP, "vt"), "bg": (bV, "mixg")}[name]
                a.wait_ge(user[0].sem, user[0].at(user[1], h - 1))
                if name == "bk":
                    a.wait_ge(bP.sem, bP.at("pk", h - 1))
                if name == "bq":
                    a.wait_ge(bP.sem, bP.at("pq", h - 1))
                if name == "aq":
                    a.wait_ge(aP.sem, aP.at(("p", 0), h - 1))
            n = U_IN0 + j
            a.wait_ge(pe_unit, n + 8 * h + 1)
            g = G_IN0 + j
            scale = float(P) ** -0.5 if name == "bk" else 1.0
            a.activation(two(dst[:]), psd[g % 2][:, :, 0:HT], func, scale=scale).then_inc(z_done.sem, 1)
            a.wait_ge(z_done.sem, z_done.at(name, h))
            a.sem_inc(evac[g % 2], 1)

        def a_act_gates(a, h):
            a.wait_ge(aV.sem, aV.at("k", h))
            a.activation(ga["f"][:], ga["f"][:], ACT.Ln).then_inc(aS.sem, 1)
            a.wait_ge(aV.sem, aV.at("b", h))
            a.activation(ga["eb"][:], ga["b"][:], ACT.Exp).then_inc(aS.sem, 1)
            a.wait_ge(aV.sem, aV.at("dk1", h))
            a.activation(ga["kh"][:], ga["kh"][:], ACT.Exp).then_inc(aS.sem, 1)

        def a_act_level(a, h, l):
            a.wait_ge(aV.sem, aV.at(("d0", l), h))
            d = dlev[l % 2][:, 0:width(l)]
            a.activation(d, d, ACT.Exp).then_inc(aS.sem, 1)

        def act_turned(a, h, dst, b0, PS, SS, name, scales=(1.0, 1.0), steps=1):
            a.wait_ge(PS.sem, PS.at(name, h))
            i = a.activation(dst[:, 0:SEQ], bank[b0], ACT.Copy, scale=scales[0])
            if steps == 2:
                i.then_inc(SS.sem, 1)
            a.activation(dst[:, SEQ:T], bank[b0 + 1][:, 0:P], ACT.Copy, scale=scales[1]).then_inc(SS.sem, 1)

        def a_act_turns(a, h):
            act_turned(a, h, ga["vt"], 0, aP, aS, "vt")
            act_turned(a, h, ga["kt"], 2, aP, aS, "kt")

        def act_headnorm(a, h, PS, VS, SS, src, buf):
            a.wait_ge(VS.sem, VS.at("u1", h))
            a.activation(buf[:], src[:], ACT.Square).then_inc(SS.sem, 1)
            a.wait_ge(PS.sem, PS.at("n", h))
            a.activation(two(buf[:]), psm[:, 2:4, 0:HT], ACT.Ln, bias=eps, scale=1.0 / P).then_inc(SS.sem, 1)
            a.wait_ge(SS.sem, SS.at("lnr", h))
            a.activation(buf[:], buf[:], ACT.Exp, scale=-0.5).then_inc(SS.sem, 1)

        def a_act_norm(a, h):
            act_headnorm(a, h, aP, aV, aS, ga["att"], ga["kh"])

        def b_act_turns(a, h):
            act_turned(a, h, gb["vt"], 0, bP, bS, "vt")
            tail = lambda i: con[:, bass.ds(CON["tail"] + 2 * h + i, 1)]
            act_turned(a, h, gb["kt"], 2, bP, bS, "kt", (tail(0), tail(1)), 2)

        def b_act_norm(a, h):
            act_headnorm(a, h, bP, bV, bS, gb["t"], gb["k"])

        mh = sem("mh")
        ml = sem("ml")

        kept = sem("kept")
        x1, h1, r1 = [16512], [at_h], [at_m]
        xp = sb("xp", [P, CI, XW], at=[at_a])
        xc = sb("xc", [P, CI, T], at=[at_a + CI * XW * 4])
        qT, kT = sb("qT", [P, KH, T], at=h1), sb("kT", [P, KH, T], at=h1)
        ktok = sb("ktok", [P, NP + 1, DH], at=h1)
        vtok = sb("vtok", [P, NP + 1, DH], at=h1)
        wqkv = sb("wqkv", [P, 3, CI, 4], at=r1)
        nS = sb("nS", [P, H, KH, NB], at=r1)
        nP = sb("nP", [P, H, KH], at=r1)
        acol = sb("acol", [P, NP + 1, H], at=r1)
        rowM = sb("rowM", [H, T], at=r1)
        rowW = sb("rowW", [H, T], at=r1)
        rowE = sb("rowE", [H, T], at=r1)
        selh = sb("selh", [H, P], at=r1)
        wl = sb("wl", [P, NP + 1], at=r1)
        dec = sb("dec", [P, NP + NB], at=r1)
        gsm = sb("gsm", [H, 2 + NB], at=r1)
        mo = sb("mo", [H, 1 + NB], at=r1)
        r2 = [r1[0]]
        cv = [sb(f"cv{s}", [P, T], at=r2) for s in range(2)]
        zb = [sb(f"zb{s}", [P, T], at=r2) for s in range(2)]
        cst = sb("cst", [P, CI, NB, NCONV - 1], at=r2)
        cpo = sb("cpo", [P, CI, NCONV - 1], at=r2)
        gt = sb("gt", [P, CI, 8], at=r2)
        gC = sb("gC", [P, CI, 8], at=r2)
        gX = sb("gX", [P, CI, 8], at=r2)
        wgx = sb("wgx", [P, 3, CI, 4, 8], at=r2)
        assert r2[0] <= 229312, r2[0]
        pre = sb("pre", [8, T], at=x1)
        fgr, igr, t1, bro, mro, i2, l2 = [sb(f"row_{n}", [H, T], at=x1) for n in
                                          ("f", "i", "t", "b", "m", "i2", "l2")]
        assert x1[0] <= at_h
        r3, x3 = [r1[0]], [16512]
        Cs = [sb(f"Cs{s}", [P, KH, DH], at=x3) for s in range(2)]
        blk = [sb(f"blk{s}", [P, 3, P], at=x3) for s in range(2)]
        w3 = [at_w]
        Cs.append(sb("Cs2", [P, KH, DH], at=w3))
        zt = sb("zt", [P, KH, T], at=w3)
        em = sb("em", [P, T], at=w3)
        rs = sb("rs", [P, T], at=w3)
        assert w3[0] <= at_w + 6 * KD * P * 4
        QZ = (KH + 1) * P - TS
        qz = [sb("qz0", [P, QZ], at=[x3[0] - 3 * P * 4])]
        assert x3[0] - 3 * P * 4 + QZ * 4 <= at_h
        assert x3[0] <= at_h
        Cp = sb("Cp", [P, KH, DH], at=r3)
        att1 = sb("att1", [P, T], at=r3)
        vtmp = [sb(f"vtmp{s}", [P, T], at=r3) for s in range(2)]
        kw = sb("kw", [P, DH], at=r3)
        vm = [sb(f"vm{s}", [P, DH], at=r3) for s in range(2)]
        qz.append(sb("qz1", [P, QZ], at=r3))
        assert r3[0] <= 229312, r3[0]

        flat = lambda p: p.rearrange("p a c -> p (a c)")
        pD = [flat(psd[s][:, :, :]) for s in range(2)]
        pM = [flat(psm[:, 2 * s:2 * s + 2, :]) for s in range(2)]
        U = [psd[0][:, 0, :], psd[0][:, 1, :], bank[2], bank[3]]
        tiles5 = range(NP + 1)

        def streams(ap, c0, w):
            return ap[:, NCONV - 1 + SEQ:XW].rearrange("p (b c) -> p b c", c=XS)[:, :, c0:c0 + w]

        BESIDE = [["dmax", "rden0"], ["rden1", ("hd", 0), ("hd", 1)], [("hd", 2), ("hd", 3)],
                  [("xc", k) for k in range(KH)], [("ln", 0), ("ln", 1), ("ln", 2)],
                  [("ln", 3)] + [("sk", k) for k in range(KH)], [("z", k) for k in range(KH)],
                  [("lo", k) for k in range(KH)]]

        class MLstm:
            def __init__(self):
                self.w_in = sem("m_w_in")
                self.pad = sem("m_pad")
                self.conv = sem("m_conv")
                self.xc = sem("m_xc")
                self.zsil = sem("m_zsil")
                self.zst = [sem(f"m_zst{s}") for s in range(2)]
                self.outs = sem("m_outs")
                self.gw = sem("m_gw")
                self.gP = Steps(sem("m_gP"), ["gate", "sel", "a"])
                self.gS = Steps(sem("m_gS"), ["pre", "abs", "exp", "ln", "E", "W", "a"])
                self.gV = Steps(sem("m_gV"), ["f", "i", "lf", "b", "i2", "l2", "lm", "ix", "lx", "m", "M", "a",
                                              "w0", "w1", "w2", "mo0", "mo1", "cpo", "cso"])
                kts = range(KH)
                self.P = Steps(sem("m_P"), base=1, names=[(x, k) for k in kts for x in ("q", "k", "v", "tk", "tv")]
                               + ["sc", "rM", "rW", "rE"]
                               + [x for t in range(NP) for x in ([("num", t), ("den", t)]
                                  + [("upd", t, k) for k in kts] + [("nu", t)])]
                               + [x for b in range(NB) for x in ([("int", b)] + [("su", b, k) for k in kts]
                                  + {2: ["sum"], 3: ["var"]}.get(b, []))]
                               + ["tok", ("den", NP), ("nu", NP), ("num", NP), "sumS", "varS"])
                self.V = Steps(sem("m_V"), base=1, names=["sel"]
                               + [x for k in kts for x in (("bq", k), ("bk", k), ("bv", k), ("v", k), ("tv", k))]
                               + ["qz"] + [("ex", t) for t in tiles5] + ["wl0", "wl1", "att", ("kw", 0), "dec0", "dec1"]
                               + [("qh", k) for k in kts]
                               + [x for t in range(NP) for x in (([("qn", t), ("kw", t)] if t else [])
                                  + [("C", t, k) for k in kts] + [("n", t)])]
                               + [("kw", NP)]
                               + [x for b in range(NB) for x in ([("vm", b)] + BESIDE[b] + [("Cs", b, k) for k in kts])]
                               + [("qn", NP), "nd", ("n", NP), "dmaxS", "rdenS", "hdS", "xcS"]
                               + [("lnS", k) for k in kts] + [("skS", k) for k in kts] + ["zS", "loS"])
                self.S = Steps(sem("m_S"), base=1, names=[(x, k) for k in kts for x in ("q", "k", "tk")] + ["w", "rE"]
                               + [("num", 0), ("num", 1)] + [("qz", 0), ("qz", 1)]
                               + [("num", t) for t in range(2, NP)] + ["dn"]
                               + [("qz", 2), ("qz", 3), ("qz", 4)] + [("sqr", k) for k in kts]
                               + [("qz", 5), "lnv", "rs", ("qz", 6), ("qz", 7)] + [("hi", k) for k in kts]
                               + ["tok", ("num", NP), "dnS", "sqrS", "lnvS", "rsS", "hiS"])
                self.cin = [sem(f"m_cin{s}") for s in range(3)]
                self.cst = [sem(f"m_cst{s}") for s in range(3)]
                self.zin = sem("m_zin")
                self.cpst = sem("m_cpst")
                self.cp_free = sem("m_cp_free")
                self.uses = [len(range(s, NB, 3)) for s in range(3)]

            def slot(self, b):
                return b % 3, b // 3

            def evac_x(self, a, i, s):
                g = G_UP1 + s
                a.wait_ge(pe_unit, U_UP1 + 2 * i + s + 1)
                dst = xp[:, bass.ds(2 * i + s, 1), :].rearrange("p a c -> p (a c)")
                a.activation(dst[:, NCONV - 1:NCONV - 1 + SEQ], pD[g % 2][:, 0:SEQ], ACT.Copy)
                a.activation(streams(dst, NCONV - 1, TS), pD[g % 2][:, SEQ:T].rearrange("p (b c) -> p b c", c=TS),
                             ACT.Copy).then_inc(evac[g % 2], 1)

            def silu_x(self, a, ft, s):
                a.wait_ge(self.conv, 4 * ft + 4)
                a.activation(xc[:, bass.ds(ft, 1), :].rearrange("p a c -> p (a c)"), cv[s][:], ACT.Silu)\
                    .then_inc(self.xc, 1)

            def conv_tile(self, v, ft, s, later):
                g = G_UP1 + s
                if later:
                    v.wait_ge(self.xc, ft - 1)
                v.wait_ge(evac[g % 2], g // 2 + (ft - s) // 2 + 1 if isinstance(ft, int) else g // 2 + self.i + 1)
                src = xp[:, bass.ds(ft, 1), :].rearrange("p a c -> p (a c)")
                out = (cv[s][:, 0:SEQ], cv[s][:, SEQ:T].rearrange("p (b c) -> p b c", c=TS))
                for tap in range(NCONV):
                    w = par[:, bass.ds(PAR["convw"] + CI * tap + ft, 1)]
                    part = (src[:, tap:tap + SEQ], streams(src, tap, TS))
                    if tap:
                        v.wait_ge(self.conv, 4 * ft + tap)
                    for n in range(2):
                        if tap == 0:
                            ins = v.tensor_scalar(out[n], part[n], w, par[:, bass.ds(PAR["convb"] + ft, 1)],
                                                  ALU.mult, ALU.add)
                        else:
                            ins = v.scalar_tensor_tensor(out[n], part[n], w, out[n], ALU.mult, ALU.add)
                    ins.then_inc(self.conv, 1)

            def act(self, a):
                a.wait_ge(norm2.lo_done, KD)
                a.dma_start(io["x_kept"], xT[:]).then_inc(kept, 16)
                a.wait_ge(a_out, 32 * H)
                a.dma_start(cst[:], io["conv"]).then_inc(self.w_in, 16)
                a.dma_start(wqkv[:], io["wqkv"]).then_inc(self.w_in, 16)
                a.dma_start(wgx[:], io["wgx"]).then_inc(self.w_in, 16)
                a.dma_start(gsm[:], io["gsm"]).then_inc(self.w_in, 16)
                a.dma_start(nS[:], io["st_n"]).then_inc(self.w_in, 16)
                for s in range(2):
                    self.evac_x(a, 0, s)
                    if s:
                        self.silu_x(a, 0, 0)
                with a.Fori(1, CI // 2) as i:
                    for s in range(2):
                        self.evac_x(a, i, s)
                        self.silu_x(a, 2 * i + s - 1, (s + 1) % 2)
                self.silu_x(a, CI - 1, 1)

                def gate_tile(i, s):
                    g = G_UP1 + CI + s
                    a.wait_ge(pe_unit, U_UP1 + CI + 2 * i + s + 1)
                    if not isinstance(i, int):
                        a.wait_ge(self.zst[s], 16 * i)
                    a.activation(two(zb[s][:]), psd[g % 2][:, :, 0:HT], ACT.Silu).then_inc(evac[g % 2], 1)
                    a.wait_ge(evac[g % 2], g // 2 + i + 1)
                    a.dma_start(io["z_kept"][bass.ds(2 * i + s, 1)].rearrange("a p c -> p (a c)"), zb[s][:])\
                        .then_inc(self.zst[s], 16)
                for s in range(2):
                    gate_tile(0, s)
                with a.Fori(1, CI // 2) as i:
                    for s in range(2):
                        gate_tile(i, s)
                P_, V_, S_ = self.gP, self.gV, self.gS
                a.wait_ge(P_.sem, P_.at("gate"))
                a.activation(pre[:], pM[0][0:8, 0:T], ACT.Copy).then_inc(S_.sem, 1)
                a.wait_ge(V_.sem, V_.at("f"))
                a.activation(t1[:], fgr[:], ACT.Abs).then_inc(S_.sem, 1)
                a.wait_ge(S_.sem, S_.at("abs"))
                a.activation(t1[:], t1[:], ACT.Exp, scale=-1.0).then_inc(S_.sem, 1)
                a.wait_ge(S_.sem, S_.at("exp"))
                a.activation(t1[:], t1[:], ACT.Ln, bias=con[0:H, CON["ones"]:CON["ones"] + 1]).then_inc(S_.sem, 1)
                a.wait_ge(V_.sem, V_.at("m"))
                a.activation(rowE[:], mro[:], ACT.Exp, scale=-1.0).then_inc(S_.sem, 1)
                a.wait_ge(V_.sem, V_.at("w2"))
                a.activation(rowW[:], rowW[:], ACT.Exp).then_inc(S_.sem, 1)
                a.wait_ge(P_.sem, P_.at("a"))
                a.activation(acol[:].rearrange("p t h -> p (t h)"), bank[1][:, 0:(NP + 1) * H], ACT.Copy)\
                    .then_inc(S_.sem, 1)
                a.wait_ge(V_.sem, V_.at("cso"))
                for dst, src in (("conv_p", cpo), ("conv_s", cst), ("m_out", mo)):
                    a.dma_start(io[dst], src[:]).then_inc(self.outs, 16)
                a.wait_ge(self.outs, 48)
                for s in range(2):
                    a.wait_ge(self.zst[s], 16 * CI // 2)
                a.sem_inc(self.S.sem, 1)
                with a.Fori(0, H) as h:
                    self.act_head(a, h)
                a.dma_start(io["n_s"], nS[:]).then_inc(self.outs, 16)
                a.dma_start(io["n_p"], nP[:]).then_inc(self.outs, 16)
                a.wait_ge(self.outs, 80)

            def fold(self, v):
                n = [0]

                def link(ins):
                    n[0] += 1
                    ins.then_inc(self.gw, 1)
                    v.wait_ge(self.gw, n[0])
                link(v.tensor_scalar(wqkv[:, 1, :, :], wqkv[:, 1, :, :], float(DH) ** -0.5, None, ALU.mult))
                for dst, xs in ((gC, (0, 1)), (gX, (2,))):
                    for x in xs:
                        for o in range(4):
                            w = wqkv[:, x, :, o:o + 1].broadcast_to([P, CI, 8])
                            first = x == xs[0] and o == 0
                            link(v.tensor_tensor((dst if first else gt)[:], wgx[:, x, :, o, :], w, ALU.mult))
                            if not first:
                                link(v.tensor_tensor(dst[:], dst[:], gt[:], ALU.add))

            def vec(self, v):
                v.wait_ge(self.w_in, 80)
                v.wait_ge(pe_unit, U_UP1)
                v.memset(xp[:, :, 0:NCONV - 1], 0.0)
                v.tensor_copy(xp[:, :, NCONV - 1 + SEQ:XW].rearrange("p f (b c) -> p f b c", c=XS)[:, :, :, 0:NCONV - 1],
                              cst[:]).then_inc(self.pad, 1)
                v.wait_ge(self.pad, 1)
                for s in range(2):
                    self.conv_tile(v, s, s, False)
                with v.Fori(1, CI // 2) as i:
                    self.i = i
                    for s in range(2):
                        self.conv_tile(v, 2 * i + s, s, True)
                self.fold(v)
                P_, V_, S_ = self.gP, self.gV, self.gS
                st = lambda r: r[:, SEQ:T].rearrange("p (b c) -> p b c", c=TS)
                first = lambda r: st(r)[:, :, 0:1]
                m0 = gsm[:, 2:2 + NB].unsqueeze(2)
                v.wait_ge(kept, 16)
                v.wait_ge(P_.sem, P_.at("sel"))
                v.tensor_scalar(fgr[:], pM[0][0:H, 0:T], gsm[:, 1:2], None, ALU.add).then_inc(V_.sem, 1)
                v.tensor_scalar(igr[:], pM[1][0:H, 0:T], gsm[:, 0:1], None, ALU.add).then_inc(V_.sem, 1)
                v.wait_ge(S_.sem, S_.at("ln"))
                v.scalar_tensor_tensor(fgr[:], fgr[:], 0.0, t1[:], ALU.min, ALU.subtract).then_inc(V_.sem, 1)
                v.wait_ge(V_.sem, V_.at("lf"))
                v.tensor_tensor_scan(bro[:], reset[0:H, :], fgr[:], 0.0, ALU.mult, ALU.add).then_inc(V_.sem, 1)
                v.tensor_copy(i2[:], igr[:]).then_inc(V_.sem, 1)
                v.tensor_copy(l2[:], fgr[:]).then_inc(V_.sem, 1)
                v.tensor_tensor(mo[:, 0:NB].unsqueeze(2), first(fgr), m0, ALU.add).then_inc(V_.sem, 1)
                v.wait_ge(V_.sem, V_.at("lm"))
                v.tensor_tensor(first(i2), first(i2), mo[:, 0:NB].unsqueeze(2), ALU.max).then_inc(V_.sem, 1)
                v.memset(first(l2), NEVER).then_inc(V_.sem, 1)
                v.wait_ge(V_.sem, V_.at("lx"))
                v.tensor_tensor_scan(mro[:], l2[:], i2[:], 0.0, ALU.add, ALU.max).then_inc(V_.sem, 1)
                v.wait_ge(V_.sem, V_.at("m"))
                v.tensor_tensor(rowM[:], bro[:], mro[:], ALU.subtract).then_inc(V_.sem, 1)
                v.tensor_tensor(igr[:], igr[:], bro[:], ALU.subtract).then_inc(V_.sem, 1)
                v.wait_ge(V_.sem, V_.at("M"))
                ch = lambda r, t0, n: r[:, t0 * P:(t0 + n) * P].rearrange("p (t c) -> p t c", c=P)
                v.tensor_copy(rowW[:, 0:P], rowM[:, 0:P]).then_inc(V_.sem, 1)
                v.tensor_tensor(ch(rowW, 1, NP - 1), ch(rowM, 1, NP - 1),
                                ch(mro, 0, NP - 1)[:, :, P - 1:P].broadcast_to([H, NP - 1, P]), ALU.add)\
                    .then_inc(V_.sem, 1)
                v.tensor_tensor(st(rowW), st(rowM), m0.broadcast_to([H, NB, TS]), ALU.add).then_inc(V_.sem, 1)
                v.tensor_copy(mo[:, 0:1], mro[:, SEQ - 1:SEQ]).then_inc(V_.sem, 1)
                v.tensor_copy(mo[:, 1:1 + NB].unsqueeze(2), st(mro)[:, :, TS - 1:TS]).then_inc(V_.sem, 1)
                v.tensor_copy(cpo[:], xp[:, :, SEQ:SEQ + NCONV - 1]).then_inc(V_.sem, 1)
                v.tensor_copy(cst[:], xp[:, :, NCONV - 1 + SEQ:XW].rearrange("p f (b c) -> p f b c", c=XS)
                              [:, :, :, TS:XS]).then_inc(V_.sem, 1)
                v.wait_ge(self.outs, 48)
                for s in range(2):
                    v.wait_ge(self.zst[s], 16 * CI // 2)
                v.memset(qz[1][:], 0.0)
                v.sem_inc(self.V.sem, 1)
                with v.Fori(0, H) as h:
                    self.vec_head(v, h)

            def pe(self, pe):
                for j in range(2):
                    pe_dense(pe, (U_UP1 + j, 0), (G_UP1 + j, 0), xh, xl, ready=(norm2.lo_done, 1) if j == 0 else None,
                             cut=SEQ)
                with pe.Fori(1, CI // 2) as i:
                    for j in range(2):
                        pe_dense(pe, (U_UP1 + j, i), (G_UP1 + j, i), xh, xl, cut=SEQ)
                with pe.Fori(CI // 2, CI) as i:
                    for j in range(2):
                        pe_dense(pe, (U_UP1 + j, i), (G_UP1 + j, i), xh, xl)
                P_, V_, S_ = self.gP, self.gV, self.gS
                pe.wait_ge(self.gw, 23)
                pe.wait_ge(self.xc, CI)
                for part in range(2):
                    for ft in range(CI):
                        xs = (xp[:, ft, NCONV - 1:NCONV - 1 + SEQ], streams(xp[:, ft, :], NCONV - 1, TS))
                        cs = (xc[:, ft, 0:SEQ], xc[:, ft, SEQ:T])
                        for w, src in ((gC, cs), (gX, xs)):
                            o = pM[0][0:8, 0:SEQ] if part == 0 else pM[0][0:8, SEQ:T]
                            mm = pe.matmul(o, w[:, ft, :], src[part], start=(ft == 0 and w is gC),
                                           stop=(ft == CI - 1 and w is gX))
                mm.then_inc(P_.sem, 1)
                pe.wait_ge(S_.sem, S_.at("pre"))
                for row, o in ((4, pM[0]), (0, pM[1])):
                    for c0, c1 in ((0, SEQ), (SEQ, T)):
                        mm = pe.matmul(o[0:H, c0:c1], con[0:8, CON["ident"] + row:CON["ident"] + row + 4],
                                       pre[:, c0:c1], start=True, stop=True)
                mm.then_inc(P_.sem, 1)
                pe.wait_ge(V_.sem, V_.at("a"))
                for t in tiles5:
                    mm = pe.transpose(bank[1][:, t * H:(t + 1) * H], igr[:, tt(t)], ident[0:H, 0:H])
                mm.then_inc(P_.sem, 1)
                pe.sem_inc(self.P.sem, 1)
                with pe.Fori(0, H) as h:
                    self.pe_head(pe, h)

            def pe_head(self, pe, h):
                P_, V_, S_ = self.P, self.V, self.S
                cuts = ((0, SEQ), (SEQ, T))
                pe.wait_ge(V_.sem, V_.rounds(h))
                pe.wait_ge(S_.sem, S_.rounds(h))
                pe.wait_ge(self.gS.sem, self.gS.n)
                n = 0
                for k in range(KH):
                    x = xp[:, bass.ds(KH * h + k, 1), :].rearrange("p a c -> p (a c)")
                    c = xc[:, bass.ds(KH * h + k, 1), :].rearrange("p a c -> p (a c)")
                    srcs = {"q": (c[:, 0:SEQ], c[:, SEQ:T]), "k": (c[:, 0:SEQ], c[:, SEQ:T]),
                            "v": (x[:, NCONV - 1:NCONV - 1 + SEQ], streams(x, NCONV - 1, TS))}
                    for j, name in enumerate("qkv"):
                        pe.wait_ge(V_.sem, V_.at(("b" + name, k), h))
                        if n >= 2:
                            before, kb = "qkv"[(n - 2) % 3], (n - 2) // 3
                            who = V_ if before == "v" else S_
                            pe.wait_ge(who.sem, who.at((before, kb), h))
                        for (c0, c1), src in zip(cuts, srcs[name]):
                            mm = pe.matmul(pD[n % 2][:, c0:c1], blk[k % 2][:, j, :], src, start=True, stop=True)
                        mm.then_inc(P_.sem, 1)
                        n += 1
                    pe.wait_ge(S_.sem, S_.at(("k", k), h))
                    for t in tiles5:
                        mm = pe.transpose(pM[0][:, tt(t)], kT[:, k, tt(t)], ident)
                    mm.then_inc(P_.sem, 1)
                    pe.wait_ge(V_.sem, V_.at(("v", k), h))
                    for t in tiles5:
                        mm = pe.transpose(pM[1][:, tt(t)], vtmp[k % 2][:, tt(t)], ident)
                    mm.then_inc(P_.sem, 1)
                pe.wait_ge(S_.sem, S_.at(("tk", KH - 1), h))
                for t in tiles5:
                    for k in range(KH):
                        mm = pe.matmul(pD[0][:, tt(t)], kT[:, k, tt(t)], qT[:, k, tt(t)], start=(k == 0),
                                       stop=(k == KH - 1))
                mm.then_inc(P_.sem, 1)
                pe.wait_ge(V_.sem, V_.at(("tv", KH - 1), h))
                for row, o in ((rowM, pD[1]), (rowW, pM[1]), (rowE, pM[0])):
                    for c0, c1 in cuts:
                        mm = pe.matmul(o[:, c0:c1], selh[:], row[:, c0:c1], start=True, stop=True)
                    mm.then_inc(P_.sem, 1)
                pe.wait_ge(V_.sem, V_.at("att", h))
                pe.wait_ge(S_.sem, S_.at("rE", h))
                for t in range(NP):
                    if t:
                        pe.wait_ge(V_.sem, V_.at(("C", t - 1, KH - 1), h))
                    if t >= 2:
                        pe.wait_ge(S_.sem, S_.at(("num", t - 2), h))
                    for f in range(KH):
                        o = bank[t % 2][:, tt(f)]
                        mm = pe.matmul(o, vtok[:, t, tt(f)], att1[:, tt(t)], start=True, stop=(t == 0))
                        for k in range(KH if t else 0):
                            mm = pe.matmul(o, Cp[:, k, tt(f)], qT[:, k, tt(t)], start=False, stop=(k == KH - 1))
                    mm.then_inc(P_.sem, 1)
                    mm = pe.matmul(pD[1][:, tt(t)], ones, att1[:, tt(t)], start=True, stop=(t == 0))
                    if t:
                        pe.wait_ge(V_.sem, V_.at(("qn", t), h))
                        for k in range(KH):
                            mm = pe.matmul(pD[1][:, tt(t)], ones, vm[0][:, tt(k)], start=False, stop=(k == KH - 1))
                    mm.then_inc(P_.sem, 1)
                    pe.wait_ge(V_.sem, V_.at(("kw", t), h))
                    for k in range(KH):
                        if t:
                            pe.wait_ge(V_.sem, V_.at(("C", t - 1, k), h))
                        elif k == 2:
                            pe.wait_ge(V_.sem, V_.at(("qh", KH - 1), h))
                        pe.matmul(U[k], kw[:, tt(k)], vtok[:, t, :], start=True, stop=True).then_inc(P_.sem, 1)
                    if t:
                        pe.wait_ge(V_.sem, V_.at(("n", t - 1), h))
                    for k in range(KH):
                        mm = pe.matmul(pD[1][:, T + 64 + k:T + 65 + k], kw[:, tt(k)], ones[:, 0:1], start=True,
                                       stop=True)
                    mm.then_inc(P_.sem, 1)
                pe.wait_ge(S_.sem, S_.at(("num", NP - 2), h))
                for b in range(NB):
                    s, n = self.slot(b)
                    pe.wait_ge(S_.sem, S_.at(("qz", b), h))
                    pe.wait_ge(self.cin[s], 16 * (self.uses[s] * h + n + 1))
                    z0 = P - TS - b * TS
                    for k in range(KH):
                        mm = pe.matmul(bank[0], qz[b % 2][:, k * P + z0:k * P + z0 + P], Cs[s][:, k, :],
                                       start=(b == 0 and k == 0), stop=False)
                    mm.then_inc(P_.sem, 1)
                    pe.wait_ge(V_.sem, V_.at(("vm", b), h))
                    for k in range(KH):
                        last = ("Cs", b - 1, k) if b else ("C", NP - 1, k)
                        pe.wait_ge(V_.sem, V_.at(last, h))
                        pe.matmul(U[k], kw[:, tt(k)], vm[b % 2][:], start=True, stop=True).then_inc(P_.sem, 1)
                    if b == 2:
                        pe.wait_ge(S_.sem, S_.at("dn", h))
                        for k in range(KH):
                            pe.wait_ge(V_.sem, V_.at(("hd", k), h))
                            mm = pe.matmul(bank[1], ones, qT[:, k, 0:SEQ], start=(k == 0), stop=(k == KH - 1))
                        mm.then_inc(P_.sem, 1)
                    if b == 3:
                        pe.wait_ge(V_.sem, V_.at(("xc", KH - 1), h))
                        for k in range(KH):
                            pe.wait_ge(S_.sem, S_.at(("sqr", k), h))
                            mm = pe.matmul(bank[1], ones, sq4[:, k, 0:SEQ], start=(k == 0), stop=(k == KH - 1))
                        mm.then_inc(P_.sem, 1)
                pe.matmul(bank[0], att1[:, tt(NP)], vtok[:, NP, :], start=False, stop=True).then_inc(P_.sem, 1)
                pe.wait_ge(V_.sem, V_.at("nd", h))
                pe.matmul(pD[1][:, tt(NP)], ones, att1[:, tt(NP)], start=True, stop=False)
                for k in range(KH):
                    mm = pe.matmul(pD[1][:, tt(NP)], ones, vm[0][:, tt(k)], start=False, stop=(k == KH - 1))
                mm.then_inc(P_.sem, 1)
                pe.wait_ge(V_.sem, V_.at(("Cs", NB - 1, KH - 1), h))
                for k in range(KH):
                    mm = pe.matmul(bank[3][:, k * NB:(k + 1) * NB], kw[:, tt(k)],
                                   con[:, CON["ind"]:CON["ind"] + NB], start=True, stop=True)
                mm.then_inc(P_.sem, 1)
                pe.wait_ge(S_.sem, S_.at("tok", h))
                for f in range(KH):
                    mm = pe.transpose(bank[1][:, tt(f)], vtmp[0][:, tt(f)], ident)
                mm.then_inc(P_.sem, 1)
                pe.wait_ge(V_.sem, V_.at("hdS", h))
                for k in range(KH):
                    mm = pe.matmul(bank[2][:, 0:P], ones, qT[:, k, SEQ:T], start=(k == 0), stop=(k == KH - 1))
                mm.then_inc(P_.sem, 1)
                pe.wait_ge(S_.sem, S_.at("sqrS", h))
                for k in range(KH):
                    mm = pe.matmul(bank[2][:, P:2 * P], ones, sq4[:, k, SEQ:T], start=(k == 0), stop=(k == KH - 1))
                mm.then_inc(P_.sem, 1)

            def vec_head(self, v, h):
                P_, V_, S_ = self.P, self.V, self.S
                v.wait_ge(P_.sem, P_.rounds(h))
                v.wait_ge(S_.sem, S_.rounds(h))
                one = lambda x, i: x[:, bass.ds(i, 1), :].rearrange("p a c -> p (a c)")
                v.tensor_copy(selh[:], con[0:H, bass.ds(CON["sel"] + P * h, P)]).then_inc(V_.sem, 1)

                def blocks(k):
                    if k >= 2:
                        v.wait_ge(P_.sem, P_.at(("v", k - 2), h))
                    for j in range(3):
                        w = wqkv[:, j, bass.ds(KH * h + k, 1), :]
                        v.tensor_tensor(blk[k % 2][:, j, :].rearrange("p (b o) -> p b o", o=4),
                                        con[:, CON["bd"]:CON["bd"] + P].rearrange("p (b o) -> p b o", o=4),
                                        w.broadcast_to([P, P // 4, 4]), ALU.mult).then_inc(V_.sem, 1)
                for k in range(KH):
                    blocks(k)
                    v.wait_ge(P_.sem, P_.at(("v", k), h))
                    if k >= 2:
                        v.wait_ge(P_.sem, P_.at(("tv", k - 2), h))
                    v.tensor_copy(vtmp[k % 2][:], pD[(3 * k + 2) % 2][:, 0:T]).then_inc(V_.sem, 1)
                    v.wait_ge(P_.sem, P_.at(("tv", k), h))
                    v.tensor_copy(vtok[:, :, tt(k)], pM[1][:, 0:T].rearrange("p (t c) -> p t c", c=P))\
                        .then_inc(V_.sem, 1)
                v.memset(qz[0][:], 0.0).then_inc(V_.sem, 1)
                v.wait_ge(P_.sem, P_.at("rM", h))
                for t in tiles5:
                    see = con[:, CON["caus"] + (P if t == NP else 0):][:, 0:P]
                    v.scalar_tensor_tensor(att1[:, tt(t)], pD[1][:, tt(t)],
                                           acol[:, t, bass.ds(h, 1)], see, ALU.add, ALU.min).then_inc(V_.sem, 1)
                v.wait_ge(S_.sem, S_.at("w", h))
                v.tensor_copy(wl[:, 0:NP].unsqueeze(2), seqs(att1, 0, NP, P)[:, :, P - 1:P]).then_inc(V_.sem, 1)
                v.tensor_reduce(wl[:, NP:NP + 1], seqs(att1, SEQ, NB, TS)[:, :, TS - 1], mybir.AxisListType.X, ALU.add)\
                    .then_inc(V_.sem, 1)
                v.wait_ge(V_.sem, V_.at("wl1", h))
                v.tensor_tensor(att1[:], att1[:], pD[0][:, 0:T], ALU.mult).then_inc(V_.sem, 1)
                v.tensor_scalar(kw[:], ktok[:, 0, :], wl[:, 0:1], None, ALU.mult).then_inc(V_.sem, 1)
                v.wait_ge(P_.sem, P_.at("rW", h))
                v.tensor_copy(dec[:, 0:NP].unsqueeze(2),
                              pM[1][:, 0:SEQ].rearrange("p (t c) -> p t c", c=P)[:, :, P - 1:P]).then_inc(V_.sem, 1)
                v.tensor_copy(dec[:, NP:NP + NB].unsqueeze(2),
                              pM[1][:, SEQ:T].rearrange("p (t c) -> p t c", c=TS)[:, :, TS - 1:TS]).then_inc(V_.sem, 1)
                for k in range(KH):
                    v.tensor_tensor(qT[:, k, :], qT[:, k, :], pM[1][:, 0:T], ALU.mult).then_inc(V_.sem, 1)
                v.wait_ge(V_.sem, V_.at(("qh", KH - 1), h))
                nh = one(nP, h)
                vmv = lambda x: x[:].rearrange("p (k c) -> p k c", c=P)
                for t in range(NP):
                    if t:
                        v.wait_ge(V_.sem, V_.at(("n", t - 1), h))
                        v.wait_ge(P_.sem, P_.at(("den", t - 1), h))
                        v.tensor_tensor(vmv(vm[0]), qT[:, :, tt(t)], nh.unsqueeze(2).broadcast_to([P, KH, P]),
                                        ALU.mult).then_inc(V_.sem, 1)
                        v.wait_ge(P_.sem, P_.at(("nu", t - 1), h))
                        v.tensor_scalar(kw[:], ktok[:, t, :], wl[:, t:t + 1], None, ALU.mult).then_inc(V_.sem, 1)
                    if t == 0:
                        v.wait_ge(self.cp_free, h + 1)
                    for k in range(KH):
                        v.wait_ge(P_.sem, P_.at(("upd", t, k), h))
                        if t == 0:
                            v.tensor_copy(Cp[:, k, :], U[k]).then_inc(V_.sem, 1)
                        else:
                            v.scalar_tensor_tensor(Cp[:, k, :], Cp[:, k, :], dec[:, t:t + 1], U[k], ALU.mult,
                                                   ALU.add).then_inc(V_.sem, 1)
                    v.wait_ge(P_.sem, P_.at(("nu", t), h))
                    nu = pD[1][:, T + 64:T + 64 + KH]
                    if t == 0:
                        v.tensor_copy(nh, nu).then_inc(V_.sem, 1)
                    else:
                        v.scalar_tensor_tensor(nh, nh, dec[:, t:t + 1], nu, ALU.mult, ALU.add).then_inc(V_.sem, 1)
                v.tensor_scalar(kw[:], ktok[:, NP, :], wl[:, NP:NP + 1], None, ALU.mult).then_inc(V_.sem, 1)
                for b in range(NB):
                    if b >= 2:
                        v.wait_ge(P_.sem, P_.at(("su", b - 2, KH - 1), h))
                    v.tensor_scalar(vm[b % 2][:], vtok[:, NP, :], con[:, CON["ind"] + b:CON["ind"] + b + 1], None,
                                    ALU.mult).then_inc(V_.sem, 1)
                    for step in BESIDE[b]:
                        self.vec_prompt(v, h, step)
                    for k in range(KH):
                        v.wait_ge(P_.sem, P_.at(("su", b, k), h))
                        C = Cs[self.slot(b)[0]][:, k, :]
                        v.scalar_tensor_tensor(C, C, dec[:, NP + b:NP + b + 1], U[k], ALU.mult, ALU.add)\
                            .then_inc(V_.sem, 1)
                ns = nS[:, bass.ds(h, 1), :, :].rearrange("p a k b -> p (a k) b")
                v.tensor_tensor(vmv(vm[0]).rearrange("p k (b c) -> p k b c", c=TS),
                                qT[:, :, SEQ:T].rearrange("p k (b c) -> p k b c", c=TS),
                                ns.unsqueeze(3).broadcast_to([P, KH, NB, TS]), ALU.mult).then_inc(V_.sem, 1)
                v.wait_ge(V_.sem, V_.at(("qn", NP), h))
                v.tensor_tensor(ns, ns, dec[:, NP:NP + NB].unsqueeze(1).broadcast_to([P, KH, NB]), ALU.mult)\
                    .then_inc(V_.sem, 1)
                v.wait_ge(P_.sem, P_.at(("nu", NP), h))
                v.wait_ge(V_.sem, V_.at("nd", h))
                v.tensor_tensor(ns, ns, bank[3][:, 0:KH * NB].rearrange("p (k b) -> p k b", b=NB), ALU.add)\
                    .then_inc(V_.sem, 1)
                hs, att, rss = qT[:, :, SEQ:T], att1[:, SEQ:T], rs[:, SEQ:T]
                all4 = lambda x: x.unsqueeze(1).broadcast_to([P, KH, P])
                v.wait_ge(S_.sem, S_.at("dnS", h))
                v.tensor_tensor(att, att, em[:, SEQ:T], ALU.max).then_inc(V_.sem, 1)
                v.wait_ge(V_.sem, V_.at("dmaxS", h))
                v.reciprocal(att, att).then_inc(V_.sem, 1)
                v.wait_ge(V_.sem, V_.at("rdenS", h))
                v.tensor_tensor(hs, hs, all4(att), ALU.mult).then_inc(V_.sem, 1)
                v.wait_ge(P_.sem, P_.at("sumS", h))
                v.scalar_tensor_tensor(hs, all4(bank[2][:, 0:P]), -1.0 / DH, hs, ALU.mult, ALU.add).then_inc(V_.sem, 1)
                v.wait_ge(S_.sem, S_.at("rsS", h))
                for k in range(KH):
                    hk = qT[:, k, SEQ:T]
                    v.scalar_tensor_tensor(hk, hk, par[:, PAR["mnorm"] + k:PAR["mnorm"] + k + 1], rss, ALU.mult,
                                           ALU.mult).then_inc(V_.sem, 1)
                for k in range(KH):
                    hk = qT[:, k, SEQ:T]
                    v.wait_ge(V_.sem, V_.at(("lnS", k), h))
                    v.scalar_tensor_tensor(hk, one(xc, KH * h + k)[:, SEQ:T], par[:, bass.ds(PAR["skip"] + KH * h + k, 1)],
                                           hk, ALU.mult, ALU.add).then_inc(V_.sem, 1)
                v.wait_ge(V_.sem, V_.at(("skS", KH - 1), h))
                v.tensor_tensor(hs, hs, zt[:, :, SEQ:T], ALU.mult).then_inc(V_.sem, 1)
                v.wait_ge(S_.sem, S_.at("hiS", h))
                v.tensor_tensor(al[:, bass.ds(KH * h, KH), SEQ:T], hs, ah[:, bass.ds(KH * h, KH), SEQ:T].bitcast(F32),
                                ALU.subtract).then_inc(V_.sem, 1)

            def vec_prompt(self, v, h, step):
                P_, V_, S_ = self.P, self.V, self.S
                name, k = step if isinstance(step, tuple) else (step, None)
                tile = lambda x: x[:, bass.ds(KH * h + k, 1), :].rearrange("p a c -> p (a c)")[:, 0:SEQ]
                att, hk = att1[:, 0:SEQ], None if k is None else qT[:, k, 0:SEQ]
                if name == "dmax":
                    v.wait_ge(S_.sem, S_.at("dn", h))
                    ins = v.tensor_tensor(att, att, em[:, 0:SEQ], ALU.max)
                elif name in ("rden0", "rden1"):
                    v.wait_ge(V_.sem, V_.at("dmax", h))
                    part = att1[:, 0:SEQ // 2] if name == "rden0" else att1[:, SEQ // 2:SEQ]
                    ins = v.reciprocal(part, part)
                elif name == "hd":
                    v.wait_ge(V_.sem, V_.at("rden1", h))
                    ins = v.tensor_tensor(hk, hk, att, ALU.mult)
                elif name == "xc":
                    v.wait_ge(P_.sem, P_.at("sum", h))
                    ins = v.scalar_tensor_tensor(hk, bank[1], -1.0 / DH, hk, ALU.mult, ALU.add)
                elif name == "ln":
                    v.wait_ge(S_.sem, S_.at("rs", h))
                    ins = v.scalar_tensor_tensor(hk, hk, par[:, PAR["mnorm"] + k:PAR["mnorm"] + k + 1], rs[:, 0:SEQ],
                                                 ALU.mult, ALU.mult)
                elif name == "sk":
                    v.wait_ge(V_.sem, V_.at(("ln", k), h))
                    ins = v.scalar_tensor_tensor(hk, tile(xc), par[:, bass.ds(PAR["skip"] + KH * h + k, 1)], hk,
                                                 ALU.mult, ALU.add)
                elif name == "z":
                    v.wait_ge(self.zin, 16 * (h + 1))
                    v.wait_ge(V_.sem, V_.at(("sk", k), h))
                    ins = v.tensor_tensor(hk, hk, zt[:, k, 0:SEQ], ALU.mult)
                else:
                    v.wait_ge(S_.sem, S_.at(("hi", k), h))
                    ins = v.tensor_tensor(tile(al), hk, tile(ah).bitcast(F32), ALU.subtract)
                ins.then_inc(V_.sem, 1)

            def act_head(self, a, h):
                P_, V_, S_ = self.P, self.V, self.S
                a.wait_ge(V_.sem, V_.rounds(h))
                a.wait_ge(P_.sem, P_.rounds(h))
                for k in range(KH):
                    for j, (name, dst) in enumerate((("q", qT), ("k", kT))):
                        a.wait_ge(P_.sem, P_.at((name, k), h))
                        a.activation(dst[:, k, :], pD[(3 * k + j) % 2][:, 0:T], ACT.Copy).then_inc(S_.sem, 1)
                    a.wait_ge(P_.sem, P_.at(("tk", k), h))
                    a.activation(ktok[:, :, tt(k)], pM[0][:, 0:T].rearrange("p (t c) -> p t c", c=P), ACT.Copy)\
                        .then_inc(S_.sem, 1)
                a.wait_ge(V_.sem, V_.at(("ex", NP), h))
                a.activation(att1[:], att1[:], ACT.Exp).then_inc(S_.sem, 1)
                a.wait_ge(P_.sem, P_.at("rE", h))
                a.activation(em[:], pM[0][:, 0:T], ACT.Copy).then_inc(S_.sem, 1)

                def num(t):
                    a.wait_ge(P_.sem, P_.at(("num", t), h))
                    if t < NP:
                        a.wait_ge(P_.sem, P_.at(("den", t), h))
                    a.activation(qT[:, :, tt(t)], bank[min(t, NP - 1) % 2].rearrange("p (k c) -> p k c", c=P), ACT.Copy)\
                        .then_inc(S_.sem, 1)

                def queries(b):
                    if b >= 2:
                        a.wait_ge(P_.sem, P_.at(("int", b - 2), h))
                    q = qz[b % 2][:, P - TS:].rearrange("p (k c) -> p k c", c=P)[:, :, 0:TS]
                    a.activation(q, qT[:, :, SEQ + b * TS:SEQ + (b + 1) * TS], ACT.Copy)\
                        .then_inc(S_.sem, 1)
                a.wait_ge(V_.sem, V_.at(("qh", KH - 1), h))
                for t in range(2):
                    num(t)
                for b in range(2):
                    queries(b)
                for t in range(2, NP):
                    num(t)
                a.activation(att1[:, 0:SEQ], pD[1][:, 0:SEQ], ACT.Abs).then_inc(S_.sem, 1)
                for b in range(2, 5):
                    queries(b)
                for k in range(KH):
                    a.wait_ge(V_.sem, V_.at(("xc", k), h))
                    a.activation(sq4[:, k, 0:SEQ], qT[:, k, 0:SEQ], ACT.Square).then_inc(S_.sem, 1)
                queries(5)
                a.wait_ge(P_.sem, P_.at("var", h))
                a.activation(rs[:, 0:SEQ], bank[1], ACT.Ln, bias=eps, scale=1.0 / DH).then_inc(S_.sem, 1)
                a.wait_ge(S_.sem, S_.at("lnv", h))
                a.activation(rs[:, 0:SEQ], rs[:, 0:SEQ], ACT.Exp, scale=-0.5).then_inc(S_.sem, 1)
                queries(6)
                queries(7)
                for k in range(KH):
                    a.wait_ge(V_.sem, V_.at(("z", k), h))
                    a.activation(ah[:, bass.ds(KH * h + k, 1), 0:SEQ].rearrange("p a c -> p (a c)"), qT[:, k, 0:SEQ],
                                 ACT.Copy).then_inc(S_.sem, 1)
                a.wait_ge(P_.sem, P_.at("tok", h))
                a.activation(vtmp[0][:, 0:DH], bank[0], ACT.Copy).then_inc(S_.sem, 1)
                a.wait_ge(V_.sem, V_.at(("qn", NP), h))
                num(NP)
                a.activation(att1[:, SEQ:T], pD[1][:, SEQ:T], ACT.Abs).then_inc(S_.sem, 1)
                a.wait_ge(V_.sem, V_.at("xcS", h))
                a.activation(sq4[:, :, SEQ:T], qT[:, :, SEQ:T], ACT.Square).then_inc(S_.sem, 1)
                a.wait_ge(P_.sem, P_.at("varS", h))
                a.activation(rs[:, SEQ:T], bank[2][:, P:2 * P], ACT.Ln, bias=eps, scale=1.0 / DH).then_inc(S_.sem, 1)
                a.wait_ge(S_.sem, S_.at("lnvS", h))
                a.activation(rs[:, SEQ:T], rs[:, SEQ:T], ACT.Exp, scale=-0.5).then_inc(S_.sem, 1)
                a.wait_ge(V_.sem, V_.at("zS", h))
                a.activation(ah[:, bass.ds(KH * h, KH), SEQ:T], qT[:, :, SEQ:T], ACT.Copy).then_inc(S_.sem, 1)

            def sp(self, sp):
                P_, V_, S_ = self.P, self.V, self.S
                sp.wait_ge(self.gS.sem, self.gS.n)
                sp.wait_ge(self.gV.sem, self.gV.n)
                sp.sem_inc(self.cp_free, 1)

                def head(h, later):
                    def load(b):
                        s, n = self.slot(b)
                        if later or n:
                            sp.wait_ge(self.cst[s], 16 * (self.uses[s] * h + n))
                        sp.dma_start(Cs[s][:], io["st_c"][bass.ds(h * NB + b, 1)].rearrange("a p k c -> p (a k) c"))\
                            .then_inc(self.cin[s], 16)

                    def store(b):
                        s, n = self.slot(b)
                        sp.wait_ge(V_.sem, V_.at(("Cs", b, KH - 1), h))
                        sp.dma_start(io["c_s"][bass.ds(h * NB + b, 1)].rearrange("a p k c -> p (a k) c"), Cs[s][:])\
                            .then_inc(self.cst[s], 16)
                    for b in range(3):
                        load(b)
                    sp.wait_ge(V_.sem, V_.rounds(h))
                    sp.dma_start(zt[:], io["z_kept"][bass.ds(KH * h, KH)].rearrange("k p c -> p k c"))\
                        .then_inc(self.zin, 16)
                    sp.wait_ge(V_.sem, V_.at(("C", NP - 1, KH - 1), h))
                    sp.dma_start(io["c_p"][bass.ds(h, 1)].rearrange("a p k c -> p (a k) c"), Cp[:])\
                        .then_inc(self.cpst, 16)
                    for b in range(NB):
                        store(b)
                        if b >= 1 and b + 2 < NB:
                            load(b + 2)
                    sp.wait_ge(self.cpst, 16 * (h + 1))
                    sp.sem_inc(self.cp_free, 1)
                sp.wait_ge(w_split, U_DN1)
                sp.wait_ge(pe_unit, U_DN1)
                head(0, False)
                with sp.Fori(1, H) as h:
                    head(h, True)
                for s in range(3):
                    sp.wait_ge(self.cst[s], 16 * self.uses[s] * H)
                sp.wait_ge(self.zin, 16 * H)
                sp.wait_ge(P_.sem, P_.at(("nu", NP), H - 1))
                sp.dma_start(xT[:], io["x_kept"]).then_inc(kept, 16)

        sq4 = kT
        mlstm = MLstm()
        def vec_residual(v, units, g0, norm=None):
            if norm is not None:
                norm.begin(v)
            with v.Fori(0, KD // 2) as i:
                for s in range(2):
                    v.wait_ge(pe_unit, units[0] + units[1] * (2 * i + s + 1))
                    x = xT[:, bass.ds(2 * i + s, 1), :].rearrange("p a (c d) -> p (a c) d", c=2)
                    v.tensor_tensor(x, x, psd[(g0 + s) % 2][:, :, 0:HT], ALU.add).then_inc(evac[(g0 + s) % 2], 1)
                    if norm is not None:
                        norm.add(v, 2 * i + s, s)

        def pe_down(pe, u0, g0, nu, nk, ready, ready_at):
            for j in range(2):
                for q in range(nu):
                    pe_dense(pe, (u0 + nu * j + q, 0), (g0 + j, 0), ah, al, k0=q * KD, nk=nk, first=q == 0,
                             last=q == nu - 1, ready=(ready, ready_at + q * KD) if j == 0 and ready is not None else None)
            with pe.Fori(1, KD // 2) as i:
                for j in range(2):
                    for q in range(nu):
                        pe_dense(pe, (u0 + nu * j + q, nu * i), (g0 + j, i), ah, al, k0=q * KD, nk=nk, first=q == 0,
                                 last=q == nu - 1)

        class FeedForward:

            def __init__(self, name, u, g, norm, after):
                self.after = after
                self.hi, self.lo = sem(f"{name}_hi"), sem(f"{name}_lo")
                self.u, self.g, self.norm = u, g, norm

            def parts(self):
                u, g, before = self.u, self.g, 0
                for f in FF_PARTS:
                    nu = -(-f // KD)
                    yield f, before, u, g, nu
                    u, g, before = u + 2 * f + KD * nu, g + 2 * f + KD, before + f

            def act(self, a):
                for f, before, u, g, nu in self.parts():
                    with a.Fori(0, f // 2) as i:
                        for s in range(2):
                            gg = g + 2 * s
                            a.wait_ge(pe_unit, u + 4 * i + 2 * s + 1)
                            a.activation(two(ffs[s][:]), psd[gg % 2][:, :, 0:HT], ACT.Silu).then_inc(evac[gg % 2], 1)
                            a.wait_ge(evac[(gg + 1) % 2], (gg + 1) // 2 + 2 * i + 1)
                            if s == 0:
                                a.wait_ge(pe_unit, u)
                            a.activation(ah[:, bass.ds(2 * i + s, 1), :].rearrange("p a c -> p (a c)"), fft[s][:],
                                         ACT.Copy).then_inc(self.hi, 1)

            def vec(self, v):
                for f, before, u, g, nu in self.parts():
                    with v.Fori(0, f // 2) as i:
                        for s in range(2):
                            gg = g + 2 * s
                            v.wait_ge(evac[gg % 2], gg // 2 + 2 * i + 1)
                            v.wait_ge(pe_unit, u + 4 * i + 2 * s + 2)
                            v.tensor_tensor(two(fft[s][:]), two(ffs[s][:]), psd[(gg + 1) % 2][:, :, 0:HT],
                                            ALU.mult).then_inc(evac[(gg + 1) % 2], 1)
                            v.wait_ge(self.hi, before + 2 * i + s + 1)
                            one = lambda x: x[:, bass.ds(2 * i + s, 1), :].rearrange("p a c -> p (a c)")
                            v.tensor_tensor(one(al), fft[s][:], one(ah).bitcast(F32), ALU.subtract)\
                                .then_inc(self.lo, 1)
                    vec_residual(v, (u + 2 * f, nu), g + 2 * f, self.after if before else None)

            def pe(self, pe):
                for f, before, u, g, nu in self.parts():
                    for j in range(4):
                        pe_dense(pe, (u + j, 0), (g + j, 0), xh, xl,
                                 ready=(self.norm.lo_done, 1) if before == 0 and j == 0 else None)
                    with pe.Fori(1, f // 2) as i:
                        for j in range(4):
                            pe_dense(pe, (u + j, 2 * i), (g + j, 2 * i), xh, xl)
                    pe_down(pe, u + 2 * f, g + 2 * f, nu, min(f, KD), self.lo, before + 1)

        ffn0 = FeedForward("ff0", U_FF0, G_FF0, norm1, norm2)
        ffn1 = FeedForward("ff1", U_FF1, G_FF1, norm3, normf)

        block = ctx.enter_context(nc.Block())

        @block.sync
        def _(sp):
            def x_part(n):
                sp.dma_start(xT[:, 2 * n:2 * n + 2, :], io["x"][:, 2 * n:2 * n + 2, :]).then_inc(x_in[n], 16)
            x_part(0)
            sp.dma_start(par[:], io["par"]).then_inc(con_in, 16)
            sp.dma_start(con[:], io["con"]).then_inc(con_in, 16)
            for n in range(1, KD // 2):
                x_part(n)
            for s in range(2):
                sp.dma_start(wraw[s][:], io["w"][s]).then_inc(w_loaded[s], 16)
            def stream(u0, u1):
                with sp.Fori(u0 // 2, u1 // 2) as i:
                    for s in range(2):
                        sp.wait_ge(w_split, 2 * i + s - 1)
                        sp.dma_start(wraw[s][:], io["w"][bass.ds(2 * i + s, 1)].rearrange("a p k c -> p (a k) c"))\
                            .then_inc(w_loaded[s], 16)
            stream(2, U_FF0 + FF_UNITS)
            stream(U_UP1, U_DN1)
            mlstm.sp(sp)
            stream(U_DN1, N_UNITS)
            for k in range(KD):
                sp.wait_ge(normf.v_done, k + 1)
                sp.dma_start(io["yT"][:, k, :], ntmp[k % 2][:]).then_inc(y_stored[k % 2], 16)
            for s in range(2):
                sp.wait_ge(y_stored[s], 16 * KD // 2)

        @block.gpsimd
        def _(pool):
            def split(n, s, i, later):
                pool.wait_ge(w_loaded[s], 16 * i + 16)
                if later:
                    pool.wait_ge(pe_unit, n - 1)
                pool.sem_inc(w_taken, 1)
                pool.tensor_copy(whi[s][:], wraw[s][:]).then_inc(w_high, 1)
                pool.wait_ge(w_high, n + 1)
                pool.tensor_tensor(wlo[s][:], wraw[s][:], whi[s][:].bitcast(F32), ALU.subtract).then_inc(w_split, 1)
            for s in range(2):
                split(s, s, 0, False)
            with pool.Fori(1, U_DN1 // 2) as i:
                for s in range(2):
                    split(2 * i + s, s, i, True)
            pool.wait_ge(mlstm.V.sem, mlstm.V.rounds(H))
            with pool.Fori(U_DN1 // 2, N_UNITS // 2) as i:
                for s in range(2):
                    split(2 * i + s, s, i, True)

        @block.scalar
        def _(a):
            def load_head(h):
                if not (isinstance(h, int) and h == 0):
                    a.wait_ge(a_out, 16 * (2 * h))
                    a.wait_ge(b_out, 16 * (2 * h))
                a.dma_start(asmp[:], io["st_hgrn"][bass.ds(h, 1)].rearrange("a p b v -> p (a b) v")).then_inc(a_in, 16)
                a.dma_start(bsmp[:], io["st_ret"][bass.ds(h, 1)].rearrange("a p b v -> p (a b) v")).then_inc(b_in, 16)
                a.dma_start(dret[:], io["dret"][bass.ds(h, 1)].rearrange("a p b v -> p (a b) v")).then_inc(b_in, 16)
                a.dma_start(win[:], io["win"][bass.ds(h, 1)].rearrange("a p b v -> p (a b) v")).then_inc(b_in, 16)

            def store_a(h):
                a.wait_ge(aV.sem, aV.at("Sa1", h))
                a.dma_start(io["hgrn_p"][bass.ds(h, 1)].rearrange("a p v -> p (a v)"), ast[:]).then_inc(a_out, 16)
                a.dma_start(io["hgrn_s"][bass.ds(h, 1)].rearrange("a p b v -> p (a b) v"), asmp[:]).then_inc(a_out, 16)

            def store_b(h):
                a.wait_ge(bV.sem, bV.at("Sa1", h))
                a.dma_start(io["ret_p"][bass.ds(h, 1)].rearrange("a p v -> p (a v)"), bst[:]).then_inc(b_out, 16)
                a.dma_start(io["ret_s"][bass.ds(h, 1)].rearrange("a p b v -> p (a b) v"), bsmp[:]).then_inc(b_out, 16)

            a.wait_ge(con_in, 16 * 2)
            for r in range(2):
                a.wait_ge(lb_done, 2)
                a.activation(lbt[:, 1 + r, :], lbt[:, 1 + r, :], ACT.Exp).then_inc(lb_act, 1)
            norm0.act(a)
            a.dma_start(vmask[:, 0:NL, :], io["masks"]).then_inc(tab_in, 16)
            a.dma_start(cos[:], io["cos"]).then_inc(tab_in, 16)
            a.dma_start(sin[:], io["sin"]).then_inc(tab_in, 16)

            load_head(0)

            def head(h, prev):
                if prev:
                    a_act_norm(a, h - 1)
                    store_a(h - 1)
                in0_evac(a, h, 0)
                if prev:
                    b_act_turns(a, h - 1)
                in0_evac(a, h, 1)
                in0_evac(a, h, 2)
                a_act_gates(a, h)
                a_act_level(a, h, 0)
                if prev:
                    b_act_norm(a, h - 1)
                    store_b(h - 1)
                in0_evac(a, h, 3)
                a_act_level(a, h, 1)
                if prev:
                    load_head(h)
                in0_evac(a, h, 4)
                a_act_level(a, h, 2)
                a_act_level(a, h, 3)
                in0_evac(a, h, 5)
                a_act_level(a, h, 4)
                a_act_level(a, h, 5)
                in0_evac(a, h, 6)
                a_act_level(a, h, 6)
                a_act_turns(a, h)
                in0_evac(a, h, 7)

            head(0, False)
            with a.Fori(1, H) as h:
                head(h, True)
            a_act_norm(a, H - 1)
            store_a(H - 1)
            b_act_turns(a, H - 1)
            b_act_norm(a, H - 1)
            store_b(H - 1)
            for k in range(8):
                a.wait_ge(aV.sem, aV.at("mixn", H - 1))
                a.wait_ge(bV.sem, bV.at("mixg", H - 1))
                a.wait_ge(pe_unit, U_OUT0)
                a.activation(xh[:, k, :], mix[:, k, :], ACT.Copy).then_inc(mh, 1)
            a.wait_ge(a_out, 32 * H)
            a.wait_ge(b_out, 32 * H)
            norm1.act(a)
            ffn0.act(a)
            norm2.act(a)
            mlstm.act(a)
            norm3.act(a)
            ffn1.act(a)
            normf.act(a)

        @block.vector
        def _(v):
            v.wait_ge(con_in, 16 * 2)
            lg = par[:, PAR["lb"]:PAR["lb"] + 8].rearrange("p (r h) -> p r h", r=2)
            v.tensor_tensor(lbt[:, 0, :], lg[:, 0, :], lg[:, 1, :], ALU.max).then_inc(lb_done, 1)
            v.wait_ge(lb_done, 1)
            v.tensor_tensor(lbt[:, 1:3, :], lg, lbt[:, 0:1, :].broadcast_to([P, 2, H]), ALU.subtract)\
                .then_inc(lb_done, 1)
            v.wait_ge(lb_act, 2)
            v.tensor_tensor(lbt[:, 0, :], lbt[:, 1, :], lbt[:, 2, :], ALU.add).then_inc(lb_done, 1)
            v.wait_ge(lb_done, 3)
            v.reciprocal(lbt[:, 0, :], lbt[:, 0, :]).then_inc(lb_done, 1)
            v.wait_ge(lb_done, 4)
            v.tensor_tensor(lbt[:, 3, :], lbt[:, 1, :], lbt[:, 0, :], ALU.mult).then_inc(lb_done, 1)
            v.wait_ge(lb_done, 5)
            v.tensor_scalar(lbt[:, 4, :], lbt[:, 3, :], -1.0, 1.0, ALU.mult, ALU.add).then_inc(lb_done, 1)
            v.wait_ge(lb_done, 6)
            norm0.vec(v)
            v.wait_ge(tab_in, 16 * 3)
            v.tensor_copy(masks[:], vmask[:, 0:NL, :]).then_inc(lb_done, 1)
            v.wait_ge(lb_done, 7)

            def head(h, prev):
                if prev:
                    a_vec_tail(v, h - 1)
                    b_vec_rot(v, h - 1)
                    b_vec_scores(v, h - 1)
                    b_vec_states(v, h - 1)
                    vec_mask_v(v, h - 1, gb, bV, bS)
                a_vec_gates(v, h)
                a_vec_diff(v, h, 0)
                if prev:
                    b_vec_tail(v, h - 1)
                a_vec_first_level(v, h)
                if prev:
                    b_vec_mix(v, h - 1)
                a_vec_levels(v, h)
                a_vec_states(v, h)

            head(0, False)
            with v.Fori(1, H) as h:
                head(h, True)
            a_vec_tail(v, H - 1)
            b_vec_rot(v, H - 1)
            b_vec_scores(v, H - 1)
            b_vec_states(v, H - 1)
            vec_mask_v(v, H - 1, gb, bV, bS)
            b_vec_tail(v, H - 1)
            b_vec_mix(v, H - 1)
            for k in range(8):
                v.wait_ge(mh, k + 1)
                v.tensor_tensor(xl[:, k, :], mix[:, k, :], xh[:, k, :].bitcast(F32), ALU.subtract).then_inc(ml, 1)
            vec_residual(v, (U_OUT0, 1), G_OUT0, norm1)
            norm1.vec(v)
            ffn0.vec(v)
            norm2.vec(v)
            mlstm.vec(v)
            v.wait_ge(kept, 32)
            vec_residual(v, (U_DN1, 2), G_DN1, norm3)
            norm3.vec(v)
            ffn1.vec(v)
            normf.vec(v)

        @block.tensor
        def _(pe):
            pe.wait_ge(con_in, 16 * 2)
            norm0.pe(pe)

            def head(h, prev):
                def both(*fs):
                    return lambda: [f(pe, h - 1) for f in fs]
                if prev:
                    in0_unit(pe, h, 0, both(a_pe_tail))
                    a_pe_norm(pe, h - 1)
                    b_pe_rot(pe, h - 1)
                    in0_unit(pe, h, 1, both(b_pe_turns))
                    b_pe_turn_k(pe, h - 1)
                    b_pe_scores(pe, h - 1)
                    in0_unit(pe, h, 2, both(b_pe_states))
                    b_pe_tail(pe, h - 1)
                else:
                    in0_unit(pe, h, 0, ready=(norm0.lo_done, 1))
                    in0_unit(pe, h, 1)
                    in0_unit(pe, h, 2)
                in0_unit(pe, h, 3)
                if prev:
                    pe.wait_ge(bV.sem, bV.at("u1", h - 1))
                a_pe_level(pe, h, 0)
                if prev:
                    b_pe_norm(pe, h - 1)
                for j, (l0, l1) in ((4, (1, 2)), (5, (3, 4)), (6, (5, 6))):
                    in0_unit(pe, h, j, lambda: a_pe_level(pe, h, l0))
                    a_pe_level(pe, h, l1)

                def last_half():
                    a_pe_level(pe, h, 7)
                    a_pe_turns(pe, h)
                in0_unit(pe, h, 7, last_half)
                a_pe_head(pe, h)

            head(0, False)
            with pe.Fori(1, H) as h:
                head(h, True)
            for f in (a_pe_tail, a_pe_norm, b_pe_rot, b_pe_turns, b_pe_turn_k, b_pe_scores, b_pe_states, b_pe_tail,
                      b_pe_norm):
                f(pe, H - 1)
            for j in range(2):
                pe_dense(pe, (U_OUT0 + j, 0), (G_OUT0 + j, 0), xh, xl, ready=(ml, 1) if j == 0 else None)
            with pe.Fori(1, 4) as i:
                for s in range(2):
                    pe_dense(pe, (U_OUT0 + s, i), (G_OUT0 + s, i), xh, xl)
            norm1.pe(pe)
            ffn0.pe(pe)
            norm2.pe(pe)
            mlstm.pe(pe)
            pe.wait_ge(mlstm.V.sem, mlstm.V.rounds(H))
            pe_down(pe, U_DN1, G_DN1, 2, 8, None, 0)
            norm3.pe(pe)
            ffn1.pe(pe)
            normf.pe(pe)


def _constants():
    import numpy as np
    f = np.float32
    con = np.zeros((P, N_CON), f)
    con[:, CON["ident"]:CON["ident"] + P] = np.eye(P)
    con[:, CON["ones"]:CON["ones"] + P] = 1
    half = P // 2
    perm = np.zeros((P, P))
    for m in range(half):
        perm[m + half, m] = -1
        perm[m, m + half] = 1
    con[:, CON["perm"]:CON["perm"] + P] = perm
    start = np.zeros(T, bool)
    start[0:SEQ:P] = True
    start[SEQ::TS] = True
    con[:, CON["reset"]:CON["reset"] + T] = ~start
    con[:, CON["ind"]:CON["ind"] + NB] = np.arange(P)[:, None] // TS == np.arange(NB)
    lg = np.log1p(-np.exp2(-5.0 - np.arange(H)))
    i = np.arange(P)
    for h in range(H):
        con[:, CON["tail"] + 2 * h] = np.exp(lg[h] * (P - 1 - i))
        con[:, CON["tail"] + 2 * h + 1] = np.exp(lg[h] * (TS - 1 - i % TS))
        con[:, CON["glast"] + 2 * h] = np.exp(lg[h] * P)
        con[:, CON["glast"] + 2 * h + 1] = np.exp(lg[h] * TS)
    con[:, CON["eps"]] = EPS
    con[:, CON["bd"]:CON["bd"] + P] = i[:, None] // 4 == i // 4
    s, j = i[:, None], i[None, :]
    same = s // TS == j // TS
    con[:, CON["caus"]:CON["caus"] + P] = np.where(s <= j, 0, NEVER)
    con[:, CON["caus"] + P:CON["caus"] + 2 * P] = np.where((s <= j) & same, 0, NEVER)
    for h in range(H):
        con[h, CON["sel"] + h * P:CON["sel"] + (h + 1) * P] = 1
    masks = np.zeros((P, len(LEVELS), P), f)
    for l, m in enumerate(LEVELS):
        masks[:, l] = (s // (2 * m) == j // (2 * m)) & (s // m % 2 == 0) & (j // m % 2 == 1)
    dret = np.zeros((H, P, 2, P), f)
    win = np.zeros((H, P, 2, P), f)
    for h in range(H):
        d = np.exp(lg[h] * np.maximum(j - s, 0)) * (s <= j)
        dret[h, :, 0] = d
        dret[h, :, 1] = d * same
        win[h, :, 0] = np.exp(lg[h] * (i + 1.0))
        win[h, :, 1] = np.exp(lg[h] * (i % TS + 1.0))
    pos = np.concatenate([np.arange(SEQ), np.tile(256 + np.arange(TS), NB)]).astype(f)
    inv = f(10000.0) ** (-(np.arange(half, dtype=f)) / f(half))
    ang = (pos[None, :] * np.tile(inv, 2)[:, None].astype(f)).astype(np.float64)
    return {"con": con, "masks": masks, "dret": dret, "win": win, "cos": np.cos(ang).astype(f),
            "sin": np.sin(ang).astype(f)}


def _arrays(a):
    import numpy as np

    def tiles(w, order=None):
        k, n = w.shape
        u = w.reshape(k // P, P, n // P, P).transpose(2, 1, 0, 3)
        return u if order is None else u[order]

    def down(w):
        u = tiles(w)
        nk = u.shape[2]
        pad = -nk % KD
        u = np.concatenate([u, np.zeros((*u.shape[:2], pad, P), u.dtype)], 2) if pad else u
        nu = u.shape[2] // KD
        return u.reshape(u.shape[0], P, nu, KD, P).transpose(0, 2, 1, 3, 4).reshape(-1, P, KD, P)

    def ffn(l):
        g, u = tiles(a["w_ffn_gate"][l]), tiles(a["w_ffn_up"][l])
        gu = np.stack([g, u], 1)
        out, at = [], 0
        for f in FF_PARTS:
            out.append(gu[at:at + f].reshape(-1, P, KD, P))
            out.append(down(a["w_ffn_down"][l][at * P:(at + f) * P]))
            at += f
        return out

    w = np.concatenate([
        tiles(a["w_in0"][0], [j * H + h for h in range(H) for j in range(8)]),
        tiles(a["w_out0"][0]), *ffn(0), tiles(a["w_up1"][0]), down(a["w_down1"][0]), *ffn(1)])
    assert w.shape[0] == N_UNITS, w.shape
    x = np.concatenate([a["x_prompt"].reshape(SEQ, D), a["x_sample"].reshape(NB * TS, D)])
    cols = lambda v: v.reshape(-1, P).T
    par = np.concatenate([cols(a["norm_mix"][0]), cols(a["norm_mix"][1]), cols(a["norm_ffn"][0]),
                          cols(a["norm_ffn"][1]), cols(a["norm_final"]), cols(a["lb_logits"][0]),
                          cols(a["lb_logits"][1]), cols(a["hgrn_norm"]), cols(a["ret_norm"]),
                          *[cols(a["conv_w"][0, i]) for i in range(4)], cols(a["conv_b"]), cols(a["mlstm_norm"]),
                          cols(a["mlstm_skip"])], 1)
    assert par.shape[1] == N_PAR
    wg = np.concatenate([a["w_ig"][0], a["w_fg"][0]], 1).reshape(3, CI, P // 4, 4, 8)
    wgx = np.repeat(wg[:, :, :, None], 4, 3).reshape(3, CI, P, 4, 8).transpose(2, 0, 1, 3, 4)
    wqkv = np.stack([a[n][0].reshape(CI, P, 4) for n in ("w_q1", "w_k1", "w_v1")]).transpose(2, 0, 1, 3)
    gsm = np.concatenate([a["b_ig"].T, a["b_fg"].T, a["state_mlstm_m"][0].T], 1)
    st_n = a["state_mlstm_n"][0].reshape(NB, H, KH, P).transpose(3, 1, 2, 0)
    st_c = a["state_mlstm_c"][0].transpose(1, 0, 3, 2).reshape(H * NB, KH, P, DH).transpose(0, 2, 1, 3)
    conv = a["state_conv"][0].reshape(NB, NCONV - 1, CI, P).transpose(3, 2, 0, 1)
    more = {"wgx": wgx, "wqkv": wqkv, "gsm": gsm, "st_n": st_n, "st_c": st_c, "conv": conv}
    return more | {"x": x.T.reshape(KD, P, T).transpose(1, 0, 2), "w": w, "par": par,
            "st_hgrn": a["state_hgrn"][0].transpose(1, 2, 0, 3), "st_ret": a["state_ret"][0].transpose(1, 2, 0, 3)}


_OUT = {"yT": (P, KD, T), "hgrn_p": (H, P, P), "hgrn_s": (H, P, NB, P), "ret_p": (H, P, P), "ret_s": (H, P, NB, P),
        "c_p": (H, P, KH, DH), "c_s": (H * NB, P, KH, DH), "n_p": (P, H, KH), "n_s": (P, H, KH, NB),
        "m_out": (H, 1 + NB), "conv_p": (P, CI, NCONV - 1), "conv_s": (P, CI, NB, NCONV - 1)}
_KEPT = {"x_kept": (P, KD, T), "z_kept": (CI, P, T)}


def kernel(**inputs):
    import numpy as np
    import concourse.bacc as bacc
    from concourse.bass_utils import run_bass_kernel_spmd
    a = {k: np.asarray(v) for k, v in inputs.items()}
    arrays = {k: np.ascontiguousarray(v) for k, v in (_arrays(a) | _constants()).items()}
    nc = bacc.Bacc("TRN2", target_bir_lowering=False, num_devices=1)
    io = {n: nc.dram_tensor(n, x.shape, F32, kind="ExternalInput").ap() for n, x in arrays.items()}
    io |= {n: nc.dram_tensor(n, s, F32, kind="ExternalOutput").ap() for n, s in _OUT.items()}
    io |= {n: nc.dram_tensor(n, s, F32, kind="Internal").ap() for n, s in _KEPT.items()}
    trunk(nc, io)
    r = run_bass_kernel_spmd(nc, [arrays], core_ids=[0]).results[0]
    y = r["yT"].transpose(2, 1, 0).reshape(T, D)
    c_s = r["c_s"].reshape(H, NB, P, KH, DH).transpose(1, 0, 4, 3, 2).reshape(1, NB, H, DH, DH)
    return tuple(np.ascontiguousarray(x) for x in (
        y[:SEQ].reshape(1, SEQ, D), y[SEQ:].reshape(NB, TS, D),
        r["hgrn_p"].reshape(1, 1, H, P, P), r["hgrn_s"].transpose(2, 0, 1, 3)[None],
        r["ret_p"].reshape(1, 1, H, P, P), r["ret_s"].transpose(2, 0, 1, 3)[None],
        r["c_p"].transpose(0, 3, 2, 1).reshape(1, 1, H, DH, DH), c_s,
        r["n_p"].transpose(1, 2, 0).reshape(1, 1, H, DH), r["n_s"].transpose(3, 1, 2, 0).reshape(1, NB, H, DH),
        r["m_out"][:, 0].reshape(1, 1, H), r["m_out"][:, 1:].T[None],
        r["conv_p"].transpose(2, 1, 0).reshape(1, 1, NCONV - 1, CI * P),
        r["conv_s"].transpose(2, 3, 1, 0).reshape(1, NB, NCONV - 1, CI * P)))
```

```python
from contextlib import ExitStack

import concourse.bass as bass
from concourse import mybir

F32 = mybir.dt.float32
F32R = mybir.dt.float32r
U8 = mybir.dt.uint8
ACT = mybir.ActivationFunctionType
ALU = mybir.AluOpType

P = 128
D = 1024
SEQ, NB, TS = 512, 8, 16
NP = SEQ // P
T = SEQ + NB * TS
HT = T // 2
KD = D // P
H = 4
FF_PARTS = (16, 6)
CI = 16
KH = 4
DH = KH * P
NCONV = 4
XS = NCONV - 1 + TS
XW = NCONV - 1 + SEQ + NB * XS
EPS = 1e-6
NEVER = -1e30
LEVELS = (1, 2, 4, 8, 16, 32, 64)

U_IN0 = 0
U_OUT0 = U_IN0 + 32
FF_UNITS = sum(2 * f + 8 * (2 if f > 8 else 1) for f in FF_PARTS)
U_FF0 = U_OUT0 + 8
U_UP1 = U_FF0 + FF_UNITS
U_DN1 = U_UP1 + 32
U_FF1 = U_DN1 + 16
N_UNITS = U_FF1 + FF_UNITS

PAR = {}
_at = 0
for _name, _n in (("mix", 16), ("ffn", 16), ("final", 8), ("lb", 8), ("hgrn", 1), ("ret", 1), ("convw", 64),
                  ("convb", 16), ("mnorm", 4), ("skip", 16)):
    PAR[_name] = _at
    _at += _n
N_PAR = _at
CON = {}
_at = 0
for _name, _n in (("ones", 128), ("eps", 1), ("ident", 128), ("perm", 128), ("reset", T), ("ind", 8), ("tail", 8),
                  ("glast", 8), ("bd", 128), ("caus", 256), ("sel", 512)):
    CON[_name] = _at
    _at += _n
N_CON = _at


class Steps:

    def __init__(self, sem, names, base=0):
        self.sem, self.names, self.n, self.base = sem, {x: i + 1 for i, x in enumerate(names)}, len(names), base

    def at(self, name, r=0):
        return r * self.n + self.base + self.names[name]

    def rounds(self, r):
        return r * self.n + self.base


def trunk(nc, io):
    ctx = ExitStack()
    with ctx:
        sem = lambda name: ctx.enter_context(nc.semaphore(name))
        top = [16512]

        def sb(name, shape, dt=F32, at=None):
            n = mybir.dt.size(dt)
            for x in shape[1:]:
                n *= x
            n = (n + 31) // 32 * 32
            if at is None:
                off = top[0]
                top[0] += n
            else:
                off = at[0]
                at[0] += n
            assert top[0] <= 229312, (name, top[0])
            return nc.alloc_sbuf_tensor_at(name, shape, dt, offset=off)

        xT = sb("xT", [P, KD, T])
        at_h = top[0]
        xh = sb("xh", [P, KD, T], F32R)
        xl = sb("xl", [P, KD, T], F32R)
        at_w = top[0]
        wraw = [sb(f"wraw{s}", [P, KD, P]) for s in range(2)]
        whi, wlo = zip(*[(sb(f"whi{s}", [P, KD, P], F32R), sb(f"wlo{s}", [P, KD, P], F32R)) for s in range(2)])
        at_a = top[0]
        ah = sb("ah", [P, CI, T], F32R)
        top[0] = at_a + CI * XW * 4
        al = sb("al", [P, CI, T], F32R)
        par = sb("par", [P, N_PAR])
        con = sb("con", [P, N_CON])
        at_m = top[0]
        masks = sb("masks", [P, len(LEVELS), P], U8)
        eps = con[:, CON["eps"]:CON["eps"] + 1]
        ident = con[:, CON["ident"]:CON["ident"] + P]
        ones = con[:, CON["ones"]:CON["ones"] + P]
        perm = con[:, CON["perm"]:CON["perm"] + P]
        reset = con[:, CON["reset"]:CON["reset"] + T]
        at_r = top[0]

        a0, r0 = [at_a], [at_r]
        zq, zf, zi, zg, zbq, zbk, zbv, zbg = [sb(f"z_{x}", [P, T], at=a0) for x in
                                              ("aq", "af", "ai", "ag", "bq", "bk", "bv", "bg")]
        mix = sb("mix", [P, 8, T], at=a0)
        ga = {x: sb(f"a_{x}", [P, T], at=a0) for x in ("f", "k", "b", "eb", "q", "kh", "att")}
        dlev = [sb(f"dlev{s}", [P, T], at=a0) for s in range(2)]
        qk = [sb(f"qk{s}", [P, T], at=a0) for s in range(2)]
        cos = sb("cos", [P, T], at=a0)
        sin = sb("sin", [P, T], at=a0)
        dret = sb("dret", [P, 2, P], at=a0)
        win = sb("win", [P, 2, P], at=a0)
        bst = sb("bst", [P, P], at=a0)
        ast = sb("ast", [P, P], at=a0)
        mid = [sb(f"mid{t}", [P, P], at=a0) for t in range(NP - 1)]
        lbt = sb("lbt", [P, 5, H], at=a0)
        assert a0[0] <= at_a + 2 * 16 * T * 4, a0[0] - at_a
        gb = {x: sb(f"b_{x}", [P, T], at=r0) for x in ("q", "k", "t", "kt", "vt")}
        ga["kt"] = sb("a_kt", [P, T], at=r0)
        ga["vt"] = sb("a_vt", [P, T], at=r0)
        asmp = sb("asmp", [P, NB, P], at=r0)
        bsmp = sb("bsmp", [P, NB, P], at=r0)
        vmask = sb("vmask", [P, NB, P], at=r0)
        assert r0[0] <= 229312, r0[0]
        n0 = [at_r]
        sq = [sb(f"sq{s}", [P, T], at=n0) for s in range(2)]
        nacc = sb("nacc", [P, T], at=n0)
        rstd = sb("rstd", [P, T], at=n0)
        ntmp = [sb(f"ntmp{s}", [P, T], at=n0) for s in range(4)]
        ffs = [sb(f"ffs{s}", [P, T], at=n0) for s in range(2)]
        fft = [sb(f"fft{s}", [P, T], at=n0) for s in range(2)]

        psd = [ctx.enter_context(nc.psum_tensor(f"psd{s}", [P, 2, 512], F32)) for s in range(2)]
        psm = ctx.enter_context(nc.psum_tensor("psm", [P, 4, 512], F32))

        w_loaded = [sem(f"w_loaded{s}") for s in range(2)]
        w_taken = sem("w_taken")
        w_high = sem("w_high")
        w_split = sem("w_split")
        pe_unit = sem("pe_unit")
        evac = [sem(f"evac{s}") for s in range(2)]
        con_in = sem("con_in")
        x_in = [sem(f"x_in{n}") for n in range(KD // 2)]
        con_all = sem("con_all")
        tab_in = sem("tab_in")

        def halves(t, k):
            return t[:, k, 0:HT], t[:, k, HT:T]

        def two(ap):
            return ap.rearrange("p (a c) -> p a c", a=2)

        def pe_dense(pe, n, g, hi, lo, k0=0, nk=8, first=True, last=True, ready=None, between=None,
                     ks=None, more=False, ready_high=None):
            ks = list(range(nk)) if ks is None else ks
            (nc_, ne), (gc, ge) = n, g
            slot, pair = nc_ % 2, gc % 2
            pe.wait_ge(w_split, nc_ + 2 * ne + 1)
            if first and not (isinstance(ge, int) and gc + 2 * ge < 2):
                pe.wait_ge(evac[pair], gc // 2 + ge)
            for k in ks:
                if ready_high is not None:
                    pe.wait_ge(*ready_high(k))
                elif ready is not None:
                    pe.wait_ge(*ready(k))
                x0, x1 = halves(hi, k0 + k)
                l0, l1 = halves(lo, k0 + k)
                wh, wl = whi[slot][:, k, :], wlo[slot][:, k, :]
                o0, o1 = psd[pair][:, 0, 0:HT], psd[pair][:, 1, 0:HT]
                st, en = first and k == ks[0], last and not more and k == ks[-1]
                pe.matmul(o0, wh, x0, start=st, stop=False)
                pe.matmul(o1, wh, x1, start=st, stop=False)
                if ready_high is not None:
                    pe.wait_ge(*ready(k))
                pe.matmul(o0, wh, l0, start=False, stop=False)
                pe.matmul(o1, wh, l1, start=False, stop=False)
                pe.matmul(o0, wl, x0, start=False, stop=en)
                mm = pe.matmul(o1, wl, x1, start=False, stop=en)
                if k == nk // 2 - 1 and between is not None:
                    between()
            if not more:
                mm.then_inc(pe_unit, 1)

        class Norm:

            def __init__(self, name, gain, g, free_at, x_at, final=False, own_sum=False):
                self.own_sum = own_sum
                self.sq_done = sem(f"{name}_sq")
                self.acc_done = sem(f"{name}_acc")
                self.sum_done = sem(f"{name}_sum")
                self.std_done = sem(f"{name}_std")
                self.v_done = sem(f"{name}_v")
                self.hi_done = sem(f"{name}_hi")
                self.lo_done = [sem(f"{name}_lo{s}") for s in range(2)]
                self.gain, self.g, self.free_at, self.x_at, self.final = gain, g, free_at, x_at, final

            def act(self, a):
                for k in range(KD):
                    a.wait_ge(*self.x_at(k))
                    if k >= 2:
                        a.wait_ge(self.acc_done, k)
                    a.activation(sq[k % 2][:], xT[:, k, :], ACT.Square).then_inc(self.sq_done, 1)
                a.wait_ge(self.sum_done, 1)
                a.activation(two(rstd[:]), psd[self.g % 2][:, :, 0:HT], ACT.Ln, bias=eps,
                             scale=1.0 / D).then_inc(self.std_done, 1)
                a.wait_ge(self.std_done, 1)
                a.activation(rstd[:], rstd[:], ACT.Exp, scale=-0.5).then_inc(self.std_done, 1)
                a.sem_inc(evac[self.g % 2], 1)
                if self.final:
                    return
                a.wait_ge(pe_unit, self.free_at)
                for k in range(KD):
                    a.wait_ge(self.v_done, k + 1)
                    a.activation(xh[:, k, :], ntmp[k % 4][:], ACT.Copy).then_inc(self.hi_done, 1)

            def begin(self, v):
                v.memset(nacc[:], 0.0).then_inc(self.acc_done, 1)

            def add(self, v, k, s):
                if isinstance(k, int) and k == KD - 1:
                    return
                v.wait_ge(self.sq_done, k + 1)
                v.wait_ge(self.acc_done, k + 1)
                v.tensor_tensor(nacc[:], nacc[:], sq[s][:], ALU.add).then_inc(self.acc_done, 1)

            def vec(self, v):
                if self.own_sum:
                    self.begin(v)
                    for k in range(KD):
                        self.add(v, k, k % 2)
                v.wait_ge(self.std_done, 2)
                for k in range(KD + 1):
                    if k < KD:
                        buf = ntmp[k % 2 if self.final else k % 4]
                        if k >= 2 and self.final:
                            v.wait_ge(y_stored[k % 2], 16 * (k // 2))
                        elif k >= 4:
                            v.wait_ge(*self.ready(k - 4))
                        v.scalar_tensor_tensor(buf[:], xT[:, k, :], par[:, self.gain + k:self.gain + k + 1],
                                               rstd[:], ALU.mult, ALU.mult).then_inc(self.v_done, 1)
                    if k % 2 == 1 and not self.final:
                        self.low(v, k - 1)

            def low(self, e, k):
                e.wait_ge(self.hi_done, k + 1)
                e.tensor_tensor(xl[:, k, :], ntmp[k % 4][:], xh[:, k, :].bitcast(F32), ALU.subtract)\
                    .then_inc(self.lo_done[k % 2], 1)

            def pool(self, pool):
                for k in range(1, KD, 2):
                    pool.wait_ge(self.v_done, k + 1)
                    self.low(pool, k)

            def ready_high(self, k):
                return self.hi_done, k + 1

            def ready(self, k):
                return self.lo_done[k % 2], k // 2 + 1

            def pe(self, p):
                o = psd[self.g % 2]
                p.wait_ge(self.acc_done, KD)
                if self.g >= 2:
                    p.wait_ge(evac[self.g % 2], self.g // 2)
                p.matmul(o[:, 0, 0:HT], ones, nacc[:, 0:HT], start=True, stop=False)
                p.matmul(o[:, 1, 0:HT], ones, nacc[:, HT:T], start=True, stop=False)
                p.wait_ge(self.sq_done, KD)
                last = sq[(KD - 1) % 2]
                p.matmul(o[:, 0, 0:HT], ones, last[:, 0:HT], start=False, stop=True)
                p.matmul(o[:, 1, 0:HT], ones, last[:, HT:T], start=False, stop=True).then_inc(self.sum_done, 1)

        G_N0 = 0
        G_IN0 = 1
        G_OUT0 = G_IN0 + 32
        G_N1 = G_OUT0 + 8
        G_FF0 = G_N1 + 1
        N_FF = sum(2 * f + 8 for f in FF_PARTS)
        G_N2 = G_FF0 + N_FF
        G_UP1 = G_N2 + 1
        G_DN1 = G_UP1 + 32
        G_N3 = G_DN1 + 8
        G_FF1 = G_N3 + 1
        G_NF = G_FF1 + N_FF

        def left(g):
            return evac[g % 2], g // 2 + 1
        y_stored = [sem(f"y_stored{s}") for s in range(2)]
        norm0 = Norm("n0", PAR["mix"], G_N0, 0, lambda k: (x_in[k // 2], 16), own_sum=True)
        norm1 = Norm("n1", PAR["ffn"], G_N1, U_FF0, lambda k: left(G_OUT0 + k))
        norm2 = Norm("n2", PAR["mix"] + 8, G_N2, U_UP1, lambda k: left(G_N2 - 8 + k))
        norm3 = Norm("n3", PAR["ffn"] + 8, G_N3, U_FF1, lambda k: left(G_DN1 + k))
        normf = Norm("nf", PAR["final"], G_NF, None, lambda k: left(G_NF - 8 + k), final=True)

        NL = len(LEVELS)
        z_done = Steps(sem("z_done"), ["aq", "af", "ai", "ag", "bq", "bk", "bv", "bg"])
        lv = [("p", l) for l in range(NL + 1)]
        aV = Steps(sem("aV"), ["f", "k", "b", "q", "dk0", "dk1", "kh"]
                   + [x for l in range(NL) for x in ((("d1", l), ("d0", l)))][:2] + [("cp", 0)]
                   + [x for l in range(NL) for x in (
                       [("qk1", l), ("qk0", l)] + ([("d1", l + 1), ("d0", l + 1)] if l + 1 < NL else []) + [("cp", l + 1)])]
                   + ["S0", "S1", "S2", "S3", "vm", "Sd", "Sa0", "Sa1", "u0", "u1", "mixg", "mixn"])
        aS = Steps(sem("aS"), ["ln", "eb", "ek"] + [("g", l) for l in range(NL)] + ["vt", "kt", "sq", "lnr", "r"])
        aP = Steps(sem("aP"), [("p", l) for l in range(NL + 1)] + ["vt", "kt", "st", "o", "s0", "s1", "oS", "n"])
        bV = Steps(sem("bV"), ["tq", "sq", "q", "tk", "sk", "k", "d0", "d1", "qh0", "qh1",
                   "S0", "S1", "S2", "S3", "vm", "Sa0", "Sa1", "u0", "u1", "mixn", "mixg"])
        bS = Steps(sem("bS"), ["vt", "kt0", "kt1", "sq", "lnr", "r"])
        bP = Steps(sem("bP"), ["pq", "pk", "vt", "kt", "att", "st", "o", "s0", "s1", "oS", "n"])
        a_in = sem("a_in")
        b_in = sem("b_in")
        a_out = sem("a_out")
        b_out = sem("b_out")
        lb_done = sem("lb_done")
        lb_act = sem("lb_act")
        cp_turn = sem("cp_turn")

        bank = [psm[:, i, :] for i in range(4)]

        def tt(i):
            return slice(i * P, (i + 1) * P)

        def a_pe_level(pe, h, l):
            if l == 0:
                pe.wait_ge(aV.sem, aV.at("k", h))
            else:
                pe.wait_ge(aV.sem, aV.at(("qk0", l - 1), h))
            b0, b1 = bank[2 * (l % 2)], bank[2 * (l % 2) + 1]
            if l == 1 and not (isinstance(h, int) and h == 0):
                pe.wait_ge(bS.sem, bS.at("lnr", h - 1))
            if l >= 2:
                pe.wait_ge(aV.sem, aV.at(("cp", l - 2), h))
            tiles = NP + (l == 0 or LEVELS[l - 1] < TS)
            for t in range(tiles):
                lhs = ga["k"][:, tt(t)] if l == 0 else qk[(l - 1) % 2][:, tt(t)]
                rhs = zq[:, tt(t)] if l == 0 else lhs
                o = b0[:, tt(t)] if t < NP else b1[:, 0:P]
                mm = pe.matmul(o, lhs, rhs, start=True, stop=True)
            mm.then_inc(aP.sem, 1)

        def pe_turn(pe, src, b0, b1, done):
            for t in range(NP + 1):
                o = b0[:, tt(t)] if t < NP else b1[:, 0:P]
                mm = pe.transpose(o, src[:, tt(t)], ident)
            mm.then_inc(done, 1)

        def pe_states(pe, h, g, PS, VS, kt_at, SS, att, q):
            pe.wait_ge(SS.sem, SS.at(kt_at, h))
            for t in range(NP):
                mm = pe.matmul(bank[2 + t % 2][:, tt(t // 2)], g["kt"][:, tt(t)], g["vt"][:, tt(t)], start=True,
                               stop=True)
            mm.then_inc(PS.sem, 1)
            for t in range(NP):
                pe.matmul(bank[0][:, tt(t)], g["vt"][:, tt(t)], att[:, tt(t)], start=(t == 0), stop=False,
                          skip_group_check=True)
            for t in range(1, NP):
                pe.wait_ge(VS.sem, VS.at(f"S{t - 1}", h))
                mm = pe.matmul(bank[0][:, tt(t)], mid[t - 1][:], q[:, tt(t)], start=False, stop=(t == NP - 1),
                               skip_group_check=True)
            mm.then_inc(PS.sem, 1)

        def pe_sample(pe, h, g, PS, VS, smp, s_in, att, q):
            pe.wait_ge(s_in, 16 * (h + 1))
            pe.wait_ge(VS.sem, VS.at("vm", h))
            for r in range(2):
                pe.matmul(bank[2 + r], g["kt"][:, tt(NP)], vmask[:, 4 * r:4 * r + 4, :].rearrange("p b v -> p (b v)"),
                          start=True, stop=True).then_inc(PS.sem, 1)
            for b in range(NB):
                c = b * TS
                pe.matmul(bank[1][:, c:c + TS], smp[:, b, :], q[:, SEQ + c:SEQ + c + TS], start=(b == 0), stop=False,
                          skip_group_check=True)
            mm = pe.matmul(bank[1][:, 0:P], g["vt"][:, tt(NP)], att[:, tt(NP)], start=False, stop=True,
                           skip_group_check=True)
            mm.then_inc(PS.sem, 1)

        def pe_headnorm(pe, h, PS, SS, src):
            pe.wait_ge(SS.sem, SS.at("sq", h))
            pe.matmul(bank[2][:, 0:HT], ones, src[:, 0:HT], start=True, stop=True)
            pe.matmul(bank[3][:, 0:HT], ones, src[:, HT:T], start=True, stop=True).then_inc(PS.sem, 1)

        def a_pe_turns(pe, h):
            pe.wait_ge(aV.sem, aV.at(("cp", NL - 1), h))
            pe_turn(pe, zi, bank[0], bank[1], aP.sem)
            pe.wait_ge(aV.sem, aV.at(("cp", NL), h))
            pe_turn(pe, ga["kh"], bank[2], bank[3], aP.sem)

        def a_pe_head(pe, h):
            pe_states(pe, h, ga, aP, aV, "kt", aS, ga["att"], ga["q"])

        def a_pe_tail(pe, h):
            pe.wait_ge(aV.sem, aV.at("S3", h))
            pe_sample(pe, h, ga, aP, aV, asmp, a_in, ga["att"], ga["q"])

        def a_pe_norm(pe, h):
            pe_headnorm(pe, h, aP, aS, ga["kh"])

        def b_pe_rot(pe, h):
            pe.wait_ge(z_done.sem, z_done.at("bk", h))
            pe.matmul(bank[0][:, 0:HT], perm, zbq[:, 0:HT], start=True, stop=True)
            pe.matmul(bank[1][:, 0:HT], perm, zbq[:, HT:T], start=True, stop=True).then_inc(bP.sem, 1)
            pe.wait_ge(aS.sem, aS.at("lnr", h))
            pe.matmul(bank[2][:, 0:HT], perm, zbk[:, 0:HT], start=True, stop=True)
            pe.matmul(bank[3][:, 0:HT], perm, zbk[:, HT:T], start=True, stop=True).then_inc(bP.sem, 1)

        def b_pe_turns(pe, h):
            pe.wait_ge(z_done.sem, z_done.at("bv", h))
            pe.wait_ge(bV.sem, bV.at("sq", h))
            pe_turn(pe, zbv, bank[0], bank[1], bP.sem)

        def b_pe_turn_k(pe, h):
            pe.wait_ge(bV.sem, bV.at("k", h))
            pe_turn(pe, gb["k"], bank[2], bank[3], bP.sem)

        def b_pe_scores(pe, h):
            pe.wait_ge(bS.sem, bS.at("vt", h))
            for t in range(NP + 1):
                o = bank[0][:, tt(t)] if t < NP else bank[1][:, 0:P]
                mm = pe.matmul(o, gb["k"][:, tt(t)], gb["q"][:, tt(t)], start=True, stop=True)
            mm.then_inc(bP.sem, 1)

        def b_pe_states(pe, h):
            pe.wait_ge(bV.sem, bV.at("qh1", h))
            pe_states(pe, h, gb, bP, bV, "kt1", bS, gb["t"], gb["q"])

        def b_pe_tail(pe, h):
            pe.wait_ge(bV.sem, bV.at("S3", h))
            pe_sample(pe, h, gb, bP, bV, bsmp, b_in, gb["t"], gb["q"])

        def b_pe_norm(pe, h):
            pe_headnorm(pe, h, bP, bS, gb["k"])

        def in0_unit(pe, h, j, between=None, **ready):
            pe_dense(pe, (U_IN0 + j, 4 * h), (G_IN0 + j, 4 * h), xh, xl, between=between, **ready)

        def seqs(ap, lo, n, w):
            return ap[:, lo:lo + n * w].rearrange("p (n w) -> p n w", w=w)

        def a_vec_gates(v, h):
            lbh, omh = lbt[:, 3, bass.ds(h, 1)], lbt[:, 4, bass.ds(h, 1)]
            v.wait_ge(z_done.sem, z_done.at("af", h))
            v.tensor_scalar(ga["f"][:], zf[:], omh, lbh, ALU.mult, ALU.add).then_inc(aV.sem, 1)
            v.wait_ge(aV.sem, aV.at("f", h))
            v.tensor_scalar(ga["k"][:], ga["f"][:], -1.0, 1.0, ALU.mult, ALU.add).then_inc(aV.sem, 1)
            v.wait_ge(aS.sem, aS.at("ln", h))
            v.tensor_tensor_scan(ga["b"][:], reset, ga["f"][:], 0.0, ALU.mult, ALU.add).then_inc(aV.sem, 1)
            v.wait_ge(aS.sem, aS.at("eb", h))
            v.tensor_tensor(ga["q"][:], zq[:], ga["eb"][:], ALU.mult).then_inc(aV.sem, 1)
            for lo, n, w in ((0, NP, P), (SEQ, NB, TS)):
                b = seqs(ga["b"], lo, n, w)
                v.tensor_tensor(seqs(ga["kh"], lo, n, w), b[:, :, w - 1:w].broadcast_to([P, n, w]), b,
                                ALU.subtract).then_inc(aV.sem, 1)
            v.wait_ge(aS.sem, aS.at("ek", h))
            v.tensor_tensor(ga["kh"][:], ga["k"][:], ga["kh"][:], ALU.mult).then_inc(aV.sem, 1)

        def width(l):
            return T if LEVELS[l] < TS else SEQ

        def a_vec_diff(v, h, l):
            m = LEVELS[l]
            n = width(l) // (2 * m)
            b = ga["b"][:, 0:width(l)].rearrange("p (n s m) -> p n s m", s=2, m=m)
            d = dlev[l % 2][:, 0:width(l)].rearrange("p (n s m) -> p n s m", s=2, m=m)
            mid = b[:, :, 0, m - 1:m].broadcast_to([P, n, m])
            if l == 0:
                v.wait_ge(aV.sem, aV.at("b", h))
            v.tensor_tensor(d[:, :, 1, :], b[:, :, 1, :], mid, ALU.subtract).then_inc(aV.sem, 1)
            v.tensor_tensor(d[:, :, 0, :], mid, b[:, :, 0, :], ALU.subtract).then_inc(aV.sem, 1)

        def a_vec_qk(v, h, l):
            m = LEVELS[l]
            four = lambda x: x[:, 0:width(l)].rearrange("p (n s m) -> p n s m", s=2, m=m)
            g, o = four(dlev[l % 2]), four(qk[l % 2])
            v.wait_ge(aS.sem, aS.at(("g", l), h))
            if l >= 2:
                v.wait_ge(aP.sem, aP.at(("p", l - 1), h))
            v.tensor_tensor(o[:, :, 1, :], four(zq)[:, :, 1, :], g[:, :, 1, :], ALU.mult).then_inc(aV.sem, 1)
            v.tensor_tensor(o[:, :, 0, :], four(ga["k"])[:, :, 0, :], g[:, :, 0, :], ALU.mult).then_inc(aV.sem, 1)

        def a_vec_take(v, h, l):
            b0, b1 = 2 * (l % 2), 2 * (l % 2) + 1
            att = ga["att"]
            v.wait_ge(aP.sem, aP.at(("p", l), h))
            if l == 0:
                v.tensor_tensor(seqs(att, 0, NP, P), bank[b0].rearrange("p (n w) -> p n w", w=P),
                                ident.unsqueeze(1).broadcast_to([P, NP, P]), ALU.mult)
                v.tensor_tensor(att[:, SEQ:T], bank[b1][:, 0:P], ident, ALU.mult).then_inc(aV.sem, 1)
                return
            mk = masks[:, l - 1, :]
            v.wait_ge(aV.sem, aV.at(("cp", l - 1), h))
            v.sem_inc(cp_turn, 1)
            if LEVELS[l - 1] < TS:
                v.copy_predicated(att[:, SEQ:T], mk, bank[b1][:, 0:P])
            v.copy_predicated(seqs(att, 0, NP, P), mk.unsqueeze(1).broadcast_to([P, NP, P]),
                              bank[b0].rearrange("p (n w) -> p n w", w=P)).then_inc(aV.sem, 1)

        def a_vec_first_level(v, h):
            a_vec_take(v, h, 0)
            a_vec_qk(v, h, 0)
            a_vec_diff(v, h, 1)

        def a_vec_levels(v, h):
            a_vec_take(v, h, 1)
            for l in range(1, NL):
                a_vec_qk(v, h, l)
                if l + 1 < NL:
                    a_vec_diff(v, h, l + 1)
                a_vec_take(v, h, l + 1)

        def vec_prompt_states(v, h, PS, VS, S, out, decay):
            v.wait_ge(PS.sem, PS.at("st", h))
            for t in range(NP):
                src = bank[2 + t % 2][:, tt(t // 2)]
                if t == 0:
                    v.tensor_copy(mid[0][:], src).then_inc(VS.sem, 1)
                    continue
                v.wait_ge(VS.sem, VS.at(f"S{t - 1}", h))
                if t == NP - 1 and (not isinstance(h, int) or h):
                    v.wait_ge(out, 16 * (2 * h))
                dst = mid[t] if t < NP - 1 else S
                v.scalar_tensor_tensor(dst[:], mid[t - 1][:], decay(t), src, ALU.mult, ALU.add).then_inc(VS.sem, 1)

        def vec_mask_v(v, h, g, VS, SS):
            ind = con[:, CON["ind"]:CON["ind"] + NB]
            v.wait_ge(SS.sem, SS.at("vt", h))
            v.tensor_tensor(vmask[:], g["vt"][:, tt(NP)].unsqueeze(1).broadcast_to([P, NB, P]),
                            ind.unsqueeze(2).broadcast_to([P, NB, P]), ALU.mult).then_inc(VS.sem, 1)

        def a_vec_states(v, h):
            vec_prompt_states(v, h, aP, aV, ast, a_out, lambda t: ga["eb"][:, t * P + P - 1:t * P + P])

        def a_vec_tail(v, h, beside=None):
            vec_mask_v(v, h, ga, aV, aS)
            if beside is not None:
                beside()
            v.wait_ge(aP.sem, aP.at("oS", h))
            dec = seqs(ga["eb"], SEQ, NB, TS)[:, :, TS - 1:TS].broadcast_to([P, NB, P])
            v.tensor_tensor(asmp[:], asmp[:], dec, ALU.mult).then_inc(aV.sem, 1)
            v.wait_ge(aV.sem, aV.at("Sd", h))
            for r in range(2):
                s = asmp[:, 4 * r:4 * r + 4, :].rearrange("p b v -> p (b v)")
                v.tensor_tensor(s, s, bank[2 + r], ALU.add).then_inc(aV.sem, 1)
            v.wait_ge(z_done.sem, z_done.at("ag", h))
            v.tensor_tensor(ga["att"][:, 0:SEQ], bank[0], zg[:, 0:SEQ], ALU.mult).then_inc(aV.sem, 1)
            v.tensor_tensor(ga["att"][:, SEQ:T], bank[1][:, 0:P], zg[:, SEQ:T], ALU.mult).then_inc(aV.sem, 1)
            v.wait_ge(aV.sem, aV.at("u1", h))
            v.tensor_scalar(mix[:, bass.ds(h, 1), :].rearrange("p a c -> p (a c)"), ga["att"][:],
                            par[:, PAR["hgrn"]:PAR["hgrn"] + 1], None, ALU.mult).then_inc(aV.sem, 1)
            v.wait_ge(aS.sem, aS.at("r", h))
            v.wait_ge(aV.sem, aV.at("mixg", h))
            m = mix[:, bass.ds(h, 1), :].rearrange("p a c -> p (a c)")
            v.tensor_tensor(m, m, ga["kh"][:], ALU.mult).then_inc(aV.sem, 1)

        def b_vec_rot(v, h):
            for z, o, b0, st in ((zbq, gb["q"], 0, ("tq", "sq", "pq")), (zbk, gb["k"], 2, ("tk", "sk", "pk"))):
                if b0 == 0:
                    v.wait_ge(z_done.sem, z_done.at("bk", h))
                v.tensor_tensor(o[:], z[:], cos[:], ALU.mult).then_inc(bV.sem, 1)
                v.wait_ge(bP.sem, bP.at(st[2], h))
                v.tensor_tensor(two(gb["t"][:]), psm[:, b0:b0 + 2, 0:HT], two(sin[:]), ALU.mult).then_inc(bV.sem, 1)
                v.wait_ge(bV.sem, bV.at(st[1], h))
                v.tensor_tensor(o[:], o[:], gb["t"][:], ALU.add).then_inc(bV.sem, 1)
                v.wait_ge(bV.sem, bV.at("q" if b0 == 0 else "k", h))

        def b_vec_scores(v, h):
            v.wait_ge(bP.sem, bP.at("att", h))
            v.wait_ge(b_in, 16 * 3 * (h + 1))
            v.tensor_tensor(seqs(gb["t"], 0, NP, P), bank[0].rearrange("p (n w) -> p n w", w=P),
                            dret[:, 0:1, :].broadcast_to([P, NP, P]), ALU.mult).then_inc(bV.sem, 1)
            v.tensor_tensor(gb["t"][:, SEQ:T], bank[1][:, 0:P], dret[:, 1, :], ALU.mult).then_inc(bV.sem, 1)
            v.tensor_tensor(seqs(gb["q"], 0, NP, P), seqs(gb["q"], 0, NP, P),
                            win[:, 0:1, :].broadcast_to([P, NP, P]), ALU.mult).then_inc(bV.sem, 1)
            v.tensor_tensor(gb["q"][:, SEQ:T], gb["q"][:, SEQ:T], win[:, 1, :], ALU.mult).then_inc(bV.sem, 1)

        def b_vec_states(v, h):
            vec_prompt_states(v, h, bP, bV, bst, b_out,
                              lambda t: con[:, bass.ds(CON["glast"] + 2 * h, 1)])

        def b_vec_tail(v, h):
            v.wait_ge(bP.sem, bP.at("oS", h))
            for r in range(2):
                s = bsmp[:, 4 * r:4 * r + 4, :].rearrange("p b v -> p (b v)")
                v.scalar_tensor_tensor(s, s, con[:, bass.ds(CON["glast"] + 2 * h + 1, 1)], bank[2 + r], ALU.mult,
                                       ALU.add).then_inc(bV.sem, 1)
            v.tensor_copy(gb["t"][:, 0:SEQ], bank[0]).then_inc(bV.sem, 1)
            v.tensor_copy(gb["t"][:, SEQ:T], bank[1][:, 0:P]).then_inc(bV.sem, 1)

        def b_vec_mix(v, h):
            v.wait_ge(bS.sem, bS.at("r", h))
            v.scalar_tensor_tensor(gb["t"][:], gb["t"][:], par[:, PAR["ret"]:PAR["ret"] + 1], gb["k"][:], ALU.mult,
                                   ALU.mult).then_inc(bV.sem, 1)
            v.wait_ge(bV.sem, bV.at("mixn", h))
            v.wait_ge(z_done.sem, z_done.at("bg", h))
            v.tensor_tensor(mix[:, bass.ds(h + 4, 1), :].rearrange("p a c -> p (a c)"), gb["t"][:], zbg[:],
                            ALU.mult).then_inc(bV.sem, 1)

        def in0_evac(a, h, j):
            name = ["aq", "af", "ai", "ag", "bq", "bk", "bv", "bg"][j]
            func = {"af": ACT.Sigmoid, "ag": ACT.Sigmoid, "bg": ACT.Silu}.get(name, ACT.Copy)
            dst = (zq, zf, zi, zg, zbq, zbk, zbv, zbg)[j]
            again = not isinstance(h, int) or h > 0
            if again:
                user = {"aq": (aV, ("qk1", NL - 1)), "af": (aV, "f"), "ai": (aP, "vt"), "ag": (aV, "u1"),
                        "bq": (bV, "k"), "bk": (bV, "k"), "bv": (bP, "vt"), "bg": (bV, "mixg")}[name]
                a.wait_ge(user[0].sem, user[0].at(user[1], h - 1))
                if name == "bk":
                    a.wait_ge(bP.sem, bP.at("pk", h - 1))
                if name == "bq":
                    a.wait_ge(bP.sem, bP.at("pq", h - 1))
                if name == "aq":
                    a.wait_ge(aP.sem, aP.at(("p", 0), h - 1))
            n = U_IN0 + j
            a.wait_ge(pe_unit, n + 8 * h + 1)
            g = G_IN0 + j
            scale = float(P) ** -0.5 if name == "bk" else 1.0
            a.activation(two(dst[:]), psd[g % 2][:, :, 0:HT], func, scale=scale).then_inc(z_done.sem, 1)
            a.wait_ge(z_done.sem, z_done.at(name, h))
            a.sem_inc(evac[g % 2], 1)

        def a_act_gates(a, h):
            a.wait_ge(aV.sem, aV.at("k", h))
            a.activation(ga["f"][:], ga["f"][:], ACT.Ln).then_inc(aS.sem, 1)
            a.wait_ge(aV.sem, aV.at("b", h))
            a.activation(ga["eb"][:], ga["b"][:], ACT.Exp).then_inc(aS.sem, 1)
            a.wait_ge(aV.sem, aV.at("dk1", h))
            a.activation(ga["kh"][:], ga["kh"][:], ACT.Exp).then_inc(aS.sem, 1)

        def a_act_level(a, h, l):
            a.wait_ge(aV.sem, aV.at(("d0", l), h))
            d = dlev[l % 2][:, 0:width(l)]
            a.activation(d, d, ACT.Exp).then_inc(aS.sem, 1)

        def act_turned(a, h, dst, b0, PS, SS, name, scales=(1.0, 1.0), steps=1):
            a.wait_ge(PS.sem, PS.at(name, h))
            i = a.activation(dst[:, 0:SEQ], bank[b0], ACT.Copy, scale=scales[0])
            if steps == 2:
                i.then_inc(SS.sem, 1)
            a.activation(dst[:, SEQ:T], bank[b0 + 1][:, 0:P], ACT.Copy, scale=scales[1]).then_inc(SS.sem, 1)

        def a_act_turns(a, h):
            act_turned(a, h, ga["vt"], 0, aP, aS, "vt")
            act_turned(a, h, ga["kt"], 2, aP, aS, "kt")

        def act_headnorm(a, h, PS, VS, SS, src, buf):
            a.wait_ge(VS.sem, VS.at("u1", h))
            a.activation(buf[:], src[:], ACT.Square).then_inc(SS.sem, 1)
            a.wait_ge(PS.sem, PS.at("n", h))
            a.activation(two(buf[:]), psm[:, 2:4, 0:HT], ACT.Ln, bias=eps, scale=1.0 / P).then_inc(SS.sem, 1)
            a.wait_ge(SS.sem, SS.at("lnr", h))
            a.activation(buf[:], buf[:], ACT.Exp, scale=-0.5).then_inc(SS.sem, 1)

        def a_act_norm(a, h):
            act_headnorm(a, h, aP, aV, aS, ga["att"], ga["kh"])

        def b_act_turns(a, h):
            act_turned(a, h, gb["vt"], 0, bP, bS, "vt")
            tail = lambda i: con[:, bass.ds(CON["tail"] + 2 * h + i, 1)]
            act_turned(a, h, gb["kt"], 2, bP, bS, "kt", (tail(0), tail(1)), 2)

        def b_act_norm(a, h):
            act_headnorm(a, h, bP, bV, bS, gb["t"], gb["k"])

        mh = sem("mh")
        ml = sem("ml")
        MIX_ORDER = [k for k in range(2 * H) if k % H < H - 1] + [H - 1, 2 * H - 1]

        kept = sem("kept")
        x1, h1, r1 = [16512], [at_h], [at_m]
        xp = sb("xp", [P, CI, XW], at=[at_a])
        xc = sb("xc", [P, CI, T], at=[at_a + CI * XW * 4])
        qT, kT = sb("qT", [P, KH, T], at=h1), sb("kT", [P, KH, T], at=h1)
        ktok = sb("ktok", [P, NP + 1, DH], at=h1)
        vtok = sb("vtok", [P, NP + 1, DH], at=h1)
        wqkv = sb("wqkv", [P, 3, CI, 4], at=r1)
        nS = sb("nS", [P, H, KH, NB], at=r1)
        nP = sb("nP", [P, H, KH], at=r1)
        acol = sb("acol", [P, NP + 1, H], at=r1)
        rowM = sb("rowM", [H, T], at=r1)
        rowW = sb("rowW", [H, T], at=r1)
        rowE = sb("rowE", [H, T], at=r1)
        selh = sb("selh", [H, P], at=r1)
        wl = sb("wl", [P, NP + 1], at=r1)
        dec = sb("dec", [P, NP + NB], at=r1)
        gsm = sb("gsm", [H, 2 + NB], at=r1)
        mo = sb("mo", [H, 1 + NB], at=r1)
        r2 = [r1[0]]
        cv = [sb(f"cv{s}", [P, T], at=r2) for s in range(2)]
        zb = [sb(f"zb{s}", [P, T], at=r2) for s in range(2)]
        cst = sb("cst", [P, CI, NB, NCONV - 1], at=r2)
        cpo = sb("cpo", [P, CI, NCONV - 1], at=r2)
        gt = sb("gt", [P, CI, 8], at=r2)
        gC = sb("gC", [P, CI, 8], at=r2)
        gX = sb("gX", [P, CI, 8], at=r2)
        wgx = sb("wgx", [P, 3, CI, 4, 8], at=r2)
        assert r2[0] <= 229312, r2[0]
        pre = sb("pre", [8, T], at=x1)
        fgr, igr, t1, bro, mro, i2, l2 = [sb(f"row_{n}", [H, T], at=x1) for n in
                                          ("f", "i", "t", "b", "m", "i2", "l2")]
        assert x1[0] <= at_h
        r3, x3 = [r1[0]], [16512]
        Cs = [sb(f"Cs{s}", [P, KH, DH], at=x3) for s in range(2)]
        blk = [sb(f"blk{s}", [P, 3, P], at=x3) for s in range(2)]
        w3 = [at_w]
        Cs.append(sb("Cs2", [P, KH, DH], at=w3))
        ztp = sb("ztp", [P, KH, SEQ], at=w3)
        assert w3[0] <= at_w + 4 * KD * P * 4
        zts = sb("zts", [P, KH, T - SEQ], at=w3)
        em = sb("em", [P, T], at=w3)
        rs = sb("rs", [P, T], at=w3)
        assert w3[0] <= at_w + 6 * KD * P * 4
        QZ = (KH + 1) * P - TS
        qz = [sb("qz0", [P, QZ], at=[x3[0] - 3 * P * 4])]
        assert x3[0] - 3 * P * 4 + QZ * 4 <= at_h
        assert x3[0] <= at_h
        Cp = sb("Cp", [P, KH, DH], at=r3)
        att1 = sb("att1", [P, T], at=r3)
        vtmp = [sb(f"vtmp{s}", [P, T], at=r3) for s in range(2)]
        kw = sb("kw", [P, DH], at=r3)
        vm = [sb(f"vm{s}", [P, DH], at=r3) for s in range(2)]
        qz.append(sb("qz1", [P, QZ], at=r3))
        assert r3[0] <= 229312, r3[0]

        flat = lambda p: p.rearrange("p a c -> p (a c)")
        pD = [flat(psd[s][:, :, :]) for s in range(2)]
        pM = [flat(psm[:, 2 * s:2 * s + 2, :]) for s in range(2)]
        U = [psd[0][:, 0, :], psd[0][:, 1, :], bank[2], bank[3]]
        tiles5 = range(NP + 1)

        def streams(ap, c0, w):
            return ap[:, NCONV - 1 + SEQ:XW].rearrange("p (b c) -> p b c", c=XS)[:, :, c0:c0 + w]

        Z_FIRST = 10
        BESIDE = [["dmax", "rden0"], ["rden1", ("hd", 0), ("hd", 1)], [("hd", 2), ("hd", 3)],
                  [("xc", k) for k in range(KH)], [("ln", 0), ("ln", 1), ("ln", 2)],
                  [("ln", 3)] + [("sk", k) for k in range(KH)], [("z", k) for k in range(KH)],
                  [("lo", k) for k in range(KH)]]

        class MLstm:
            def __init__(self):
                self.w_in = sem("m_w_in")
                self.pad = sem("m_pad")
                self.conv = sem("m_conv")
                self.xc = sem("m_xc")
                self.zsil = sem("m_zsil")
                self.zst = [sem(f"m_zst{s}") for s in range(2)]
                self.outs = sem("m_outs")
                self.gw = sem("m_gw")
                self.gP = Steps(sem("m_gP"), ["gate", "sel", "a"])
                self.gS = Steps(sem("m_gS"), ["pre", "abs", "exp", "ln", "E", "W", "a"])
                self.gV = Steps(sem("m_gV"), ["f", "i", "lf", "b", "i2", "l2", "lm", "ix", "lx", "m", "M", "a",
                                              "w0", "w1", "w2", "mo0", "mo1", "cpo", "cso"])
                kts = range(KH)
                self.P = Steps(sem("m_P"), base=1, names=[x for k in kts for x in
                               ([("k", k)] if k else []) + [("v", k), ("tk", k)] + ([("q", k + 1)] if k < KH - 1 else [])]
                               + ["sc", "rM", "rW", "rE"]
                               + [x for t in range(NP) for x in ([("num", t), ("den", t)]
                                  + [("upd", t, k) for k in kts] + [("nu", t)])]
                               + [x for b in range(NB) for x in ([("int", b)] + [("su", b, k) for k in kts]
                                  + {2: ["sum"], 3: ["var"]}.get(b, []))]
                               + ["tok", ("den", NP), ("nu", NP), ("num", NP), "sumS", "varS"])
                self.V = Steps(sem("m_V"), base=1, names=["sel"]
                               + [x for k in kts for x in ([("b" + y, k + 1) for y in "qkv"] if k < KH - 1 else [])
                                  + [("v", k)]]
                               + ["qz"] + [("ex", t) for t in tiles5] + ["wl0", "wl1", "att", ("kw", 0), "dec0", "dec1"]
                               + [("qh", k) for k in kts]
                               + [x for t in range(NP) for x in (([("qn", t), ("qs", t), ("kw", t)] if t else [])
                                  + [("C", t, k) for k in kts] + [("n", t)])]
                               + [("kw", NP)]
                               + [x for b in range(NB) for x in ([("vm", b)] + BESIDE[b] + [("Cs", b, k) for k in kts])]
                               + [("qn", NP), ("qs", NP), "nd", ("n", NP), "dmaxS", "rdenS", "hdS", "xcS"]
                               + [("lnS", k) for k in kts] + [("skS", k) for k in kts] + ["zS", "loS"])
                self.S = Steps(sem("m_S"), base=1, names=[(x, k) for k in kts for x in (("x", "q", "k", "tk") if k else ("tk",))]
                               + ["w", "rE"]
                               + [("num", 0), ("num", 1)] + [("qz", 0), ("qz", 1)]
                               + [("num", t) for t in range(2, NP)] + ["dn"]
                               + [("qz", 2), ("qz", 3), ("qz", 4)] + [("sqr", k) for k in kts]
                               + [("qz", 5), "lnv", "rs", ("qz", 6), ("qz", 7)] + [("hi", k) for k in kts]
                               + ["tok", ("num", NP), "dnS", "sqrS", "lnvS", "rsS", "hiS"])
                self.B = Steps(sem("m_B"), ["q", "k", "v"])
                self.Q = Steps(sem("m_Q"), ["q", "k"])
                self.G = Steps(sem("m_G"), [(x, k) for x in "hs" for k in range(1, KH)])
                self.T = Steps(sem("m_T"), ["k", "q"])
                self.X = Steps(sem("m_X"), ["x"])
                self.cin = [sem(f"m_cin{s}") for s in range(3)]
                self.cst = [sem(f"m_cst{s}") for s in range(3)]
                self.zin = sem("m_zin")
                self.cpst = sem("m_cpst")
                self.cp_free = sem("m_cp_free")
                self.uses = [len(range(s, NB, 3)) for s in range(3)]

            def slot(self, b):
                return b % 3, b // 3

            def evac_x(self, a, i, s):
                g = G_UP1 + s
                a.wait_ge(pe_unit, U_UP1 + 2 * i + s + 1)
                dst = xp[:, bass.ds(2 * i + s, 1), :].rearrange("p a c -> p (a c)")
                src = psd[g % 2]
                a.activation(dst[:, NCONV - 1:NCONV - 1 + HT], src[:, 0, 0:HT], ACT.Copy)
                a.activation(dst[:, NCONV - 1 + HT:NCONV - 1 + SEQ], src[:, 1, 0:SEQ - HT], ACT.Copy)
                a.activation(streams(dst, NCONV - 1, TS), src[:, 1, SEQ - HT:HT].rearrange("p (b c) -> p b c", c=TS),
                             ACT.Copy).then_inc(evac[g % 2], 1)

            def silu_x(self, a, ft, s):
                a.wait_ge(self.conv, 4 * ft + 4)
                a.activation(xc[:, bass.ds(ft, 1), :].rearrange("p a c -> p (a c)"), cv[s][:], ACT.Silu)\
                    .then_inc(self.xc, 1)

            def conv_tile(self, v, ft, s, later):
                g = G_UP1 + s
                if later:
                    v.wait_ge(self.xc, ft - 1)
                v.wait_ge(evac[g % 2], g // 2 + (ft - s) // 2 + 1 if isinstance(ft, int) else g // 2 + self.i + 1)
                src = xp[:, bass.ds(ft, 1), :].rearrange("p a c -> p (a c)")
                out = (cv[s][:, 0:SEQ], cv[s][:, SEQ:T].rearrange("p (b c) -> p b c", c=TS))
                for tap in range(NCONV):
                    w = par[:, bass.ds(PAR["convw"] + CI * tap + ft, 1)]
                    part = (src[:, tap:tap + SEQ], streams(src, tap, TS))
                    if tap:
                        v.wait_ge(self.conv, 4 * ft + tap)
                    for n in range(2):
                        if tap == 0:
                            ins = v.tensor_scalar(out[n], part[n], w, par[:, bass.ds(PAR["convb"] + ft, 1)],
                                                  ALU.mult, ALU.add)
                        else:
                            ins = v.scalar_tensor_tensor(out[n], part[n], w, out[n], ALU.mult, ALU.add)
                    ins.then_inc(self.conv, 1)

            def act(self, a):
                a.wait_ge(norm2.v_done, KD)
                a.dma_start(io["x_kept"], xT[:]).then_inc(kept, 16)
                a.wait_ge(norm2.hi_done, KD)
                for s in range(2):
                    a.wait_ge(norm2.lo_done[s], KD // 2)
                a.wait_ge(a_out, 32 * H)
                a.dma_start(cst[:], io["conv"]).then_inc(self.w_in, 16)
                a.dma_start(wqkv[:], io["wqkv"]).then_inc(self.w_in, 16)
                a.dma_start(wgx[:], io["wgx"]).then_inc(self.w_in, 16)
                a.dma_start(gsm[:], io["gsm"]).then_inc(self.w_in, 16)
                a.dma_start(nS[:], io["st_n"]).then_inc(self.w_in, 16)
                for s in range(2):
                    self.evac_x(a, 0, s)
                    if s:
                        self.silu_x(a, 0, 0)
                with a.Fori(1, CI // 2) as i:
                    for s in range(2):
                        self.evac_x(a, i, s)
                        self.silu_x(a, 2 * i + s - 1, (s + 1) % 2)
                self.silu_x(a, CI - 1, 1)

                def gate_tile(i, s):
                    g = G_UP1 + CI + s
                    a.wait_ge(pe_unit, U_UP1 + CI + 2 * i + s + 1)
                    if not (isinstance(i, int) and i == 0):
                        a.wait_ge(self.zst[s], 16 * i)
                    a.activation(two(zb[s][:]), psd[g % 2][:, :, 0:HT], ACT.Silu).then_inc(evac[g % 2], 1)
                    a.wait_ge(evac[g % 2], g // 2 + i + 1)
                    a.dma_start(io["z_kept"][bass.ds(2 * i + s, 1)].rearrange("a p c -> p (a c)"), zb[s][:])\
                        .then_inc(self.zst[s], 16)
                for s in range(2):
                    gate_tile(0, s)
                with a.Fori(1, Z_FIRST // 2) as i:
                    for s in range(2):
                        gate_tile(i, s)
                P_, V_, S_ = self.gP, self.gV, self.gS
                a.wait_ge(P_.sem, P_.at("gate"))
                a.activation(pre[:], pM[0][0:8, 0:T], ACT.Copy).then_inc(S_.sem, 1)
                a.wait_ge(V_.sem, V_.at("f"))
                a.activation(t1[:], fgr[:], ACT.Abs).then_inc(S_.sem, 1)
                a.wait_ge(S_.sem, S_.at("abs"))
                a.activation(t1[:], t1[:], ACT.Exp, scale=-1.0).then_inc(S_.sem, 1)
                a.wait_ge(S_.sem, S_.at("exp"))
                a.activation(t1[:], t1[:], ACT.Ln, bias=con[0:H, CON["ones"]:CON["ones"] + 1]).then_inc(S_.sem, 1)
                for s in range(2):
                    gate_tile(Z_FIRST // 2, s)
                a.wait_ge(V_.sem, V_.at("m"))
                a.activation(rowE[:], mro[:], ACT.Exp, scale=-1.0).then_inc(S_.sem, 1)
                a.wait_ge(V_.sem, V_.at("w2"))
                a.activation(rowW[:], rowW[:], ACT.Exp).then_inc(S_.sem, 1)
                a.wait_ge(V_.sem, V_.at("cso"))
                for dst, src in (("conv_p", cpo), ("conv_s", cst), ("m_out", mo)):
                    a.dma_start(io[dst], src[:]).then_inc(self.outs, 16)
                for i in range(Z_FIRST // 2 + 1, CI // 2):
                    for s in range(2):
                        gate_tile(i, s)
                a.wait_ge(P_.sem, P_.at("a"))
                a.activation(acol[:].rearrange("p t h -> p (t h)"), bank[1][:, 0:(NP + 1) * H], ACT.Copy)\
                    .then_inc(S_.sem, 1)
                a.sem_inc(self.S.sem, 1)
                self.act_first(a, 0, "k")
                self.act_first(a, 0, "q")
                a.wait_ge(self.outs, 48)
                for s in range(2):
                    a.wait_ge(self.zst[s], 16 * CI // 2)
                self.act_input(a, 0, 0, self.X.sem)
                with a.Fori(0, H - 1) as h:
                    self.act_head(a, h, True)
                self.act_head(a, H - 1, False)
                a.dma_start(io["n_s"], nS[:]).then_inc(self.outs, 16)
                a.dma_start(io["n_p"], nP[:]).then_inc(self.outs, 16)
                a.wait_ge(self.outs, 80)

            def fold(self, v):
                n = [0]

                def link(ins):
                    n[0] += 1
                    ins.then_inc(self.gw, 1)
                    v.wait_ge(self.gw, n[0])
                link(v.tensor_scalar(wqkv[:, 1, :, :], wqkv[:, 1, :, :], float(DH) ** -0.5, None, ALU.mult))
                for dst, xs in ((gC, (0, 1)), (gX, (2,))):
                    for x in xs:
                        for o in range(4):
                            w = wqkv[:, x, :, o:o + 1].broadcast_to([P, CI, 8])
                            first = x == xs[0] and o == 0
                            link(v.tensor_tensor((dst if first else gt)[:], wgx[:, x, :, o, :], w, ALU.mult))
                            if not first:
                                link(v.tensor_tensor(dst[:], dst[:], gt[:], ALU.add))

            def vec(self, v):
                v.wait_ge(self.w_in, 80)
                v.wait_ge(pe_unit, U_UP1)
                v.memset(xp[:, :, 0:NCONV - 1], 0.0)
                v.tensor_copy(xp[:, :, NCONV - 1 + SEQ:XW].rearrange("p f (b c) -> p f b c", c=XS)[:, :, :, 0:NCONV - 1],
                              cst[:]).then_inc(self.pad, 1)
                v.wait_ge(self.pad, 1)
                for s in range(2):
                    self.conv_tile(v, s, s, False)
                with v.Fori(1, CI // 2) as i:
                    self.i = i
                    for s in range(2):
                        self.conv_tile(v, 2 * i + s, s, True)
                self.fold(v)
                P_, V_, S_ = self.gP, self.gV, self.gS
                st = lambda r: r[:, SEQ:T].rearrange("p (b c) -> p b c", c=TS)
                first = lambda r: st(r)[:, :, 0:1]
                m0 = gsm[:, 2:2 + NB].unsqueeze(2)
                v.wait_ge(kept, 16)
                v.wait_ge(P_.sem, P_.at("sel"))
                v.tensor_scalar(fgr[:], pM[0][0:H, 0:T], gsm[:, 1:2], None, ALU.add).then_inc(V_.sem, 1)
                v.tensor_scalar(igr[:], pM[1][0:H, 0:T], gsm[:, 0:1], None, ALU.add).then_inc(V_.sem, 1)
                v.wait_ge(S_.sem, S_.at("ln"))
                v.scalar_tensor_tensor(fgr[:], fgr[:], 0.0, t1[:], ALU.min, ALU.subtract).then_inc(V_.sem, 1)
                v.wait_ge(V_.sem, V_.at("lf"))
                v.tensor_tensor_scan(bro[:], reset[0:H, :], fgr[:], 0.0, ALU.mult, ALU.add).then_inc(V_.sem, 1)
                v.tensor_copy(i2[:], igr[:]).then_inc(V_.sem, 1)
                v.tensor_copy(l2[:], fgr[:]).then_inc(V_.sem, 1)
                v.tensor_tensor(mo[:, 0:NB].unsqueeze(2), first(fgr), m0, ALU.add).then_inc(V_.sem, 1)
                v.wait_ge(V_.sem, V_.at("lm"))
                v.tensor_tensor(first(i2), first(i2), mo[:, 0:NB].unsqueeze(2), ALU.max).then_inc(V_.sem, 1)
                v.memset(first(l2), NEVER).then_inc(V_.sem, 1)
                v.wait_ge(V_.sem, V_.at("lx"))
                v.tensor_tensor_scan(mro[:], l2[:], i2[:], 0.0, ALU.add, ALU.max).then_inc(V_.sem, 1)
                v.wait_ge(V_.sem, V_.at("m"))
                v.tensor_tensor(rowM[:], bro[:], mro[:], ALU.subtract).then_inc(V_.sem, 1)
                v.tensor_tensor(igr[:], igr[:], bro[:], ALU.subtract).then_inc(V_.sem, 1)
                v.wait_ge(V_.sem, V_.at("M"))
                ch = lambda r, t0, n: r[:, t0 * P:(t0 + n) * P].rearrange("p (t c) -> p t c", c=P)
                v.tensor_copy(rowW[:, 0:P], rowM[:, 0:P]).then_inc(V_.sem, 1)
                v.tensor_tensor(ch(rowW, 1, NP - 1), ch(rowM, 1, NP - 1),
                                ch(mro, 0, NP - 1)[:, :, P - 1:P].broadcast_to([H, NP - 1, P]), ALU.add)\
                    .then_inc(V_.sem, 1)
                v.tensor_tensor(st(rowW), st(rowM), m0.broadcast_to([H, NB, TS]), ALU.add).then_inc(V_.sem, 1)
                v.tensor_copy(mo[:, 0:1], mro[:, SEQ - 1:SEQ]).then_inc(V_.sem, 1)
                v.tensor_copy(mo[:, 1:1 + NB].unsqueeze(2), st(mro)[:, :, TS - 1:TS]).then_inc(V_.sem, 1)
                v.tensor_copy(cpo[:], xp[:, :, SEQ:SEQ + NCONV - 1]).then_inc(V_.sem, 1)
                v.tensor_copy(cst[:], xp[:, :, NCONV - 1 + SEQ:XW].rearrange("p f (b c) -> p f b c", c=XS)
                              [:, :, :, TS:XS]).then_inc(V_.sem, 1)
                v.sem_inc(self.V.sem, 1)
                self.blocks(v, 0, 0, self.B.sem)
                v.wait_ge(self.outs, 48)
                for s in range(2):
                    v.wait_ge(self.zst[s], 16 * CI // 2)
                with v.Fori(0, H - 1) as h:
                    self.vec_head(v, h, True)
                self.vec_head(v, H - 1, False)

            def pe(self, pe):
                for j in range(2):
                    pe_dense(pe, (U_UP1 + j, 0), (G_UP1 + j, 0), xh, xl, ready=norm2.ready if j == 0 else None,
                             ready_high=norm2.ready_high if j == 0 else None)
                with pe.Fori(1, CI // 2) as i:
                    for j in range(2):
                        pe_dense(pe, (U_UP1 + j, i), (G_UP1 + j, i), xh, xl)
                with pe.Fori(CI // 2, (CI + Z_FIRST) // 2) as i:
                    for j in range(2):
                        pe_dense(pe, (U_UP1 + j, i), (G_UP1 + j, i), xh, xl)
                P_, V_, S_ = self.gP, self.gV, self.gS
                pe.wait_ge(self.gw, 23)
                pe.wait_ge(self.xc, CI)
                for part in range(2):
                    for ft in range(CI):
                        xs = (xp[:, ft, NCONV - 1:NCONV - 1 + SEQ], streams(xp[:, ft, :], NCONV - 1, TS))
                        cs = (xc[:, ft, 0:SEQ], xc[:, ft, SEQ:T])
                        for w, src in ((gC, cs), (gX, xs)):
                            o = pM[0][0:8, 0:SEQ] if part == 0 else pM[0][0:8, SEQ:T]
                            mm = pe.matmul(o, w[:, ft, :], src[part], start=(ft == 0 and w is gC),
                                           stop=(ft == CI - 1 and w is gX))
                mm.then_inc(P_.sem, 1)
                pe.wait_ge(S_.sem, S_.at("pre"))
                for row, o in ((4, pM[0]), (0, pM[1])):
                    for c0, c1 in ((0, SEQ), (SEQ, T)):
                        mm = pe.matmul(o[0:H, c0:c1], con[0:8, CON["ident"] + row:CON["ident"] + row + 4],
                                       pre[:, c0:c1], start=True, stop=True)
                mm.then_inc(P_.sem, 1)
                with pe.Fori((CI + Z_FIRST) // 2, CI) as i:
                    for j in range(2):
                        pe_dense(pe, (U_UP1 + j, i), (G_UP1 + j, i), xh, xl)
                pe.wait_ge(V_.sem, V_.at("a"))
                for t in tiles5:
                    mm = pe.transpose(bank[1][:, t * H:(t + 1) * H], igr[:, tt(t)], ident[0:H, 0:H])
                mm.then_inc(P_.sem, 1)
                pe.sem_inc(self.P.sem, 1)
                pe.wait_ge(self.gS.sem, self.gS.n)
                self.pe_project(pe, 0, 0, "q")
                self.pe_project(pe, 0, 0, "k")
                with pe.Fori(0, H - 1) as h:
                    self.pe_head(pe, h, True)
                self.pe_head(pe, H - 1, False)

            def pe_project(self, pe, h, k, name):
                tile = lambda x: x[:, KH * h + k, :] if isinstance(h, int) else \
                    x[:, bass.ds(KH * h + k, 1), :].rearrange("p a c -> p (a c)")
                c = tile(xc)
                if k == 0:
                    pe.wait_ge(self.B.sem, self.B.at(name, h))
                else:
                    pe.wait_ge(self.V.sem, self.V.at(("b" + name, k), h))
                j = "qk".index(name)
                for c0, c1 in ((0, SEQ), (SEQ, T)):
                    mm = pe.matmul(pD[j][:, c0:c1], blk[k % 2][:, j, :], c[:, c0:c1], start=True, stop=True)
                mm.then_inc((self.P if k else self.Q).sem, 1)

            def pe_head(self, pe, h, more):
                P_, V_, S_ = self.P, self.V, self.S
                cuts = ((0, SEQ), (SEQ, T))

                def project(name, k):
                    if k == 1:
                        pe.wait_ge(self.T.sem, self.T.at(name, h))
                    else:
                        pe.wait_ge(S_.sem, S_.at((name, k - 1), h))
                    self.pe_project(pe, h, k, name)
                for k in range(KH):
                    if k:
                        project("k", k)
                    if k:
                        pe.wait_ge(S_.sem, S_.at(("x", k), h))
                    else:
                        pe.wait_ge(self.X.sem, self.X.at("x", h))
                        pe.wait_ge(self.T.sem, self.T.at("k", h))
                    pe.wait_ge(*((V_.sem, V_.at(("bv", k), h)) if k else (self.B.sem, self.B.at("v", h))))
                    if k:
                        pe.wait_ge(V_.sem, V_.at(("v", k - 1), h))
                    for t in tiles5:
                        mm = pe.matmul(pM[1][:, tt(t)], vtmp[k % 2][:, tt(t)], blk[k % 2][:, 2, :], start=True, stop=True)
                    mm.then_inc(P_.sem, 1)
                    if k:
                        pe.wait_ge(S_.sem, S_.at(("k", k), h))
                    for t in tiles5:
                        mm = pe.transpose(pM[0][:, tt(t)], kT[:, k, tt(t)], ident)
                    mm.then_inc(P_.sem, 1)
                    if k < KH - 1:
                        project("q", k + 1)
                pe.wait_ge(S_.sem, S_.at(("tk", KH - 1), h))
                for t in tiles5:
                    for k in range(KH):
                        mm = pe.matmul(pD[0][:, tt(t)], kT[:, k, tt(t)], qT[:, k, tt(t)], start=(k == 0),
                                       stop=(k == KH - 1))
                mm.then_inc(P_.sem, 1)
                pe.wait_ge(V_.sem, V_.at(("v", KH - 1), h))
                for row, o in ((rowM, pD[1]), (rowW, pM[1]), (rowE, pM[0])):
                    for c0, c1 in cuts:
                        mm = pe.matmul(o[:, c0:c1], selh[:], row[:, c0:c1], start=True, stop=True)
                    mm.then_inc(P_.sem, 1)
                pe.wait_ge(V_.sem, V_.at("att", h))
                pe.wait_ge(S_.sem, S_.at("rE", h))
                for t in range(NP):
                    if t:
                        pe.wait_ge(V_.sem, V_.at(("C", t - 1, KH - 1), h))
                    if t >= 2:
                        pe.wait_ge(S_.sem, S_.at(("num", t - 2), h))
                    for f in range(KH):
                        o = bank[t % 2][:, tt(f)]
                        mm = pe.matmul(o, vtok[:, t, tt(f)], att1[:, tt(t)], start=True, stop=(t == 0))
                        for k in range(KH if t else 0):
                            mm = pe.matmul(o, Cp[:, k, tt(f)], qT[:, k, tt(t)], start=False, stop=(k == KH - 1))
                    mm.then_inc(P_.sem, 1)
                    mm = pe.matmul(pD[1][:, tt(t)], ones, att1[:, tt(t)], start=True, stop=(t == 0))
                    if t:
                        pe.wait_ge(V_.sem, V_.at(("qs", t), h))
                        mm = pe.matmul(pD[1][:, tt(t)], ones, vm[1][:, 0:P], start=False, stop=True)
                    mm.then_inc(P_.sem, 1)
                    pe.wait_ge(V_.sem, V_.at(("kw", t), h))
                    for k in range(KH):
                        if t:
                            pe.wait_ge(V_.sem, V_.at(("C", t - 1, k), h))
                        elif k == 2:
                            pe.wait_ge(V_.sem, V_.at(("qh", KH - 1), h))
                        pe.matmul(U[k], kw[:, tt(k)], vtok[:, t, :], start=True, stop=True).then_inc(P_.sem, 1)
                    if t:
                        pe.wait_ge(V_.sem, V_.at(("n", t - 1), h))
                    for k in range(KH):
                        mm = pe.matmul(pD[1][:, T + 64 + k:T + 65 + k], kw[:, tt(k)], ones[:, 0:1], start=True,
                                       stop=True)
                    mm.then_inc(P_.sem, 1)
                pe.wait_ge(S_.sem, S_.at(("num", NP - 2), h))
                for b in range(NB):
                    s, n = self.slot(b)
                    pe.wait_ge(S_.sem, S_.at(("qz", b), h))
                    pe.wait_ge(self.cin[s], 16 * (self.uses[s] * h + n + 1))
                    z0 = P - TS - b * TS
                    for k in range(KH):
                        mm = pe.matmul(bank[0], qz[b % 2][:, k * P + z0:k * P + z0 + P], Cs[s][:, k, :],
                                       start=(b == 0 and k == 0), stop=False)
                    mm.then_inc(P_.sem, 1)
                    pe.wait_ge(V_.sem, V_.at(("vm", b), h))
                    for k in range(KH):
                        last = ("Cs", b - 1, k) if b else ("C", NP - 1, k)
                        pe.wait_ge(V_.sem, V_.at(last, h))
                        pe.matmul(U[k], kw[:, tt(k)], vm[b % 2][:], start=True, stop=True).then_inc(P_.sem, 1)
                    if b == 2:
                        pe.wait_ge(S_.sem, S_.at("dn", h))
                        pe.wait_ge(self.G.sem, self.G.at(("h", KH - 1), h))
                        pe.matmul(bank[1], ones, sq4[:, 0, 0:SEQ], start=True, stop=True).then_inc(P_.sem, 1)
                    if b == 3:
                        pe.wait_ge(V_.sem, V_.at(("xc", KH - 1), h))
                        pe.wait_ge(self.G.sem, self.G.at(("s", KH - 1), h))
                        pe.matmul(bank[1], ones, sq4[:, 0, 0:SEQ], start=True, stop=True).then_inc(P_.sem, 1)
                pe.matmul(bank[0], att1[:, tt(NP)], vtok[:, NP, :], start=False, stop=True).then_inc(P_.sem, 1)
                pe.wait_ge(V_.sem, V_.at("nd", h))
                pe.matmul(pD[1][:, tt(NP)], ones, att1[:, tt(NP)], start=True, stop=False)
                pe.matmul(pD[1][:, tt(NP)], ones, vm[1][:, 0:P], start=False, stop=True).then_inc(P_.sem, 1)
                pe.wait_ge(V_.sem, V_.at(("Cs", NB - 1, KH - 1), h))
                for k in range(KH):
                    mm = pe.matmul(bank[3][:, k * NB:(k + 1) * NB], kw[:, tt(k)],
                                   con[:, CON["ind"]:CON["ind"] + NB], start=True, stop=True)
                mm.then_inc(P_.sem, 1)
                pe.wait_ge(S_.sem, S_.at("tok", h))
                for f in range(KH):
                    mm = pe.transpose(bank[1][:, tt(f)], vtmp[0][:, tt(f)], ident)
                mm.then_inc(P_.sem, 1)
                if more:
                    self.pe_project(pe, h + 1, 0, "q")
                    pe.wait_ge(S_.sem, S_.at("dnS", h))
                    self.pe_project(pe, h + 1, 0, "k")
                pe.wait_ge(V_.sem, V_.at("hdS", h))
                for k in range(KH):
                    mm = pe.matmul(bank[2][:, 0:P], ones, qT[:, k, SEQ:T], start=(k == 0), stop=(k == KH - 1))
                mm.then_inc(P_.sem, 1)
                pe.wait_ge(S_.sem, S_.at("sqrS", h))
                for k in range(KH):
                    mm = pe.matmul(bank[2][:, P:2 * P], ones, sq4[:, k, SEQ:T], start=(k == 0), stop=(k == KH - 1))
                mm.then_inc(P_.sem, 1)

            def blocks(self, v, h, k, done):
                for j in range(3):
                    w = wqkv[:, j, bass.ds(KH * h + k, 1), :]
                    v.tensor_tensor(blk[k % 2][:, j, :].rearrange("p (b o) -> p b o", o=4),
                                    con[:, CON["bd"]:CON["bd"] + P].rearrange("p (b o) -> p b o", o=4),
                                    w.broadcast_to([P, P // 4, 4]), ALU.mult).then_inc(done, 1)

            def vec_head(self, v, h, more):
                P_, V_, S_ = self.P, self.V, self.S
                v.wait_ge(P_.sem, P_.rounds(h))
                v.wait_ge(S_.sem, S_.rounds(h))
                one = lambda x, i: x[:, bass.ds(i, 1), :].rearrange("p a c -> p (a c)")
                v.tensor_copy(selh[:], con[0:H, bass.ds(CON["sel"] + P * h, P)]).then_inc(V_.sem, 1)

                for k in range(KH):
                    if k < KH - 1:
                        self.blocks(v, h, k + 1, V_.sem)
                    v.wait_ge(P_.sem, P_.at(("v", k), h))
                    v.tensor_copy(vtok[:, :, tt(k)], pM[1][:, 0:T].rearrange("p (t c) -> p t c", c=P))\
                        .then_inc(V_.sem, 1)
                v.memset(qz[1][:], 0.0)
                v.memset(qz[0][:], 0.0).then_inc(V_.sem, 1)
                v.wait_ge(P_.sem, P_.at("rM", h))
                for t in tiles5:
                    see = con[:, CON["caus"] + (P if t == NP else 0):][:, 0:P]
                    v.scalar_tensor_tensor(att1[:, tt(t)], pD[1][:, tt(t)],
                                           acol[:, t, bass.ds(h, 1)], see, ALU.add, ALU.min).then_inc(V_.sem, 1)
                v.wait_ge(S_.sem, S_.at("w", h))
                v.tensor_copy(wl[:, 0:NP].unsqueeze(2), seqs(att1, 0, NP, P)[:, :, P - 1:P]).then_inc(V_.sem, 1)
                v.tensor_reduce(wl[:, NP:NP + 1], seqs(att1, SEQ, NB, TS)[:, :, TS - 1], mybir.AxisListType.X, ALU.add)\
                    .then_inc(V_.sem, 1)
                v.wait_ge(V_.sem, V_.at("wl1", h))
                v.tensor_tensor(att1[:], att1[:], pD[0][:, 0:T], ALU.mult).then_inc(V_.sem, 1)
                v.tensor_scalar(kw[:], ktok[:, 0, :], wl[:, 0:1], None, ALU.mult).then_inc(V_.sem, 1)
                v.wait_ge(P_.sem, P_.at("rW", h))
                v.tensor_copy(dec[:, 0:NP].unsqueeze(2),
                              pM[1][:, 0:SEQ].rearrange("p (t c) -> p t c", c=P)[:, :, P - 1:P]).then_inc(V_.sem, 1)
                v.tensor_copy(dec[:, NP:NP + NB].unsqueeze(2),
                              pM[1][:, SEQ:T].rearrange("p (t c) -> p t c", c=TS)[:, :, TS - 1:TS]).then_inc(V_.sem, 1)
                for k in range(KH):
                    v.tensor_tensor(qT[:, k, :], qT[:, k, :], pM[1][:, 0:T], ALU.mult).then_inc(V_.sem, 1)
                v.wait_ge(V_.sem, V_.at(("qh", KH - 1), h))
                nh = one(nP, h)
                vmv = lambda x: x[:].rearrange("p (k c) -> p k c", c=P)

                def feature_sum(t):
                    v.wait_ge(V_.sem, V_.at(("qn", t), h))
                    v.tensor_reduce(vm[1][:, 0:P], vm[0][:].rearrange("p (k c) -> p c k", c=P),
                                    mybir.AxisListType.X, ALU.add).then_inc(V_.sem, 1)
                for t in range(NP):
                    if t:
                        v.wait_ge(V_.sem, V_.at(("n", t - 1), h))
                        v.wait_ge(P_.sem, P_.at(("den", t - 1), h))
                        v.tensor_tensor(vmv(vm[0]), qT[:, :, tt(t)], nh.unsqueeze(2).broadcast_to([P, KH, P]),
                                        ALU.mult).then_inc(V_.sem, 1)
                        feature_sum(t)
                        v.wait_ge(P_.sem, P_.at(("nu", t - 1), h))
                        v.tensor_scalar(kw[:], ktok[:, t, :], wl[:, t:t + 1], None, ALU.mult).then_inc(V_.sem, 1)
                    if t == 0:
                        v.wait_ge(self.cp_free, h + 1)
                    for k in range(KH):
                        v.wait_ge(P_.sem, P_.at(("upd", t, k), h))
                        if t == 0:
                            v.tensor_copy(Cp[:, k, :], U[k]).then_inc(V_.sem, 1)
                        else:
                            v.scalar_tensor_tensor(Cp[:, k, :], Cp[:, k, :], dec[:, t:t + 1], U[k], ALU.mult,
                                                   ALU.add).then_inc(V_.sem, 1)
                    v.wait_ge(P_.sem, P_.at(("nu", t), h))
                    nu = pD[1][:, T + 64:T + 64 + KH]
                    if t == 0:
                        v.tensor_copy(nh, nu).then_inc(V_.sem, 1)
                    else:
                        v.scalar_tensor_tensor(nh, nh, dec[:, t:t + 1], nu, ALU.mult, ALU.add).then_inc(V_.sem, 1)
                v.tensor_scalar(kw[:], ktok[:, NP, :], wl[:, NP:NP + 1], None, ALU.mult).then_inc(V_.sem, 1)
                for b in range(NB):
                    if b >= 2:
                        v.wait_ge(P_.sem, P_.at(("su", b - 2, KH - 1), h))
                    v.tensor_scalar(vm[b % 2][:], vtok[:, NP, :], con[:, CON["ind"] + b:CON["ind"] + b + 1], None,
                                    ALU.mult).then_inc(V_.sem, 1)
                    for step in BESIDE[b]:
                        self.vec_prompt(v, h, step)
                    for k in range(KH):
                        v.wait_ge(P_.sem, P_.at(("su", b, k), h))
                        C = Cs[self.slot(b)[0]][:, k, :]
                        v.scalar_tensor_tensor(C, C, dec[:, NP + b:NP + b + 1], U[k], ALU.mult, ALU.add)\
                            .then_inc(V_.sem, 1)
                ns = nS[:, bass.ds(h, 1), :, :].rearrange("p a k b -> p (a k) b")
                v.tensor_tensor(vmv(vm[0]).rearrange("p k (b c) -> p k b c", c=TS),
                                qT[:, :, SEQ:T].rearrange("p k (b c) -> p k b c", c=TS),
                                ns.unsqueeze(3).broadcast_to([P, KH, NB, TS]), ALU.mult).then_inc(V_.sem, 1)
                feature_sum(NP)
                v.tensor_tensor(ns, ns, dec[:, NP:NP + NB].unsqueeze(1).broadcast_to([P, KH, NB]), ALU.mult)\
                    .then_inc(V_.sem, 1)
                v.wait_ge(P_.sem, P_.at(("nu", NP), h))
                v.wait_ge(V_.sem, V_.at("nd", h))
                v.tensor_tensor(ns, ns, bank[3][:, 0:KH * NB].rearrange("p (k b) -> p k b", b=NB), ALU.add)\
                    .then_inc(V_.sem, 1)
                if more:
                    self.blocks(v, h + 1, 0, self.B.sem)
                hs, att, rss = qT[:, :, SEQ:T], att1[:, SEQ:T], rs[:, SEQ:T]
                all4 = lambda x: x.unsqueeze(1).broadcast_to([P, KH, P])
                v.wait_ge(S_.sem, S_.at("dnS", h))
                v.tensor_tensor(att, att, em[:, SEQ:T], ALU.max).then_inc(V_.sem, 1)
                v.wait_ge(V_.sem, V_.at("dmaxS", h))
                v.reciprocal(att, att).then_inc(V_.sem, 1)
                v.wait_ge(V_.sem, V_.at("rdenS", h))
                v.tensor_tensor(hs, hs, all4(att), ALU.mult).then_inc(V_.sem, 1)
                v.wait_ge(P_.sem, P_.at("sumS", h))
                v.scalar_tensor_tensor(hs, all4(bank[2][:, 0:P]), -1.0 / DH, hs, ALU.mult, ALU.add).then_inc(V_.sem, 1)
                v.wait_ge(S_.sem, S_.at("rsS", h))
                for k in range(KH):
                    hk = qT[:, k, SEQ:T]
                    v.scalar_tensor_tensor(hk, hk, par[:, PAR["mnorm"] + k:PAR["mnorm"] + k + 1], rss, ALU.mult,
                                           ALU.mult).then_inc(V_.sem, 1)
                for k in range(KH):
                    hk = qT[:, k, SEQ:T]
                    v.wait_ge(V_.sem, V_.at(("lnS", k), h))
                    v.scalar_tensor_tensor(hk, one(xc, KH * h + k)[:, SEQ:T], par[:, bass.ds(PAR["skip"] + KH * h + k, 1)],
                                           hk, ALU.mult, ALU.add).then_inc(V_.sem, 1)
                v.wait_ge(V_.sem, V_.at(("skS", KH - 1), h))
                zs = zts[:]
                v.tensor_tensor(zs, hs, zs, ALU.mult).then_inc(V_.sem, 1)
                v.wait_ge(S_.sem, S_.at("hiS", h))
                v.tensor_tensor(al[:, bass.ds(KH * h, KH), SEQ:T], zs, ah[:, bass.ds(KH * h, KH), SEQ:T].bitcast(F32),
                                ALU.subtract).then_inc(V_.sem, 1)

            def vec_prompt(self, v, h, step):
                P_, V_, S_ = self.P, self.V, self.S
                name, k = step if isinstance(step, tuple) else (step, None)
                tile = lambda x: x[:, bass.ds(KH * h + k, 1), :].rearrange("p a c -> p (a c)")[:, 0:SEQ]
                att, hk = att1[:, 0:SEQ], None if k is None else qT[:, k, 0:SEQ]
                if name == "dmax":
                    v.wait_ge(S_.sem, S_.at("dn", h))
                    ins = v.tensor_tensor(att, att, em[:, 0:SEQ], ALU.max)
                elif name in ("rden0", "rden1"):
                    v.wait_ge(V_.sem, V_.at("dmax", h))
                    part = att1[:, 0:SEQ // 2] if name == "rden0" else att1[:, SEQ // 2:SEQ]
                    ins = v.reciprocal(part, part)
                elif name == "hd":
                    v.wait_ge(V_.sem, V_.at("rden1", h))
                    ins = v.tensor_tensor(hk, hk, att, ALU.mult)
                elif name == "xc":
                    v.wait_ge(P_.sem, P_.at("sum", h))
                    ins = v.scalar_tensor_tensor(hk, bank[1], -1.0 / DH, hk, ALU.mult, ALU.add)
                elif name == "ln":
                    v.wait_ge(S_.sem, S_.at("rs", h))
                    ins = v.scalar_tensor_tensor(hk, hk, par[:, PAR["mnorm"] + k:PAR["mnorm"] + k + 1], rs[:, 0:SEQ],
                                                 ALU.mult, ALU.mult)
                elif name == "sk":
                    v.wait_ge(V_.sem, V_.at(("ln", k), h))
                    ins = v.scalar_tensor_tensor(hk, tile(xc), par[:, bass.ds(PAR["skip"] + KH * h + k, 1)], hk,
                                                 ALU.mult, ALU.add)
                elif name == "z":
                    v.wait_ge(self.zin, 32 * (h + 1))
                    v.wait_ge(V_.sem, V_.at(("sk", k), h))
                    ins = v.tensor_tensor(hk, hk, ztp[:, k, :], ALU.mult)
                else:
                    v.wait_ge(S_.sem, S_.at(("hi", k), h))
                    ins = v.tensor_tensor(tile(al), hk, tile(ah).bitcast(F32), ALU.subtract)
                ins.then_inc(V_.sem, 1)

            def act_first(self, a, h, name):
                a.wait_ge(self.Q.sem, self.Q.at(name, h))
                a.activation((qT if name == "q" else kT)[:, 0, :], pD["qk".index(name)][:, 0:T], ACT.Copy)\
                    .then_inc(self.T.sem, 1)

            def act_input(self, a, h, k, done):
                x = xp[:, bass.ds(KH * h + k, 1), :].rearrange("p a c -> p (a c)")
                a.activation(vtmp[k % 2][:, 0:SEQ], x[:, NCONV - 1:NCONV - 1 + SEQ], ACT.Copy)
                a.activation(vtmp[k % 2][:, SEQ:T].rearrange("p (b c) -> p b c", c=TS), streams(x, NCONV - 1, TS),
                             ACT.Copy).then_inc(done, 1)

            def act_head(self, a, h, more):
                P_, V_, S_ = self.P, self.V, self.S
                for k in range(KH):
                    if k >= 2:
                        a.wait_ge(P_.sem, P_.at(("v", k - 2), h))
                    if k:
                        self.act_input(a, h, k, S_.sem)
                    for name, dst in (("q", qT), ("k", kT)):
                        if k:
                            a.wait_ge(P_.sem, P_.at((name, k), h))
                            a.activation(dst[:, k, :], pD["qk".index(name)][:, 0:T], ACT.Copy).then_inc(S_.sem, 1)
                    a.wait_ge(P_.sem, P_.at(("tk", k), h))
                    a.activation(ktok[:, :, tt(k)], pM[0][:, 0:T].rearrange("p (t c) -> p t c", c=P), ACT.Copy)\
                        .then_inc(S_.sem, 1)
                a.wait_ge(V_.sem, V_.at(("ex", NP), h))
                a.activation(att1[:], att1[:], ACT.Exp).then_inc(S_.sem, 1)
                a.wait_ge(P_.sem, P_.at("rE", h))
                a.activation(em[:], pM[0][:, 0:T], ACT.Copy).then_inc(S_.sem, 1)

                def num(t):
                    a.wait_ge(P_.sem, P_.at(("num", t), h))
                    if t < NP:
                        a.wait_ge(P_.sem, P_.at(("den", t), h))
                    a.activation(qT[:, :, tt(t)], bank[min(t, NP - 1) % 2].rearrange("p (k c) -> p k c", c=P), ACT.Copy)\
                        .then_inc(S_.sem, 1)

                def queries(b):
                    if b >= 2:
                        a.wait_ge(P_.sem, P_.at(("int", b - 2), h))
                    q = qz[b % 2][:, P - TS:].rearrange("p (k c) -> p k c", c=P)[:, :, 0:TS]
                    a.activation(q, qT[:, :, SEQ + b * TS:SEQ + (b + 1) * TS], ACT.Copy)\
                        .then_inc(S_.sem, 1)
                a.wait_ge(V_.sem, V_.at(("qh", KH - 1), h))
                for t in range(2):
                    num(t)
                for b in range(2):
                    queries(b)
                for t in range(2, NP):
                    num(t)
                a.activation(att1[:, 0:SEQ], pD[1][:, 0:SEQ], ACT.Abs).then_inc(S_.sem, 1)
                for b in range(2, 5):
                    queries(b)
                for k in range(KH):
                    a.wait_ge(V_.sem, V_.at(("xc", k), h))
                    a.activation(sq4[:, k, 0:SEQ], qT[:, k, 0:SEQ], ACT.Square).then_inc(S_.sem, 1)
                queries(5)
                a.wait_ge(P_.sem, P_.at("var", h))
                a.activation(rs[:, 0:SEQ], bank[1], ACT.Ln, bias=eps, scale=1.0 / DH).then_inc(S_.sem, 1)
                a.wait_ge(S_.sem, S_.at("lnv", h))
                a.activation(rs[:, 0:SEQ], rs[:, 0:SEQ], ACT.Exp, scale=-0.5).then_inc(S_.sem, 1)
                queries(6)
                queries(7)
                for k in range(KH):
                    a.wait_ge(V_.sem, V_.at(("z", k), h))
                    a.activation(ah[:, bass.ds(KH * h + k, 1), 0:SEQ].rearrange("p a c -> p (a c)"), qT[:, k, 0:SEQ],
                                 ACT.Copy).then_inc(S_.sem, 1)
                a.wait_ge(P_.sem, P_.at("tok", h))
                a.activation(vtmp[0][:, 0:DH], bank[0], ACT.Copy).then_inc(S_.sem, 1)
                a.wait_ge(V_.sem, V_.at(("qn", NP), h))
                num(NP)
                a.activation(att1[:, SEQ:T], pD[1][:, SEQ:T], ACT.Abs).then_inc(S_.sem, 1)
                a.wait_ge(V_.sem, V_.at("xcS", h))
                a.activation(sq4[:, :, SEQ:T], qT[:, :, SEQ:T], ACT.Square).then_inc(S_.sem, 1)
                if more:
                    self.act_input(a, h + 1, 0, self.X.sem)
                a.wait_ge(P_.sem, P_.at("varS", h))
                a.activation(rs[:, SEQ:T], bank[2][:, P:2 * P], ACT.Ln, bias=eps, scale=1.0 / DH).then_inc(S_.sem, 1)
                a.wait_ge(S_.sem, S_.at("lnvS", h))
                a.activation(rs[:, SEQ:T], rs[:, SEQ:T], ACT.Exp, scale=-0.5).then_inc(S_.sem, 1)
                if more:
                    self.act_first(a, h + 1, "k")
                a.wait_ge(V_.sem, V_.at("zS", h))
                if more:
                    self.act_first(a, h + 1, "q")
                a.activation(ah[:, bass.ds(KH * h, KH), SEQ:T], zts[:], ACT.Copy).then_inc(S_.sem, 1)

            def pool_head(self, pool, h):
                V_, S_, G_ = self.V, self.S, self.G
                one = sq4[:, 0, 0:SEQ]
                pool.wait_ge(self.P.sem, self.P.at("sc", h))
                for x in "hs":
                    for k in range(1, KH):
                        if x == "h":
                            pool.wait_ge(V_.sem, V_.at(("hd", k), h))
                            a, b = (qT[:, 0, 0:SEQ] if k == 1 else one), qT[:, k, 0:SEQ]
                        else:
                            pool.wait_ge(S_.sem, S_.at(("sqr", k), h))
                            a, b = one, sq4[:, k, 0:SEQ]
                        if k > 1:
                            pool.wait_ge(G_.sem, G_.at((x, k - 1), h))
                        pool.tensor_tensor(one, a, b, ALU.add).then_inc(G_.sem, 1)

            def sp(self, sp):
                P_, V_, S_ = self.P, self.V, self.S
                sp.wait_ge(self.gS.sem, self.gS.n)
                sp.wait_ge(self.gV.sem, self.gV.n)
                sp.sem_inc(self.cp_free, 1)

                def head(h, later):
                    def load(b):
                        s, n = self.slot(b)
                        if later or n:
                            sp.wait_ge(self.cst[s], 16 * (self.uses[s] * h + n))
                        sp.dma_start(Cs[s][:], io["st_c"][bass.ds(h * NB + b, 1)].rearrange("a p k c -> p (a k) c"))\
                            .then_inc(self.cin[s], 16)

                    def store(b):
                        s, n = self.slot(b)
                        sp.wait_ge(V_.sem, V_.at(("Cs", b, KH - 1), h))
                        sp.dma_start(io["c_s"][bass.ds(h * NB + b, 1)].rearrange("a p k c -> p (a k) c"), Cs[s][:])\
                            .then_inc(self.cst[s], 16)
                    for b in range(3):
                        load(b)
                    sp.wait_ge(V_.sem, V_.rounds(h))
                    for z, c0, c1 in ((ztp, 0, SEQ), (zts, SEQ, T)):
                        sp.dma_start(z[:], io["z_kept"][bass.ds(KH * h, KH), :, c0:c1].rearrange("k p c -> p k c"))\
                            .then_inc(self.zin, 16)
                    sp.wait_ge(V_.sem, V_.at(("C", NP - 1, KH - 1), h))
                    sp.dma_start(io["c_p"][bass.ds(h, 1)].rearrange("a p k c -> p (a k) c"), Cp[:])\
                        .then_inc(self.cpst, 16)
                    for b in range(NB):
                        store(b)
                        if b >= 1 and b + 2 < NB:
                            load(b + 2)
                    sp.wait_ge(self.cpst, 16 * (h + 1))
                    sp.sem_inc(self.cp_free, 1)
                sp.wait_ge(w_split, U_DN1)
                sp.wait_ge(pe_unit, U_DN1)
                head(0, False)
                with sp.Fori(1, H) as h:
                    head(h, True)
                for s in (2, 0, 1):
                    sp.wait_ge(self.cst[s], 16 * self.uses[s] * H)
                    if s == 2:
                        for u in range(2):
                            sp.dma_start(wraw[u][:], io["w"][U_DN1 + u]).then_inc(w_loaded[u], 16)
                sp.wait_ge(self.zin, 32 * H)
                sp.wait_ge(P_.sem, P_.at(("nu", NP), H - 1))
                sp.dma_start(xT[:], io["x_kept"]).then_inc(kept, 16)

        sq4 = kT
        mlstm = MLstm()
        def vec_residual(v, units, g0, norm=None):
            if norm is not None:
                norm.begin(v)

            def tile(i, s):
                v.wait_ge(pe_unit, units[0] + units[1] * (2 * i + s + 1))
                x = xT[:, bass.ds(2 * i + s, 1), :].rearrange("p a (c d) -> p (a c) d", c=2)
                v.tensor_tensor(x, x, psd[(g0 + s) % 2][:, :, 0:HT], ALU.add).then_inc(evac[(g0 + s) % 2], 1)
                if norm is not None:
                    norm.add(v, 2 * i + s, s)
            with v.Fori(0, KD // 2 - 1) as i:
                for s in range(2):
                    tile(i, s)
            for s in range(2):
                tile(KD // 2 - 1, s)

        def pe_down(pe, u0, g0, nu, nk, ready, ready_at):
            for j in range(2):
                for q in range(nu):
                    pe_dense(pe, (u0 + nu * j + q, 0), (g0 + j, 0), ah, al, k0=q * KD, nk=nk, first=q == 0,
                             last=q == nu - 1,
                             ready=(lambda k: (ready, ready_at + q * KD + k)) if j == 0 and ready is not None else None)
            with pe.Fori(1, KD // 2) as i:
                for j in range(2):
                    for q in range(nu):
                        pe_dense(pe, (u0 + nu * j + q, nu * i), (g0 + j, i), ah, al, k0=q * KD, nk=nk, first=q == 0,
                                 last=q == nu - 1)

        class FeedForward:

            def __init__(self, name, u, g, norm, after):
                self.after = after
                self.hi, self.lo = sem(f"{name}_hi"), sem(f"{name}_lo")
                self.u, self.g, self.norm = u, g, norm

            def parts(self):
                u, g, before = self.u, self.g, 0
                for f in FF_PARTS:
                    nu = -(-f // KD)
                    yield f, before, u, g, nu
                    u, g, before = u + 2 * f + KD * nu, g + 2 * f + KD, before + f

            def act(self, a):
                for f, before, u, g, nu in self.parts():
                    with a.Fori(0, f // 2) as i:
                        for s in range(2):
                            gg = g + 2 * s
                            a.wait_ge(pe_unit, u + 4 * i + 2 * s + 1)
                            a.activation(two(ffs[s][:]), psd[gg % 2][:, :, 0:HT], ACT.Silu).then_inc(evac[gg % 2], 1)
                            a.wait_ge(evac[(gg + 1) % 2], (gg + 1) // 2 + 2 * i + 1)
                            if s == 0:
                                a.wait_ge(pe_unit, u)
                            a.activation(ah[:, bass.ds(2 * i + s, 1), :].rearrange("p a c -> p (a c)"), fft[s][:],
                                         ACT.Copy).then_inc(self.hi, 1)

            def vec(self, v):
                for f, before, u, g, nu in self.parts():
                    with v.Fori(0, f // 2) as i:
                        for s in range(2):
                            gg = g + 2 * s
                            v.wait_ge(evac[gg % 2], gg // 2 + 2 * i + 1)
                            v.wait_ge(pe_unit, u + 4 * i + 2 * s + 2)
                            v.tensor_tensor(two(fft[s][:]), two(ffs[s][:]), psd[(gg + 1) % 2][:, :, 0:HT],
                                            ALU.mult).then_inc(evac[(gg + 1) % 2], 1)
                            v.wait_ge(self.hi, before + 2 * i + s + 1)
                            one = lambda x: x[:, bass.ds(2 * i + s, 1), :].rearrange("p a c -> p (a c)")
                            v.tensor_tensor(one(al), fft[s][:], one(ah).bitcast(F32), ALU.subtract)\
                                .then_inc(self.lo, 1)
                    vec_residual(v, (u + 2 * f, nu), g + 2 * f, self.after if before else None)

            def pe(self, pe):
                for f, before, u, g, nu in self.parts():
                    for j in range(4):
                        pe_dense(pe, (u + j, 0), (g + j, 0), xh, xl,
                                 ready=self.norm.ready if before == 0 and j == 0 else None,
                                 ready_high=self.norm.ready_high if before == 0 and j == 0 else None)
                    with pe.Fori(1, f // 2) as i:
                        for j in range(4):
                            pe_dense(pe, (u + j, 2 * i), (g + j, 2 * i), xh, xl)
                    pe_down(pe, u + 2 * f, g + 2 * f, nu, min(f, KD), self.lo, before + 1)

        ffn0 = FeedForward("ff0", U_FF0, G_FF0, norm1, norm2)
        ffn1 = FeedForward("ff1", U_FF1, G_FF1, norm3, normf)

        block = ctx.enter_context(nc.Block())

        @block.sync
        def _(sp):
            def x_part(n):
                sp.dma_start(xT[:, 2 * n:2 * n + 2, :], io["x"][:, 2 * n:2 * n + 2, :]).then_inc(x_in[n], 16)
            x_part(0)
            first = CON["ident"]
            sp.dma_start(con[:, 0:first], io["con"][:, 0:first]).then_inc(con_in, 16)
            sp.dma_start(par[:], io["par"]).then_inc(con_in, 16)
            for n in range(1, KD // 2):
                x_part(n)
            for s in range(2):
                sp.dma_start(wraw[s][:], io["w"][s]).then_inc(w_loaded[s], 16)
            sp.dma_start(con[:, first:], io["con"][:, first:]).then_inc(con_all, 16)
            def stream(u0, u1):
                with sp.Fori(u0 // 2, u1 // 2) as i:
                    for s in range(2):
                        sp.wait_ge(w_split, 2 * i + s - 1)
                        sp.dma_start(wraw[s][:], io["w"][bass.ds(2 * i + s, 1)].rearrange("a p k c -> p (a k) c"))\
                            .then_inc(w_loaded[s], 16)
            stream(2, U_FF0 + FF_UNITS)
            stream(U_UP1, U_DN1)
            mlstm.sp(sp)
            stream(U_DN1 + 2, N_UNITS)
            for k in range(KD):
                sp.wait_ge(normf.v_done, k + 1)
                sp.dma_start(io["yT"][:, k, :], ntmp[k % 2][:]).then_inc(y_stored[k % 2], 16)
            for s in range(2):
                sp.wait_ge(y_stored[s], 16 * KD // 2)

        @block.gpsimd
        def _(pool):
            def split(n, s, i, later):
                pool.wait_ge(w_loaded[s], 16 * i + 16)
                if later:
                    pool.wait_ge(pe_unit, n - 1)
                pool.sem_inc(w_taken, 1)
                pool.tensor_copy(whi[s][:], wraw[s][:]).then_inc(w_high, 1)
                pool.wait_ge(w_high, n + 1)
                pool.tensor_tensor(wlo[s][:], wraw[s][:], whi[s][:].bitcast(F32), ALU.subtract).then_inc(w_split, 1)
            for s in range(2):
                split(s, s, 0, False)

            def splits(u0, u1):
                with pool.Fori(u0 // 2, u1 // 2) as i:
                    for s in range(2):
                        split(2 * i + s, s, i, True)
            norm0.pool(pool)
            splits(2, U_FF0 + 2)
            norm1.pool(pool)
            splits(U_FF0 + 2, U_UP1 + 2)
            norm2.pool(pool)
            splits(U_UP1 + 2, U_DN1)
            with pool.Fori(0, H) as h:
                mlstm.pool_head(pool, h)
            pool.wait_ge(mlstm.V.sem, mlstm.V.at(("z", KH - 1), H - 1))
            split(U_DN1, 0, U_DN1 // 2, True)
            pool.wait_ge(mlstm.V.sem, mlstm.V.rounds(H))
            split(U_DN1 + 1, 1, U_DN1 // 2, True)
            splits(U_DN1 + 2, U_FF1 + 2)
            norm3.pool(pool)
            splits(U_FF1 + 2, N_UNITS)

        @block.scalar
        def _(a):
            def load_head(h):
                if not (isinstance(h, int) and h == 0):
                    a.wait_ge(a_out, 16 * (2 * h))
                    a.wait_ge(b_out, 16 * (2 * h))
                a.dma_start(asmp[:], io["st_hgrn"][bass.ds(h, 1)].rearrange("a p b v -> p (a b) v")).then_inc(a_in, 16)
                a.dma_start(bsmp[:], io["st_ret"][bass.ds(h, 1)].rearrange("a p b v -> p (a b) v")).then_inc(b_in, 16)
                a.dma_start(dret[:], io["dret"][bass.ds(h, 1)].rearrange("a p b v -> p (a b) v")).then_inc(b_in, 16)
                a.dma_start(win[:], io["win"][bass.ds(h, 1)].rearrange("a p b v -> p (a b) v")).then_inc(b_in, 16)

            def store_a(h):
                a.wait_ge(aV.sem, aV.at("Sa1", h))
                a.dma_start(io["hgrn_p"][bass.ds(h, 1)].rearrange("a p v -> p (a v)"), ast[:]).then_inc(a_out, 16)
                a.dma_start(io["hgrn_s"][bass.ds(h, 1)].rearrange("a p b v -> p (a b) v"), asmp[:]).then_inc(a_out, 16)

            def store_b(h):
                a.wait_ge(bV.sem, bV.at("Sa1", h))
                a.dma_start(io["ret_p"][bass.ds(h, 1)].rearrange("a p v -> p (a v)"), bst[:]).then_inc(b_out, 16)
                a.dma_start(io["ret_s"][bass.ds(h, 1)].rearrange("a p b v -> p (a b) v"), bsmp[:]).then_inc(b_out, 16)

            a.wait_ge(con_in, 16 * 2)
            norm0.act(a)
            for r in range(2):
                a.wait_ge(lb_done, 2)
                a.activation(lbt[:, 1 + r, :], lbt[:, 1 + r, :], ACT.Exp).then_inc(lb_act, 1)
            for s in range(2):
                a.wait_ge(norm0.lo_done[s], KD // 2)
            a.dma_start(vmask[:, 0:NL, :], io["masks"]).then_inc(tab_in, 16)
            a.dma_start(cos[:], io["cos"]).then_inc(tab_in, 16)
            a.dma_start(sin[:], io["sin"]).then_inc(tab_in, 16)

            load_head(0)

            def head(h, prev):
                if prev:
                    a_act_norm(a, h - 1)
                    store_a(h - 1)
                in0_evac(a, h, 0)
                if prev:
                    b_act_turns(a, h - 1)
                in0_evac(a, h, 1)
                in0_evac(a, h, 2)
                a_act_gates(a, h)
                a_act_level(a, h, 0)
                if prev:
                    b_act_norm(a, h - 1)
                    store_b(h - 1)
                in0_evac(a, h, 3)
                a_act_level(a, h, 1)
                if prev:
                    load_head(h)
                in0_evac(a, h, 4)
                a_act_level(a, h, 2)
                a_act_level(a, h, 3)
                in0_evac(a, h, 5)
                a_act_level(a, h, 4)
                a_act_level(a, h, 5)
                in0_evac(a, h, 6)
                a_act_level(a, h, 6)
                a_act_turns(a, h)
                in0_evac(a, h, 7)

            head(0, False)
            with a.Fori(1, H) as h:
                head(h, True)
            def high(ks):
                for k in ks:
                    V_, step = (aV, "mixn") if k < H else (bV, "mixg")
                    a.wait_ge(V_.sem, V_.at(step, k % H))
                    a.activation(xh[:, k, :], mix[:, k, :], ACT.Copy).then_inc(mh, 1)
            a.wait_ge(pe_unit, U_OUT0)
            high(MIX_ORDER[0:3])
            a_act_norm(a, H - 1)
            store_a(H - 1)
            high(MIX_ORDER[3:7])
            b_act_turns(a, H - 1)
            b_act_norm(a, H - 1)
            high(MIX_ORDER[7:8])
            store_b(H - 1)
            a.wait_ge(a_out, 32 * H)
            a.wait_ge(b_out, 32 * H)
            norm1.act(a)
            ffn0.act(a)
            norm2.act(a)
            mlstm.act(a)
            norm3.act(a)
            ffn1.act(a)
            normf.act(a)

        @block.vector
        def _(v):
            v.wait_ge(con_in, 16 * 2)
            norm0.vec(v)
            lg = par[:, PAR["lb"]:PAR["lb"] + 8].rearrange("p (r h) -> p r h", r=2)
            v.tensor_tensor(lbt[:, 0, :], lg[:, 0, :], lg[:, 1, :], ALU.max).then_inc(lb_done, 1)
            v.wait_ge(lb_done, 1)
            v.tensor_tensor(lbt[:, 1:3, :], lg, lbt[:, 0:1, :].broadcast_to([P, 2, H]), ALU.subtract)\
                .then_inc(lb_done, 1)
            v.wait_ge(lb_act, 2)
            v.tensor_tensor(lbt[:, 0, :], lbt[:, 1, :], lbt[:, 2, :], ALU.add).then_inc(lb_done, 1)
            v.wait_ge(lb_done, 3)
            v.reciprocal(lbt[:, 0, :], lbt[:, 0, :]).then_inc(lb_done, 1)
            v.wait_ge(lb_done, 4)
            v.tensor_tensor(lbt[:, 3, :], lbt[:, 1, :], lbt[:, 0, :], ALU.mult).then_inc(lb_done, 1)
            v.wait_ge(lb_done, 5)
            v.tensor_scalar(lbt[:, 4, :], lbt[:, 3, :], -1.0, 1.0, ALU.mult, ALU.add).then_inc(lb_done, 1)
            v.wait_ge(lb_done, 6)
            v.wait_ge(con_all, 16)
            v.wait_ge(tab_in, 16 * 3)
            v.tensor_copy(masks[:], vmask[:, 0:NL, :]).then_inc(lb_done, 1)
            v.wait_ge(lb_done, 7)

            def head(h, prev):
                if prev:
                    a_vec_tail(v, h - 1)
                    b_vec_rot(v, h - 1)
                    b_vec_scores(v, h - 1)
                    b_vec_states(v, h - 1)
                    vec_mask_v(v, h - 1, gb, bV, bS)
                a_vec_gates(v, h)
                a_vec_diff(v, h, 0)
                if prev:
                    b_vec_tail(v, h - 1)
                a_vec_first_level(v, h)
                if prev:
                    b_vec_mix(v, h - 1)
                a_vec_levels(v, h)
                a_vec_states(v, h)

            head(0, False)
            with v.Fori(1, H) as h:
                head(h, True)

            def low(n0, n1):
                for n in range(n0, n1):
                    k = MIX_ORDER[n]
                    v.wait_ge(mh, n + 1)
                    v.tensor_tensor(xl[:, k, :], mix[:, k, :], xh[:, k, :].bitcast(F32), ALU.subtract).then_inc(ml, 1)
            a_vec_tail(v, H - 1, lambda: low(0, 3))
            b_vec_rot(v, H - 1)
            low(3, 7)
            b_vec_scores(v, H - 1)
            b_vec_states(v, H - 1)
            vec_mask_v(v, H - 1, gb, bV, bS)
            b_vec_tail(v, H - 1)
            b_vec_mix(v, H - 1)
            low(7, 8)
            vec_residual(v, (U_OUT0, 1), G_OUT0, norm1)
            norm1.vec(v)
            ffn0.vec(v)
            norm2.vec(v)
            mlstm.vec(v)
            v.wait_ge(kept, 32)
            vec_residual(v, (U_DN1, 2), G_DN1, norm3)
            norm3.vec(v)
            ffn1.vec(v)
            normf.vec(v)

        @block.tensor
        def _(pe):
            pe.wait_ge(con_in, 16 * 2)
            norm0.pe(pe)

            def head(h, prev):
                def both(*fs):
                    return lambda: [f(pe, h - 1) for f in fs]
                if prev:
                    in0_unit(pe, h, 0, both(a_pe_tail))
                    a_pe_norm(pe, h - 1)
                    b_pe_rot(pe, h - 1)
                    in0_unit(pe, h, 1, both(b_pe_turns))
                    b_pe_turn_k(pe, h - 1)
                    b_pe_scores(pe, h - 1)
                    in0_unit(pe, h, 2, both(b_pe_states))
                    b_pe_tail(pe, h - 1)
                else:
                    in0_unit(pe, h, 0, ready=norm0.ready, ready_high=norm0.ready_high)
                    in0_unit(pe, h, 1)
                    in0_unit(pe, h, 2)
                in0_unit(pe, h, 3)
                if not prev:
                    pe.wait_ge(con_all, 16)
                if prev:
                    pe.wait_ge(bV.sem, bV.at("u1", h - 1))
                a_pe_level(pe, h, 0)
                if prev:
                    b_pe_norm(pe, h - 1)
                for j, (l0, l1) in ((4, (1, 2)), (5, (3, 4)), (6, (5, 6))):
                    in0_unit(pe, h, j, lambda: a_pe_level(pe, h, l0))
                    a_pe_level(pe, h, l1)

                def last_half():
                    a_pe_level(pe, h, 7)
                    a_pe_turns(pe, h)
                in0_unit(pe, h, 7, last_half)
                a_pe_head(pe, h)

            head(0, False)
            with pe.Fori(1, H) as h:
                head(h, True)

            def out0(j, ks, first=False, more=True):
                pe_dense(pe, (U_OUT0 + j, 0), (G_OUT0 + j, 0), xh, xl, ready=lambda k: (ml, MIX_ORDER.index(k) + 1),
                         ks=ks, first=first, more=more)
            a_pe_tail(pe, H - 1)
            out0(0, [0, 1], first=True)
            a_pe_norm(pe, H - 1)
            out0(0, [2])
            b_pe_rot(pe, H - 1)
            out0(1, [0, 1], first=True)
            b_pe_turns(pe, H - 1)
            out0(1, [2])
            b_pe_turn_k(pe, H - 1)
            b_pe_scores(pe, H - 1)
            out0(0, [4, 5])
            b_pe_states(pe, H - 1)
            out0(0, [6])
            b_pe_tail(pe, H - 1)
            out0(1, [4, 5, 6])
            b_pe_norm(pe, H - 1)
            for j in range(2):
                out0(j, [3])
            for j in range(2):
                out0(j, [7], more=False)
            with pe.Fori(1, 4) as i:
                for s in range(2):
                    pe_dense(pe, (U_OUT0 + s, i), (G_OUT0 + s, i), xh, xl)
            norm1.pe(pe)
            ffn0.pe(pe)
            norm2.pe(pe)
            mlstm.pe(pe)
            pe.wait_ge(mlstm.V.sem, mlstm.V.rounds(H))
            pe_down(pe, U_DN1, G_DN1, 2, 8, None, 0)
            norm3.pe(pe)
            ffn1.pe(pe)
            normf.pe(pe)


def _constants():
    import numpy as np
    f = np.float32
    con = np.zeros((P, N_CON), f)
    con[:, CON["ident"]:CON["ident"] + P] = np.eye(P)
    con[:, CON["ones"]:CON["ones"] + P] = 1
    half = P // 2
    perm = np.zeros((P, P))
    for m in range(half):
        perm[m + half, m] = -1
        perm[m, m + half] = 1
    con[:, CON["perm"]:CON["perm"] + P] = perm
    start = np.zeros(T, bool)
    start[0:SEQ:P] = True
    start[SEQ::TS] = True
    con[:, CON["reset"]:CON["reset"] + T] = ~start
    con[:, CON["ind"]:CON["ind"] + NB] = np.arange(P)[:, None] // TS == np.arange(NB)
    lg = np.log1p(-np.exp2(-5.0 - np.arange(H)))
    i = np.arange(P)
    for h in range(H):
        con[:, CON["tail"] + 2 * h] = np.exp(lg[h] * (P - 1 - i))
        con[:, CON["tail"] + 2 * h + 1] = np.exp(lg[h] * (TS - 1 - i % TS))
        con[:, CON["glast"] + 2 * h] = np.exp(lg[h] * P)
        con[:, CON["glast"] + 2 * h + 1] = np.exp(lg[h] * TS)
    con[:, CON["eps"]] = EPS
    con[:, CON["bd"]:CON["bd"] + P] = i[:, None] // 4 == i // 4
    s, j = i[:, None], i[None, :]
    same = s // TS == j // TS
    con[:, CON["caus"]:CON["caus"] + P] = np.where(s <= j, 0, NEVER)
    con[:, CON["caus"] + P:CON["caus"] + 2 * P] = np.where((s <= j) & same, 0, NEVER)
    for h in range(H):
        con[h, CON["sel"] + h * P:CON["sel"] + (h + 1) * P] = 1
    masks = np.zeros((P, len(LEVELS), P), f)
    for l, m in enumerate(LEVELS):
        masks[:, l] = (s // (2 * m) == j // (2 * m)) & (s // m % 2 == 0) & (j // m % 2 == 1)
    dret = np.zeros((H, P, 2, P), f)
    win = np.zeros((H, P, 2, P), f)
    for h in range(H):
        d = np.exp(lg[h] * np.maximum(j - s, 0)) * (s <= j)
        dret[h, :, 0] = d
        dret[h, :, 1] = d * same
        win[h, :, 0] = np.exp(lg[h] * (i + 1.0))
        win[h, :, 1] = np.exp(lg[h] * (i % TS + 1.0))
    pos = np.concatenate([np.arange(SEQ), np.tile(256 + np.arange(TS), NB)]).astype(f)
    inv = f(10000.0) ** (-(np.arange(half, dtype=f)) / f(half))
    ang = (pos[None, :] * np.tile(inv, 2)[:, None].astype(f)).astype(np.float64)
    return {"con": con, "masks": masks, "dret": dret, "win": win, "cos": np.cos(ang).astype(f),
            "sin": np.sin(ang).astype(f)}


def _arrays(a):
    import numpy as np

    def tiles(w, order=None):
        k, n = w.shape
        u = w.reshape(k // P, P, n // P, P).transpose(2, 1, 0, 3)
        return u if order is None else u[order]

    def down(w):
        u = tiles(w)
        nk = u.shape[2]
        pad = -nk % KD
        u = np.concatenate([u, np.zeros((*u.shape[:2], pad, P), u.dtype)], 2) if pad else u
        nu = u.shape[2] // KD
        return u.reshape(u.shape[0], P, nu, KD, P).transpose(0, 2, 1, 3, 4).reshape(-1, P, KD, P)

    def ffn(l):
        g, u = tiles(a["w_ffn_gate"][l]), tiles(a["w_ffn_up"][l])
        gu = np.stack([g, u], 1)
        out, at = [], 0
        for f in FF_PARTS:
            out.append(gu[at:at + f].reshape(-1, P, KD, P))
            out.append(down(a["w_ffn_down"][l][at * P:(at + f) * P]))
            at += f
        return out

    w = np.concatenate([
        tiles(a["w_in0"][0], [j * H + h for h in range(H) for j in range(8)]),
        tiles(a["w_out0"][0]), *ffn(0), tiles(a["w_up1"][0]), down(a["w_down1"][0]), *ffn(1)])
    assert w.shape[0] == N_UNITS, w.shape
    x = np.concatenate([a["x_prompt"].reshape(SEQ, D), a["x_sample"].reshape(NB * TS, D)])
    cols = lambda v: v.reshape(-1, P).T
    par = np.concatenate([cols(a["norm_mix"][0]), cols(a["norm_mix"][1]), cols(a["norm_ffn"][0]),
                          cols(a["norm_ffn"][1]), cols(a["norm_final"]), cols(a["lb_logits"][0]),
                          cols(a["lb_logits"][1]), cols(a["hgrn_norm"]), cols(a["ret_norm"]),
                          *[cols(a["conv_w"][0, i]) for i in range(4)], cols(a["conv_b"]), cols(a["mlstm_norm"]),
                          cols(a["mlstm_skip"])], 1)
    assert par.shape[1] == N_PAR
    wg = np.concatenate([a["w_ig"][0], a["w_fg"][0]], 1).reshape(3, CI, P // 4, 4, 8)
    wgx = np.repeat(wg[:, :, :, None], 4, 3).reshape(3, CI, P, 4, 8).transpose(2, 0, 1, 3, 4)
    wqkv = np.stack([a[n][0].reshape(CI, P, 4) for n in ("w_q1", "w_k1", "w_v1")]).transpose(2, 0, 1, 3)
    gsm = np.concatenate([a["b_ig"].T, a["b_fg"].T, a["state_mlstm_m"][0].T], 1)
    st_n = a["state_mlstm_n"][0].reshape(NB, H, KH, P).transpose(3, 1, 2, 0)
    st_c = a["state_mlstm_c"][0].transpose(1, 0, 3, 2).reshape(H * NB, KH, P, DH).transpose(0, 2, 1, 3)
    conv = a["state_conv"][0].reshape(NB, NCONV - 1, CI, P).transpose(3, 2, 0, 1)
    more = {"wgx": wgx, "wqkv": wqkv, "gsm": gsm, "st_n": st_n, "st_c": st_c, "conv": conv}
    return more | {"x": x.T.reshape(KD, P, T).transpose(1, 0, 2), "w": w, "par": par,
            "st_hgrn": a["state_hgrn"][0].transpose(1, 2, 0, 3), "st_ret": a["state_ret"][0].transpose(1, 2, 0, 3)}


_OUT = {"yT": (P, KD, T), "hgrn_p": (H, P, P), "hgrn_s": (H, P, NB, P), "ret_p": (H, P, P), "ret_s": (H, P, NB, P),
        "c_p": (H, P, KH, DH), "c_s": (H * NB, P, KH, DH), "n_p": (P, H, KH), "n_s": (P, H, KH, NB),
        "m_out": (H, 1 + NB), "conv_p": (P, CI, NCONV - 1), "conv_s": (P, CI, NB, NCONV - 1)}
_KEPT = {"x_kept": (P, KD, T), "z_kept": (CI, P, T)}


def kernel(**inputs):
    import numpy as np
    import concourse.bacc as bacc
    from concourse.bass_utils import run_bass_kernel_spmd
    a = {k: np.asarray(v) for k, v in inputs.items()}
    arrays = {k: np.ascontiguousarray(v) for k, v in (_arrays(a) | _constants()).items()}
    nc = bacc.Bacc("TRN2", target_bir_lowering=False, num_devices=1)
    io = {n: nc.dram_tensor(n, x.shape, F32, kind="ExternalInput").ap() for n, x in arrays.items()}
    io |= {n: nc.dram_tensor(n, s, F32, kind="ExternalOutput").ap() for n, s in _OUT.items()}
    io |= {n: nc.dram_tensor(n, s, F32, kind="Internal").ap() for n, s in _KEPT.items()}
    trunk(nc, io)
    r = run_bass_kernel_spmd(nc, [arrays], core_ids=[0]).results[0]
    y = r["yT"].transpose(2, 1, 0).reshape(T, D)
    c_s = r["c_s"].reshape(H, NB, P, KH, DH).transpose(1, 0, 4, 3, 2).reshape(1, NB, H, DH, DH)
    return tuple(np.ascontiguousarray(x) for x in (
        y[:SEQ].reshape(1, SEQ, D), y[SEQ:].reshape(NB, TS, D),
        r["hgrn_p"].reshape(1, 1, H, P, P), r["hgrn_s"].transpose(2, 0, 1, 3)[None],
        r["ret_p"].reshape(1, 1, H, P, P), r["ret_s"].transpose(2, 0, 1, 3)[None],
        r["c_p"].transpose(0, 3, 2, 1).reshape(1, 1, H, DH, DH), c_s,
        r["n_p"].transpose(1, 2, 0).reshape(1, 1, H, DH), r["n_s"].transpose(3, 1, 2, 0).reshape(1, NB, H, DH),
        r["m_out"][:, 0].reshape(1, 1, H), r["m_out"][:, 1:].T[None],
        r["conv_p"].transpose(2, 1, 0).reshape(1, 1, NCONV - 1, CI * P),
        r["conv_s"].transpose(2, 3, 1, 0).reshape(1, NB, NCONV - 1, CI * P)))
```
